# Optimizing a Trainium2 kernel written in Bass

```python
import math
import jax, jax.numpy as jnp
from jax import lax
import numpy as np

D_MODEL = 1024
BATCH = 1
SEQ = 512
DEPTH = 1

N_MIXERS = 2
N_ATTN_LAYERS = (DEPTH + N_MIXERS - 1) // N_MIXERS
N_FOURIER_LAYERS = DEPTH // N_MIXERS
N_DIFF_HEADS = 8
DIFF_HEAD_DIM = D_MODEL // N_DIFF_HEADS // 2
DIFF_V_DIM = 2 * DIFF_HEAD_DIM
Q_BLOCK = 128
N_FOURIER_GROUPS = 4
FOURIER_GROUP_DIM = D_MODEL // N_FOURIER_GROUPS
N_EXPERT_GROUPS = 4
EXPERTS_PER_GROUP = 4
N_EXPERTS = N_EXPERT_GROUPS * EXPERTS_PER_GROUP
EXPERT_TOP_K = 2
D_EXPERT = D_MODEL // 2
N_ADA = 6
ADA_INIT_SCALE = 0.5
EPS = 1e-6


def rmsnorm(x, g):
    xf = x.astype(jnp.float32)
    y = xf * lax.rsqrt(jnp.mean(xf * xf, axis=-1, keepdims=True) + EPS)
    return (y * g.astype(jnp.float32)).astype(x.dtype)

def modulate(h, shift, scale):
    return h * (1.0 + scale[:, None, :]) + shift[:, None, :]

def alibi_slopes(n_heads):
    return 2.0 ** (-8.0 * jnp.arange(1, n_heads + 1, dtype=jnp.float32) / n_heads)

def diff_attention(h, w_in, lam_q1, lam_k1, lam_q2, lam_k2, subln_g, w_out, layer_idx):
    B, S, D = h.shape
    H, dh, dv = N_DIFF_HEADS, DIFF_HEAD_DIM, DIFF_V_DIM
    qkv = h @ w_in
    q, k, v = jnp.split(qkv, 3, axis=-1)
    q = q.reshape(B, S, H, 2, dh) * (dh ** -0.5)
    k = k.reshape(B, S, H, 2, dh)
    v = v.reshape(B, S, H, dv)
    q1, q2 = q[..., 0, :], q[..., 1, :]
    k1, k2 = k[..., 0, :], k[..., 1, :]
    lam_init = 0.8 - 0.6 * math.exp(-0.3 * layer_idx)
    lam = (jnp.exp(jnp.sum(lam_q1.astype(jnp.float32) * lam_k1.astype(jnp.float32)))
           - jnp.exp(jnp.sum(lam_q2.astype(jnp.float32) * lam_k2.astype(jnp.float32)))
           + lam_init)
    slopes = alibi_slopes(H)
    pos = jnp.arange(S, dtype=jnp.float32)
    nb = S // Q_BLOCK
    q1b = q1.reshape(B, nb, Q_BLOCK, H, dh).transpose(1, 0, 3, 2, 4)
    q2b = q2.reshape(B, nb, Q_BLOCK, H, dh).transpose(1, 0, 3, 2, 4)
    posb = pos.reshape(nb, Q_BLOCK)

    def block(args):
        qa, qb, pq = args
        bias = -slopes[:, None, None] * jnp.abs(pq[:, None] - pos[None, :])
        s1 = jnp.einsum('bhqd,bkhd->bhqk', qa, k1, preferred_element_type=jnp.float32) + bias
        s2 = jnp.einsum('bhqd,bkhd->bhqk', qb, k2, preferred_element_type=jnp.float32) + bias
        a = jax.nn.softmax(s1, axis=-1) - lam * jax.nn.softmax(s2, axis=-1)
        return jnp.einsum('bhqk,bkhd->bqhd', a.astype(v.dtype), v)

    o = lax.map(block, (q1b, q2b, posb))
    o = o.transpose(1, 0, 2, 3, 4).reshape(B, S, H, dv)
    o = rmsnorm(o, subln_g) * (1.0 - lam_init)
    return o.reshape(B, S, H * dv) @ w_out

def fourier_mix(h, w_in, w_out):
    B, S, D = h.shape
    u = (h @ w_in).reshape(B, S, N_FOURIER_GROUPS, FOURIER_GROUP_DIM).astype(jnp.float32)
    f = jnp.fft.fft2(u, axes=(1, 3), norm="ortho").real
    return f.reshape(B, S, D).astype(h.dtype) @ w_out

def hier_moe(h, w_rg, b_rg, w_re, b_re, w_gate, w_up, w_down):
    B, S, D = h.shape
    t = h.reshape(B * S, D)
    T = t.shape[0]
    g_logits = (t @ w_rg).astype(jnp.float32) + b_rg.astype(jnp.float32)
    g_prob = jax.nn.softmax(g_logits, axis=-1)
    g_idx = jnp.argmax(g_logits, axis=-1)
    g_w = jnp.take_along_axis(g_prob, g_idx[:, None], axis=-1)
    e_logits = jnp.einsum('td,dge->tge', t, w_re).astype(jnp.float32) + b_re.astype(jnp.float32)
    e_sel = jnp.take_along_axis(e_logits, g_idx[:, None, None], axis=1)[:, 0]
    top_v, top_i = lax.top_k(e_sel, EXPERT_TOP_K)
    top_w = jax.nn.softmax(top_v, axis=-1)
    e_w = jnp.sum(jax.nn.one_hot(top_i, EXPERTS_PER_GROUP, dtype=jnp.float32) * top_w[..., None], axis=1)
    gates = (jax.nn.one_hot(g_idx, N_EXPERT_GROUPS, dtype=jnp.float32)[:, :, None]
             * (g_w[:, :, None] * e_w[:, None, :])).reshape(T, N_EXPERTS)
    hid = jax.nn.silu(jnp.einsum('td,edf->tef', t, w_gate)) * jnp.einsum('td,edf->tef', t, w_up)
    hid = hid * gates.astype(hid.dtype)[:, :, None]
    y = jnp.einsum('tef,efd->td', hid, w_down)
    return y.reshape(B, S, D)

def first_inputs(seed: int = 0) -> dict:
    key = jax.random.key(seed)
    ks = jax.random.split(key, 24)
    D = D_MODEL

    def nrm(k, shape, scale):
        return jax.random.normal(k, shape, jnp.float32) * scale

    return {
        "x": nrm(ks[0], (BATCH, SEQ, D), 1.0),
        "c": nrm(ks[1], (BATCH, D), 1.0),
        "ada_w": nrm(ks[2], (DEPTH, D, N_ADA * D), ADA_INIT_SCALE * D ** -0.5),
        "ada_b": nrm(ks[3], (DEPTH, N_ADA * D), 0.02),
        "norm_mix": 1.0 + nrm(ks[4], (DEPTH, D), 0.02),
        "norm_ffn": 1.0 + nrm(ks[5], (DEPTH, D), 0.02),
        "attn_w_in": nrm(ks[6], (N_ATTN_LAYERS, D, 3 * D), D ** -0.5),
        "attn_lam_q1": nrm(ks[7], (N_ATTN_LAYERS, DIFF_HEAD_DIM), 0.1),
        "attn_lam_k1": nrm(ks[8], (N_ATTN_LAYERS, DIFF_HEAD_DIM), 0.1),
        "attn_lam_q2": nrm(ks[9], (N_ATTN_LAYERS, DIFF_HEAD_DIM), 0.1),
        "attn_lam_k2": nrm(ks[10], (N_ATTN_LAYERS, DIFF_HEAD_DIM), 0.1),
        "attn_subln": 1.0 + nrm(ks[11], (N_ATTN_LAYERS, DIFF_V_DIM), 0.02),
        "attn_w_out": nrm(ks[12], (N_ATTN_LAYERS, N_DIFF_HEADS * DIFF_V_DIM, D), (N_DIFF_HEADS * DIFF_V_DIM) ** -0.5),
        "fourier_w_in": nrm(ks[13], (N_FOURIER_LAYERS, D, D), D ** -0.5),
        "fourier_w_out": nrm(ks[14], (N_FOURIER_LAYERS, D, D), D ** -0.5),
        "router_group_w": nrm(ks[15], (DEPTH, D, N_EXPERT_GROUPS), D ** -0.5),
        "router_group_b": nrm(ks[16], (DEPTH, N_EXPERT_GROUPS), 0.01),
        "router_expert_w": nrm(ks[17], (DEPTH, D, N_EXPERT_GROUPS, EXPERTS_PER_GROUP), D ** -0.5),
        "router_expert_b": nrm(ks[18], (DEPTH, N_EXPERT_GROUPS, EXPERTS_PER_GROUP), 0.01),
        "expert_w_gate": nrm(ks[19], (DEPTH, N_EXPERTS, D, D_EXPERT), D ** -0.5),
        "expert_w_up": nrm(ks[20], (DEPTH, N_EXPERTS, D, D_EXPERT), D ** -0.5),
        "expert_w_down": nrm(ks[21], (DEPTH, N_EXPERTS, D_EXPERT, D), D_EXPERT ** -0.5),
        "norm_final": 1.0 + nrm(ks[22], (D,), 0.02),
    }

def first_block(x, c, ada_w, ada_b, norm_mix, norm_ffn, attn_w_in, attn_lam_q1, attn_lam_k1,
              attn_lam_q2, attn_lam_k2, attn_subln, attn_w_out, fourier_w_in, fourier_w_out,
              router_group_w, router_group_b, router_expert_w, router_expert_b,
              expert_w_gate, expert_w_up, expert_w_down, norm_final):
    cond = jax.nn.silu(c)
    for i in range(DEPTH):
        mod = cond @ ada_w[i] + ada_b[i]
        sh1, sc1, g1, sh2, sc2, g2 = jnp.split(mod, N_ADA, axis=-1)
        h = modulate(rmsnorm(x, norm_mix[i]), sh1, sc1)
        j = i // N_MIXERS
        if i % N_MIXERS == 0:
            y = diff_attention(h, attn_w_in[j], attn_lam_q1[j], attn_lam_k1[j], attn_lam_q2[j],
                               attn_lam_k2[j], attn_subln[j], attn_w_out[j], i)
        else:
            y = fourier_mix(h, fourier_w_in[j], fourier_w_out[j])
        x = x + g1[:, None, :] * y
        h = modulate(rmsnorm(x, norm_ffn[i]), sh2, sc2)
        y = hier_moe(h, router_group_w[i], router_group_b[i], router_expert_w[i], router_expert_b[i],
                     expert_w_gate[i], expert_w_up[i], expert_w_down[i])
        x = x + g2[:, None, :] * y
    return rmsnorm(x, norm_final)


CHUNK = 64
FOX_HEADS = 8
FOX_HEAD_DIM = 64
FOX_WIDTH = FOX_HEADS * FOX_HEAD_DIM
RWKV_HEADS = 8
RWKV_HEAD_DIM = 64
RWKV_WIDTH = RWKV_HEADS * RWKV_HEAD_DIM
W_LORA = 64
A_LORA = 64
G_LORA = 128
GN_EPS = 64e-5
PEER_HEADS = 8
PEER_N_KEYS = 128
PEER_N_EXPERTS = PEER_N_KEYS * PEER_N_KEYS
PEER_HALF = 128
PEER_TOPK = 16
PEER_TOKEN_BLOCK = 128
DN_ALPHA = (2 * DEPTH) ** 0.25
DN_BETA = (8 * DEPTH) ** -0.25
LN_EPS = 1e-5
FOX_SPLITS = (FOX_WIDTH, FOX_WIDTH, FOX_WIDTH, FOX_HEADS)
RWKV_SPLITS = (RWKV_WIDTH, RWKV_WIDTH, RWKV_WIDTH, W_LORA, A_LORA, G_LORA)
FOX_COLS = 3 * FOX_WIDTH + FOX_HEADS
RWKV_COLS = 3 * RWKV_WIDTH + W_LORA + A_LORA + G_LORA
IN_WIDTH = FOX_COLS + RWKV_COLS + 2 * D_MODEL


def _split(t, sizes):
    out = []
    start = 0
    for n in sizes:
        out.append(t[..., start:start + n])
        start += n
    return out

def _layer_norm(x, g, b):
    xf = x.astype(jnp.float32)
    mu = jnp.mean(xf, axis=-1, keepdims=True)
    var = jnp.mean(jnp.square(xf - mu), axis=-1, keepdims=True)
    return ((xf - mu) * lax.rsqrt(var + LN_EPS) * g + b).astype(x.dtype)

def _token_shift(p, mu):
    prev = jnp.pad(p, ((0, 0), (1, 0), (0, 0)))[:, :-1]
    return p + mu * (prev - p)

def _forgetting_attention(q, k, v, f_logit):
    B, S = q.shape[0], q.shape[1]
    heads = lambda t: t.reshape(B, S, FOX_HEADS, FOX_HEAD_DIM).transpose(0, 2, 1, 3)
    q, k, v = heads(q), heads(k), heads(v)
    log_f = jax.nn.log_sigmoid(f_logit.astype(jnp.float32))
    c = jnp.cumsum(log_f, axis=1).transpose(0, 2, 1)
    scale = FOX_HEAD_DIM ** -0.5
    outs = []
    for blk in range(S // Q_BLOCK):
        q0 = blk * Q_BLOCK
        q1 = q0 + Q_BLOCK
        s = jnp.einsum('bhqd,bhkd->bhqk', q[:, :, q0:q1], k[:, :, :q1]).astype(jnp.float32) * scale
        s = s + c[:, :, q0:q1, None] - c[:, :, None, :q1]
        causal = jnp.arange(q0, q1)[:, None] >= jnp.arange(q1)[None, :]
        s = jnp.where(causal, s, -jnp.inf)
        p = jax.nn.softmax(s, axis=-1).astype(v.dtype)
        outs.append(jnp.einsum('bhqk,bhkd->bhqd', p, v[:, :, :q1]))
    o = jnp.concatenate(outs, axis=2)
    return o.transpose(0, 2, 1, 3).reshape(B, S, FOX_WIDTH)

def _rwkv7_time_mix(r, k, v, w_lora, a_lora, g_lora, w0, w2, a0, a2, g2, k_k, k_a, r_k, ln_g, ln_b):
    B, S = r.shape[0], r.shape[1]
    f32 = jnp.float32
    H, N = RWKV_HEADS, RWKV_HEAD_DIM
    w_pre = (w0 + jnp.tanh(w_lora) @ w2).astype(f32)
    decay = jnp.exp(-jnp.exp(-jax.nn.softplus(-w_pre) - 0.5))
    a = jax.nn.sigmoid((a0 + a_lora @ a2).astype(f32))
    g = jax.nn.sigmoid(g_lora) @ g2
    heads = lambda t: t.astype(f32).reshape(B, S, H, N)
    kk = heads(k * k_k)
    kk = kk / jnp.maximum(jnp.sqrt(jnp.sum(kk * kk, axis=-1, keepdims=True)), 1e-12)
    k_mod = k.astype(f32) * (1.0 + (a - 1.0) * k_a.astype(f32))
    r_h, k_h, v_h, w_h, a_h = heads(r), heads(k_mod), heads(v), heads(decay), heads(a)

    def to_chunks(t):
        return t.transpose(1, 0, 2, 3).reshape(S // CHUNK, CHUNK, B, H, N)

    def frame_step(state, inp):
        r_t, w_t, k_t, v_t, kk_t, a_t = inp
        sa = jnp.einsum('bhij,bhj->bhi', state, -kk_t)
        state = (state * w_t[:, :, None, :] + sa[..., None] * (kk_t * a_t)[:, :, None, :]
                 + v_t[..., None] * k_t[:, :, None, :])
        return state, jnp.einsum('bhij,bhj->bhi', state, r_t)

    def chunk_step(state, chunk_inp):
        return lax.scan(frame_step, state, chunk_inp)

    state0 = jnp.zeros((B, H, N, N), f32)
    xs = (to_chunks(r_h), to_chunks(w_h), to_chunks(k_h), to_chunks(v_h), to_chunks(kk), to_chunks(a_h))
    _, y = lax.scan(chunk_step, state0, xs)
    y = y.reshape(S, B, H, N).transpose(1, 0, 2, 3)
    mu = jnp.mean(y, axis=-1, keepdims=True)
    var = jnp.mean(jnp.square(y - mu), axis=-1, keepdims=True)
    y = ((y - mu) * lax.rsqrt(var + GN_EPS)).reshape(B, S, RWKV_WIDTH) * ln_g + ln_b
    bonus = jnp.sum(r_h * k_h * r_k.astype(f32).reshape(H, N), axis=-1, keepdims=True) * v_h
    y = (y + bonus.reshape(B, S, RWKV_WIDTH)) * g
    return y.astype(r.dtype)

def _peer(x, w_q, sub_keys, u_table, v_table):
    B, S, D = x.shape
    xt = x.reshape((B * S) // PEER_TOKEN_BLOCK, PEER_TOKEN_BLOCK, D)
    K = PEER_TOPK

    def block(xb):
        t = xb.shape[0]
        q = (xb @ w_q).reshape(t, PEER_HEADS, 2, PEER_HALF)
        s = jnp.einsum('thpd,hpkd->thpk', q, sub_keys).astype(jnp.float32)
        top_s, top_i = lax.top_k(s, K)
        cand_s = top_s[:, :, 0, :, None] + top_s[:, :, 1, None, :]
        cand_i = top_i[:, :, 0, :, None] * PEER_N_KEYS + top_i[:, :, 1, None, :]
        best_s, best_pos = lax.top_k(cand_s.reshape(t, PEER_HEADS, K * K), K)
        idx = jnp.take_along_axis(cand_i.reshape(t, PEER_HEADS, K * K), best_pos, axis=-1)
        gate = jax.nn.softmax(best_s, axis=-1).astype(xb.dtype)
        h = jax.nn.gelu(jnp.einsum('thkd,td->thk', u_table[idx], xb), approximate=False)
        return jnp.einsum('thk,thkd->td', gate * h, v_table[idx])

    return lax.map(block, xt).reshape(B, S, D)

def second_inputs(seed: int = 0) -> dict:
    key = jax.random.key(seed)
    ks = jax.random.split(key, 32)
    L = DEPTH
    nrm = lambda k, shape, scale: jax.random.normal(k, shape, jnp.float32) * scale
    return {
        "x": nrm(ks[0], (BATCH, SEQ, D_MODEL), 1.0),
        "w_in": nrm(ks[1], (L, D_MODEL, IN_WIDTH), D_MODEL ** -0.5),
        "fox_f_bias": 3.0 + nrm(ks[2], (L, FOX_HEADS), 0.5),
        "rwkv_mu": jax.random.uniform(ks[3], (L, RWKV_COLS), jnp.float32),
        "rwkv_w0": nrm(ks[4], (L, RWKV_WIDTH), 1.0),
        "rwkv_w2": nrm(ks[5], (L, W_LORA, RWKV_WIDTH), 0.1 * W_LORA ** -0.5),
        "rwkv_a0": nrm(ks[6], (L, RWKV_WIDTH), 0.5),
        "rwkv_a2": nrm(ks[7], (L, A_LORA, RWKV_WIDTH), A_LORA ** -0.5),
        "rwkv_g2": nrm(ks[8], (L, G_LORA, RWKV_WIDTH), G_LORA ** -0.5),
        "rwkv_k_k": 0.85 + nrm(ks[9], (L, RWKV_WIDTH), 0.05),
        "rwkv_k_a": 1.0 + nrm(ks[10], (L, RWKV_WIDTH), 0.05),
        "rwkv_r_k": nrm(ks[11], (L, RWKV_WIDTH), 0.1),
        "rwkv_ln_g": 1.0 + nrm(ks[12], (L, RWKV_WIDTH), 0.05),
        "rwkv_ln_b": nrm(ks[13], (L, RWKV_WIDTH), 0.01),
        "p_fox": nrm(ks[14], (L, FOX_WIDTH, D_MODEL), FOX_WIDTH ** -0.5),
        "p_rwkv": nrm(ks[15], (L, RWKV_WIDTH, D_MODEL), RWKV_WIDTH ** -0.5),
        "w_o": nrm(ks[16], (L, D_MODEL, D_MODEL), DN_BETA * D_MODEL ** -0.5),
        "ln1_g": 1.0 + nrm(ks[17], (L, D_MODEL), 0.05),
        "ln1_b": nrm(ks[18], (L, D_MODEL), 0.01),
        "peer_w_q": nrm(ks[19], (L, D_MODEL, PEER_HEADS * 2 * PEER_HALF), D_MODEL ** -0.5),
        "peer_sub_keys": nrm(ks[20], (L, PEER_HEADS, 2, PEER_N_KEYS, PEER_HALF), PEER_HALF ** -0.5),
        "peer_u": nrm(ks[21], (L, PEER_N_EXPERTS, D_MODEL), D_MODEL ** -0.5),
        "peer_v": nrm(ks[22], (L, PEER_N_EXPERTS, D_MODEL), DN_BETA * PEER_HEADS ** -0.5),
        "ln2_g": 1.0 + nrm(ks[23], (L, D_MODEL), 0.05),
        "ln2_b": nrm(ks[24], (L, D_MODEL), 0.01),
    }

def second_block(x, w_in, fox_f_bias, rwkv_mu, rwkv_w0, rwkv_w2, rwkv_a0, rwkv_a2, rwkv_g2,
              rwkv_k_k, rwkv_k_a, rwkv_r_k, rwkv_ln_g, rwkv_ln_b, p_fox, p_rwkv, w_o,
              ln1_g, ln1_b, peer_w_q, peer_sub_keys, peer_u, peer_v, ln2_g, ln2_b):
    for l in range(DEPTH):
        p = x @ w_in[l]
        fox_cols = p[..., :FOX_COLS]
        rwkv_cols = _token_shift(p[..., FOX_COLS:FOX_COLS + RWKV_COLS], rwkv_mu[l])
        gate_cols = p[..., FOX_COLS + RWKV_COLS:]
        q, k, v, f_logit = _split(fox_cols, FOX_SPLITS)
        r_r, r_k, r_v, r_wl, r_al, r_gl = _split(rwkv_cols, RWKV_SPLITS)
        gate_fox, gate_rwkv = _split(gate_cols, (D_MODEL, D_MODEL))

        y_fox = _forgetting_attention(q, k, v, f_logit + fox_f_bias[l])
        y_rwkv = _rwkv7_time_mix(r_r, r_k, r_v, r_wl, r_al, r_gl,
                                 rwkv_w0[l], rwkv_w2[l], rwkv_a0[l], rwkv_a2[l], rwkv_g2[l],
                                 rwkv_k_k[l], rwkv_k_a[l], rwkv_r_k[l], rwkv_ln_g[l], rwkv_ln_b[l])
        merged = (jax.nn.sigmoid(gate_fox) * (y_fox @ p_fox[l])
                  + jax.nn.sigmoid(gate_rwkv) * (y_rwkv @ p_rwkv[l]))
        x = _layer_norm(DN_ALPHA * x + merged @ w_o[l], ln1_g[l], ln1_b[l])
        x = _layer_norm(DN_ALPHA * x + _peer(x, peer_w_q[l], peer_sub_keys[l], peer_u[l], peer_v[l]),
                        ln2_g[l], ln2_b[l])
    return x


def setup_inputs(seed=0):
    out = dict(first_inputs(seed))
    for name, value in second_inputs(seed + 1).items():
        if name != "x":
            out[name + "_2"] = value
    return out


def reference(
    x, c, ada_w, ada_b, norm_mix, norm_ffn, attn_w_in, attn_lam_q1, attn_lam_k1, attn_lam_q2,
    attn_lam_k2, attn_subln, attn_w_out, fourier_w_in, fourier_w_out, router_group_w,
    router_group_b, router_expert_w, router_expert_b, expert_w_gate, expert_w_up, expert_w_down,
    norm_final, w_in_2, fox_f_bias_2, rwkv_mu_2, rwkv_w0_2, rwkv_w2_2, rwkv_a0_2, rwkv_a2_2,
    rwkv_g2_2, rwkv_k_k_2, rwkv_k_a_2, rwkv_r_k_2, rwkv_ln_g_2, rwkv_ln_b_2, p_fox_2, p_rwkv_2,
    w_o_2, ln1_g_2, ln1_b_2, peer_w_q_2, peer_sub_keys_2, peer_u_2, peer_v_2, ln2_g_2, ln2_b_2,
):
    x = first_block(
        x, c, ada_w, ada_b, norm_mix, norm_ffn, attn_w_in, attn_lam_q1, attn_lam_k1,
        attn_lam_q2, attn_lam_k2, attn_subln, attn_w_out, fourier_w_in, fourier_w_out,
        router_group_w, router_group_b, router_expert_w, router_expert_b, expert_w_gate,
        expert_w_up, expert_w_down, norm_final,
    )
    return second_block(
        x, w_in_2, fox_f_bias_2, rwkv_mu_2, rwkv_w0_2, rwkv_w2_2, rwkv_a0_2, rwkv_a2_2,
        rwkv_g2_2, rwkv_k_k_2, rwkv_k_a_2, rwkv_r_k_2, rwkv_ln_g_2, rwkv_ln_b_2, p_fox_2,
        p_rwkv_2, w_o_2, ln1_g_2, ln1_b_2, peer_w_q_2, peer_sub_keys_2, peer_u_2, peer_v_2,
        ln2_g_2, ln2_b_2,
    )


_drawn_inputs = setup_inputs


def setup_inputs(seed=0):
    import zlib

    import numpy as np

    out = dict(_drawn_inputs(seed))
    spreads = {}
    factors = {'norm_mix': 5.221,
     'norm_ffn': 4.347,
     'attn_lam_q1': 3.978,
     'attn_lam_k1': 5.337,
     'attn_lam_q2': 7.913,
     'attn_lam_k2': 8.0,
     'attn_subln': 5.272,
     'router_group_b': 8.0,
     'router_expert_b': 8.0,
     'fox_f_bias_2': 37.088,
     'rwkv_w2_2': 8.0,
     'rwkv_k_k_2': 42.693,
     'rwkv_k_a_2': 4.1,
     'rwkv_ln_g_2': 4.932,
     'rwkv_ln_b_2': 33.058,
     'ln1_b_2': 4.093,
     'ln2_b_2': 5.685}
    for name, (base, spread) in spreads.items():
        noise = np.random.default_rng([zlib.crc32(name.encode()), seed]).standard_normal(out[name].shape)
        drawn = base * np.exp(spread * noise) if base else spread * noise
        out[name] = __import__('jax').numpy.asarray(drawn.astype(out[name].dtype))
    for name, factor in factors.items():
        out[name] = (out[name] * factor).astype(out[name].dtype)
    return out
```

```python
import math
from contextlib import ExitStack, contextmanager

import numpy as np

import concourse.bass as bass
from concourse import mybir

F32 = mybir.dt.float32
F32R = mybir.dt.float32r
I32 = mybir.dt.int32
U32 = mybir.dt.uint32
ALU = mybir.AluOpType
ACT = mybir.ActivationFunctionType
AX = mybir.AxisListType

P = 128
D = 1024
T = 512
KT = D // P
TT = T // P
HEADS = 8
DH = 64
EXPERTS = 16
EXPERT_GROUPS = 4
EPS = 1e-6
LN_EPS = 1e-5
GN_EPS = 64e-5
ALPHA = 2.0 ** 0.25
LAM_INIT = 0.8 - 0.6 * math.exp(0.0)
CHUNK = 64
NCHUNK = T // CHUNK
KEYS = 128
TOPK = 16
NEG = -1e30

VEC_NAMES = [("c", 8), ("norm_mix", 8), ("norm_ffn", 8), ("norm_final", 8), ("ln1_g", 8), ("ln1_b", 8),
             ("ada_b", 48), ("subln", 1), ("mu", 14), ("w0", 4), ("a0", 4), ("k_k", 4), ("k_a", 4),
             ("r_k", 4), ("ln_g", 4), ("ln_b", 4)]
VEC_AT, _n = {}, 0
for _name, _w in VEC_NAMES:
    VEC_AT[_name] = (_n, _n + _w)
    _n += _w
NVEC = _n

FOX_Q, FOX_V, FOX_F, RWKV_AT, GATE_AT = 0, 1024, 1536, 1544, 3336


class Shared:
    pass


class Chain:

    def __init__(self, eng, sem):
        self.eng, self.sem, self.base, self.k, self.reg, self.per = eng, sem, 0, 0, None, 0

    def value(self):
        v = self.base + self.k
        return v if self.reg is None else self.reg * self.per + v

    def __call__(self, ins):
        ins.then_inc(self.sem, 1)
        self.k += 1
        self.eng.wait_ge(self.sem, self.value())

    @contextmanager
    def loop(self, n, per):
        self.base, self.k = self.base + self.k, 0
        with self.eng.Fori(0, n) as i:
            self.reg, self.per = i, per
            yield i
        assert self.k == per, (self.k, per)
        self.reg, self.base, self.k = None, self.base + n * per, 0

    @contextmanager
    def fresh_loop(self, n):
        with self.eng.Fori(0, n) as i:
            self.eng.sem_clear(self.sem)
            self.base = self.k = 0
            yield i


def settle(m, eng, sem, value):
    eng.wait_ge(sem, value)
    eng.sem_inc(m.settled, 1)


RAW = 3
AHEAD = 3
CH = 1024


class Stream:

    def __init__(self, m, segments):
        self.m, self.start, self.segments = m, {}, segments
        n = 0
        for name, (rounds, period, parts) in segments.items():
            self.start[name] = n
            n += rounds * period
        self.total = n

    def count(self, name, k, it, per_chunk=1, more=0):
        n = per_chunk * (self.start[name] + k) + more
        return n if isinstance(it, int) and it == 0 else it * (per_chunk * self.segments[name][1]) + n

    def full(self, name, k, it):
        n = self.start[name] + k
        value = 16 * (n // RAW + 1)
        period = self.segments[name][1]
        if isinstance(it, int) and it == 0:
            return value
        assert period % RAW == 0
        return it * (16 * period // RAW) + value

    def done(self, eng, name, k, it=0):
        eng.wait_ge(self.m.chunk_done, self.count(name, k, it, more=1))

    def weights(self, pe, name, k, it=0):
        pe.wait_ge(self.m.split_done, self.count(name, k, it, more=1))
        slot = (self.start[name] + k) % AHEAD
        return self.m.w_high[:, slot, :], self.m.w_low[:, slot, :]

    def high(self, act, name, k, it=0):
        n = self.start[name] + k + AHEAD
        if n >= self.total:
            return
        act.wait_ge(self.m.slot_full[n % RAW], self.full(name, k + AHEAD, it))
        self.m.nc.scalar.copy(self.m.w_high[:, n % AHEAD, :], self.m.raw[:, n % RAW, :]
                              ).then_inc(self.m.high_done, 1)

    def low(self, dve, name, k, it=0):
        n = self.start[name] + k + AHEAD
        if n >= self.total:
            return
        dve.wait_ge(self.m.high_done, self.count(name, k, it, more=AHEAD + 1))
        self.m.nc.vector.tensor_tensor(self.m.w_low[:, n % AHEAD, :], self.m.raw[:, n % RAW, :],
                                       self.m.w_high[:, n % AHEAD, :].bitcast(F32), ALU.subtract
                                       ).then_inc(self.m.split_done, 1)

    def load(self, sp, name, k, it=0, first=False):
        rounds, period, parts = self.segments[name]
        slot = (self.start[name] + k) % RAW
        if not first:
            settle(self.m, sp, self.m.split_done, self.count(name, k, it, more=1 - RAW))
        dst, src = parts(self.m.raw[:, slot, :], k, it)
        sp.dma_start(dst, src).then_inc(self.m.slot_full[slot], 16)

    def loads(self, sp, *names):
        rounds, period, _ = self.segments[names[-1]]
        lo = self.start[names[0]] + RAW + AHEAD
        hi = min(self.start[names[-1]] + rounds * period + RAW + AHEAD, self.total)
        for name, (rounds, period, _) in self.segments.items():
            at = self.start[name]
            a, b = max(lo, at), min(hi, at + rounds * period)
            if a >= b:
                continue
            off, whole = a - at, (b - a) // period
            if rounds > 1 and whole > 1:
                with sp.Fori(0, whole) as it:
                    for j in range(off, off + period):
                        self.load(sp, name, j % period, it + j // period)
                off += whole * period
            for j in range(off, b - at):
                self.load(sp, name, j % period, j // period)


def columns(w, period):
    kt = w.shape[0] // P
    width = CH // kt
    src = w.rearrange("(k p) f -> p k f", p=P)

    def parts(slot, k, it):
        return slot.rearrange("p (k f) -> p k f", k=kt), src[:, :, bass.ds(it * (period * width) + k * width, width)]
    return parts


def wide_columns(w, period):
    src = w.rearrange("(k p) f -> p k f", p=P)

    def parts(slot, k, it):
        return (slot.rearrange("p (k f) -> p k f", f=256),
                src[:, (k % 2) * 4:(k % 2) * 4 + 4, bass.ds(it * (period * P) + (k // 2) * 256, 256)])
    return parts


def expert_parts(gate, up, down):
    views = [w.rearrange("e (k p) f -> p e k f", p=P) for w in (gate, up, down)]

    def parts(slot, k, it):
        which, at = (k % 2, k // 2) if k < 8 else (2, k - 8)
        kt = KT if k < 8 else 4
        width = CH // kt
        src = views[which][:, bass.ds(it, 1), :, at * width:(at + 1) * width].rearrange("p e k f -> p (e k) f")
        return slot.rearrange("p (k f) -> p k f", k=kt), src
    return parts


STEP = 6


def table_parts(u, v, tiles):
    def parts(slot, k, it):
        which, first = tiles[k]
        return slot, (v if which == "v" else u)[bass.ds(it * STEP + first, 1)].rearrange("a p f -> p (a f)")
    return parts


def merge_parts(w_in, p_fox, p_rwkv):
    gates, fox, rwkv = (w.rearrange("(k p) f -> p k f", p=P) for w in (w_in, p_fox, p_rwkv))

    def parts(slot, k, it):
        group, k = divmod(k, 6)
        at = it * 512 + group * 256
        if k < 4:
            return (slot.rearrange("p (k f) -> p k f", k=KT),
                    gates[:, :, bass.ds(at + (GATE_AT + (k // 2) * D + (k % 2) * P), P)])
        return slot.rearrange("p (k f) -> p k f", k=4), (fox, rwkv)[k - 4][:, :, bass.ds(at, 256)]
    return parts


def times(nc, out, w, a, start, stop, **more):
    nc.tensor.matmul(out, w[0], a[0], start=start, stop=False, **more)
    nc.tensor.matmul(out, w[0], a[1], start=False, stop=False, **more)
    return nc.tensor.matmul(out, w[1], a[0], start=False, stop=stop, **more)


def setup(nc, m):
    vec_loaded, lam_loaded, x_loaded, made, chain_s, silu_done = (
        m.sem(n) for n in ("vec_loaded", "lam_loaded", "x_loaded", "made", "setup_chain", "silu_done"))
    with nc.Block() as block:
        @block.sync
        def _(sp):
            sp.dma_start(m.vec[:], m.i["vecs"]).then_inc(vec_loaded, 16)
            for n in range(RAW):
                m.stream.load(sp, "ada", n, first=True)
            sp.dma_start(m.lam_row[:], m.i["lams"].broadcast_to([P, 4 * DH])).then_inc(lam_loaded, 16)
            sp.dma_start(m.xT[:], m.i["xT"].rearrange("(k p) t -> p k t", p=P)).then_inc(x_loaded, 16)
            sp.dma_start(m.router_w[:], m.i["router_w"].rearrange("(k p) f -> p k f", p=P)).then_inc(x_loaded, 16)
            sp.dma_start(m.router_b[:], m.i["router_b"].broadcast_to([P, 20])).then_inc(x_loaded, 16)
            for n in range(RAW, RAW + AHEAD):
                m.stream.load(sp, "ada", n)
            sp.wait_ge(x_loaded, 48)

        @block.gpsimd
        def _(pool):
            link = Chain(pool, chain_s)
            link(nc.gpsimd.memset(m.ones[:], 1.0))
            link(nc.gpsimd.memset(m.zeros[:], 0.0))
            link(nc.gpsimd.memset(m.ident[:], 0.0))
            link(nc.gpsimd.affine_select(out=m.ident[:], in_=m.ident[:], compare_op=ALU.not_equal, fill=1.0,
                                         base=0, pattern=[[-1, P]], channel_multiplier=1))
            link(nc.gpsimd.memset(m.halves[:], 0.0))
            link(nc.gpsimd.memset(m.halves[0:DH, 0:DH], 1.0))
            link(nc.gpsimd.memset(m.halves[DH:P, DH:P], 1.0))
            link(nc.gpsimd.iota(m.iota_i[:], pattern=[[1, P]], base=0, channel_multiplier=0))
            link(nc.gpsimd.tensor_copy(m.iota[:], m.iota_i[:]))

        @block.scalar
        def _(act):
            act.wait_ge(vec_loaded, 16)
            nc.scalar.activation(m.cond[:], m.v("c"), ACT.Silu).then_inc(silu_done, 1)
            for n in range(AHEAD):
                m.stream.high(act, "ada", n - AHEAD)
            act.wait_ge(silu_done, 1)
            nc.scalar.copy(m.cond_high[:], m.cond[:].unsqueeze(2).to_broadcast([P, KT, P])).then_inc(silu_done, 1)
            act.wait_ge(x_loaded, 48)
            nc.scalar.copy(m.router_h[:], m.router_w[:]).then_inc(silu_done, 1)

        @block.vector
        def _(dve):
            link = Chain(dve, made)
            dve.wait_ge(lam_loaded, 16)
            link(nc.vector.tensor_tensor(m.lam_prod[:], m.lam_row[:].rearrange("p (a b d) -> p a b d", a=2, b=2)[:, :, 0, :],
                                         m.lam_row[:].rearrange("p (a b d) -> p a b d", a=2, b=2)[:, :, 1, :], ALU.mult))
            link(nc.vector.tensor_reduce(m.lam_dot[:], m.lam_prod[:], AX.X, ALU.add))
            for n in range(AHEAD):
                m.stream.low(dve, "ada", n - AHEAD)
            dve.wait_ge(silu_done, 3)
            link(nc.vector.tensor_tensor(m.cond_low[:], m.cond[:].unsqueeze(2).to_broadcast([P, KT, P]),
                                         m.cond_high[:].bitcast(F32), ALU.subtract))
            link(nc.vector.tensor_tensor(m.router_l[:], m.router_w[:], m.router_h[:].bitcast(F32), ALU.subtract))


def modulation(nc, m):
    mod_free, mod_chain, lam_exp, steps = (m.sem(n) for n in ("mod_free", "mod_chain", "lam_exp", "mod_steps"))
    with nc.Block() as block, ExitStack() as mem:
        own = mem.enter_context(nc.sbuf_tensor("mod_own", [P, KT, P], F32))

        @block.sync
        def _(sp):
            m.stream.loads(sp, "ada")

        @block.tensor
        def _(pe):
            pe.sem_inc(mod_free, 3)
            with pe.Fori(0, 2) as it:
                for v in range(3):
                    pe.wait_ge(mod_free, it * 3 + (v + 1))
                    for k in range(KT):
                        w = m.stream.weights(pe, "ada", v * KT + k, it)
                        for j in range(4):
                            c = 4 * (k % 2) + j
                            last = times(nc, m.ps[:, 2 * v + k // 4, (k // 2 % 2) * 256:(k // 2 % 2 + 1) * 256],
                                         [m.cond_high[:, c, :], m.cond_low[:, c, :]],
                                         [x[:, j * 256:(j + 1) * 256] for x in w], start=c == 0, stop=c == KT - 1)
                        last.then_inc(m.chunk_done, 1)

        @block.scalar
        def _(act):
            nc.scalar.activation(m.lam_e[:], m.lam_dot[:], ACT.Exp).then_inc(lam_exp, 1)
            with act.Fori(0, 2) as it:
                for k in range(3 * KT):
                    m.stream.done(act, "ada", k, it)
                    m.stream.high(act, "ada", k, it)

        @block.vector
        def _(dve):
            link = Chain(dve, steps)
            with link.loop(2, 6) as it:
                for v in range(3):
                    for k in range(KT):
                        m.stream.done(dve, "ada", v * KT + k, it)
                        m.stream.low(dve, "ada", v * KT + k, it)
                    link(nc.vector.tensor_tensor(own[:], m.ps[:, 2 * v:2 * v + 2, :].rearrange(
                        "p b (k c) -> p (b k) c", c=P), m.ident[:].unsqueeze(1).to_broadcast([P, KT, P]), ALU.mult))
                    tiles = bass.ds(it * (3 * KT) + v * KT, KT)
                    link(nc.vector.tensor_reduce(m.mod[:, tiles], own[:], AX.X, ALU.add))
                    nc.vector.tensor_tensor(m.mod[:, tiles], m.mod[:, tiles], m.v("ada_b")[:, tiles], ALU.add
                                            ).then_inc(mod_free, 1)
            dve.wait_ge(mod_free, 9)
            link = Chain(dve, mod_chain)
            for out, scale, norm in ((m.norm1, 1, "norm_mix"), (m.norm2, 4, "norm_ffn")):
                link(nc.vector.tensor_scalar(out[:], m.mod[:, scale * KT:(scale + 1) * KT], 1.0, None, ALU.add))
                link(nc.vector.tensor_tensor(out[:], out[:], m.v(norm), ALU.mult))
            dve.wait_ge(lam_exp, 1)
            link(nc.vector.tensor_tensor(m.neg_lam[:], m.lam_e[:, 1:2], m.lam_e[:, 0:1], ALU.subtract))
            link(nc.vector.tensor_scalar(m.neg_lam[:], m.neg_lam[:], -LAM_INIT, None, ALU.add))


def rms_norm(nc, m, name, scale, shift, high, low, keep=False):
    squared, summed, rooted, chain_s, scaled, highs = (m.sem(f"{name}_{n}") for n in (
        "squared", "summed", "rooted", "chain", "scaled", "highs"))
    with nc.Block() as block, ExitStack() as mem:
        sq = mem.enter_context(nc.sbuf_tensor(f"{name}_sq", [P, KT, T], F32))
        var = mem.enter_context(nc.sbuf_tensor(f"{name}_var", [P, T], F32))
        rstd = mem.enter_context(nc.sbuf_tensor(f"{name}_rstd", [P, T], F32))
        out = m.xT if keep else sq

        @block.scalar
        def _(act):
            for k in range(KT):
                nc.scalar.activation(sq[:, k, :], m.xT[:, k, :], ACT.Square).then_inc(squared, 1)
            act.wait_ge(chain_s, 1)
            nc.scalar.activation(rstd[:], var[:], ACT.Sqrt).then_inc(rooted, 1)
            for k in range(KT):
                act.wait_ge(scaled, k + 1)
                nc.scalar.copy(high[:, k, :], out[:, k, :]).then_inc(highs, 1)

        @block.tensor
        def _(pe):
            for k in range(KT):
                pe.wait_ge(squared, k + 1)
                last = nc.tensor.matmul(m.ps[:, 0, :], m.ones[:], sq[:, k, :], start=k == 0, stop=k == KT - 1)
            last.then_inc(summed, 1)

        @block.vector
        def _(dve):
            link = Chain(dve, chain_s)
            dve.wait_ge(summed, 1)
            link(nc.vector.tensor_scalar(var[:], m.ps[:, 0, :], 1.0 / D, EPS, ALU.mult, ALU.add))
            dve.wait_ge(rooted, 1)
            link(nc.vector.reciprocal(rstd[:], rstd[:]))

            def rest(k):
                dve.wait_ge(highs, k + 1)
                nc.vector.tensor_tensor(low[:, k, :], out[:, k, :], high[:, k, :].bitcast(F32), ALU.subtract)

            for k in range(KT):
                ins = nc.vector.scalar_tensor_tensor(out=out[:, k, :], in0=m.xT[:, k, :], scalar=scale[:, k:k + 1],
                                                     in1=rstd[:], op0=ALU.mult, op1=ALU.mult)
                if shift is not None:
                    link(ins)
                    ins = nc.vector.tensor_scalar(out[:, k, :], out[:, k, :], shift[:, k:k + 1], None, ALU.add)
                ins.then_inc(scaled, 1)
                if k:
                    rest(k - 1)
            rest(KT - 1)


def project(nc, m, pe, name, high, low, bank_free, chunks=8, n0=0, banks=8):
    if n0 == 0:
        pe.sem_inc(bank_free, banks)
    for k in range(chunks):
        w = [x.rearrange("p (c f) -> p c f", c=KT) for x in m.stream.weights(pe, name, k)]
        n = n0 + k
        pe.wait_ge(bank_free, n + 1)
        for c in range(KT):
            last = times(nc, m.ps[:, n % banks, :], [x[:, c, :] for x in w], [high[:, c, :], low[:, c, :]],
                         start=c == 0, stop=c == KT - 1)
        last.then_inc(m.chunk_done, 1)


def token_major(nc, m, pe, name, high, low, bank_free, groups, n0, banks=8):
    for k in range(2 * groups):
        w = m.stream.weights(pe, name, k)
        n = n0 + 4 * (k // 2)
        for tt in range(TT):
            if k % 2 == 0:
                pe.wait_ge(bank_free, n + tt + 1)
            toks = slice(tt * P, (tt + 1) * P)
            for j in range(4):
                c = 4 * (k % 2) + j
                last = times(nc, m.ps[:, (n + tt) % banks, 0:256], [high[:, c, toks], low[:, c, toks]],
                             [x[:, j * 256:(j + 1) * 256] for x in w], start=c == 0, stop=c == KT - 1)
        last.then_inc(m.chunk_done, 1)


def read_token_major(nc, bank_free, ps, out, k, n0, banks=8):
    if k % 2:
        for tt in range(TT):
            nc.scalar.copy(out[:, tt, (k // 2) * 256:(k // 2 + 1) * 256], ps[:, (n0 + 4 * (k // 2) + tt) % banks, 0:256]
                           ).then_inc(bank_free, 1)


def qkv_projection(nc, m, high, low, qT, kT, v):
    bank_free = m.sem("qkv_bank_free")
    with nc.Block() as block:
        @block.sync
        def _(sp):
            m.stream.loads(sp, "attn_qk", "attn_v")

        @block.tensor
        def _(pe):
            project(nc, m, pe, "attn_qk", high, low, bank_free, chunks=16)
            token_major(nc, m, pe, "attn_v", high, low, bank_free, 4, 16)

        @block.scalar
        def _(act):
            for n in range(16):
                m.stream.done(act, "attn_qk", n)
                if n < HEADS:
                    nc.scalar.mul(qT[:, n, :], m.ps[:, n % 8, :], DH ** -0.5).then_inc(bank_free, 1)
                else:
                    nc.scalar.copy(kT[:, n - HEADS, :], m.ps[:, n % 8, :]).then_inc(bank_free, 1)
                m.stream.high(act, "attn_qk", n)
            for n in range(8):
                m.stream.done(act, "attn_v", n)
                read_token_major(nc, bank_free, m.ps, v, n, 16)
                m.stream.high(act, "attn_v", n)

        @block.vector
        def _(dve):
            for n in range(16 + 8):
                m.stream.done(dve, "attn_qk", n)
                m.stream.low(dve, "attn_qk", n)


def diff_attention(nc, m, qT, kT, v):
    (qk_staged, v_staged, scored, biased, maxed, exped, mixed, turned, turned_out, unit_done, o_out, dist_made,
     chain_s) = (m.sem("da_" + n) for n in (
         "qk_staged", "v_staged", "scored", "biased", "maxed", "exped", "mixed", "turned", "turned_out",
         "unit_done", "o_out", "dist_made", "chain"))
    rounds, per = HEADS // 2, 2 * TT
    with nc.Block() as block, ExitStack() as mem:
        sb = lambda n, s, dt=F32: mem.enter_context(nc.sbuf_tensor("da_" + n, s, dt))
        dist_i = sb("dist_i", [P, TT, T], I32)
        dist = sb("dist", [P, TT, T])
        slope = sb("slope", [P, HEADS])
        q_st = sb("q_st", [P, 2, T])
        k_st = sb("k_st", [P, 2, T])
        v_st = sb("v_st", [P, 2, TT, P])
        s = sb("s", [P, 2, 2, T])
        e = sb("e", [P, 2, 2, T])
        neg_max = sb("neg_max", [P, 2, 2])
        z = sb("z", [P, 2, 2])
        a = sb("a", [P, 2, T])
        aT = sb("aT", [P, 2, TT, P])

        @block.gpsimd
        def _(pool):
            nc.gpsimd.iota(dist_i[:], pattern=[[P, TT], [-1, T]], base=0, channel_multiplier=1).then_inc(dist_made, 1)
            with pool.Fori(0, rounds) as it:
                for j in range(2):
                    pool.wait_ge(unit_done, it * per + TT * (j + 1))
                    for staged, whole in ((q_st, qT), (k_st, kT)):
                        nc.gpsimd.tensor_copy(staged[:, j, :], whole[:, bass.ds(it * 2 + j, 1), :].rearrange(
                            "p a t -> p (a t)")).then_inc(qk_staged, 1)
                    nc.gpsimd.tensor_copy(v_st[:, j, :, :], v[:, :, bass.ds((it * 2 + j) * P, P)]
                                          ).then_inc(v_staged, 1)

        @block.tensor
        def _(pe):
            pe.sem_inc(unit_done, per)
            pe.sem_inc(biased, 4)
            pe.sem_inc(turned_out, 2)
            pe.sem_inc(o_out, 2)

            def values(it, u):
                j, b = u // TT, u % 2
                pe.wait_ge(mixed, it * per + (u + 1))
                pe.wait_ge(turned_out, it * per + (u + 1))
                for kt in range(TT):
                    last = nc.tensor.transpose(m.ps[:, 4 * b + 2, kt * P:(kt + 1) * P],
                                               a[:, b, kt * P:(kt + 1) * P], m.ident[:])
                last.then_inc(turned, 1)
                if u % TT == 0:
                    pe.wait_ge(v_staged, it * 2 + (j + 1))
                pe.wait_ge(turned_out, it * per + (u + 3))
                pe.wait_ge(o_out, it * per + (u + 1))
                for kt in range(TT):
                    last = nc.tensor.matmul(m.ps[:, 4 * b + 3, 0:P], v_st[:, j, kt, :], aT[:, b, kt, :],
                                            start=kt == 0, stop=kt == TT - 1)
                last.then_inc(unit_done, 1)

            with pe.Fori(0, rounds) as it:
                for u in range(per):
                    j, qt = divmod(u, TT)
                    if qt == 0:
                        pe.wait_ge(qk_staged, it * 4 + 2 * (j + 1))
                    pe.wait_ge(biased, it * (2 * per) + (2 * u + 2))
                    for c in range(2):
                        rows = slice(c * DH, (c + 1) * DH)
                        nc.tensor.matmul(m.ps[:, 4 * (u % 2) + c, :], q_st[rows, j, qt * P:(qt + 1) * P],
                                         k_st[rows, j, :], start=True, stop=True).then_inc(scored, 1)
                    if u >= 1:
                        values(it, u - 1)
                values(it, per - 1)

        @block.scalar
        def _(act):
            def outputs(it, u):
                act.wait_ge(turned, it * per + (u + 1))
                nc.scalar.copy(aT[:, u % 2, :, :], m.ps[:, 4 * (u % 2) + 2, :].rearrange("p (k q) -> p k q", k=TT)
                               ).then_inc(turned_out, 1)
                act.wait_ge(unit_done, it * per + (per + u + 1))
                nc.scalar.copy(m.oT[:, bass.ds(it * 2 + u // TT, 1), (u % TT) * P:(u % TT + 1) * P],
                               m.ps[:, 4 * (u % 2) + 3, 0:P].rearrange("p (a q) -> p a q", a=1)).then_inc(o_out, 1)

            act.wait_ge(dist_made, 1)
            nc.scalar.activation(dist[:], dist_i[:], ACT.Abs).then_inc(dist_made, 1)
            with act.Fori(0, rounds) as it:
                for u in range(per):
                    b = u % 2
                    act.wait_ge(maxed, it * per + (u + 1))
                    for c in range(2):
                        nc.scalar.activation(e[:, b, c, :], s[:, b, c, :], ACT.Exp, bias=neg_max[:, b, c:c + 1],
                                             accum_out=z[:, b, c:c + 1]).then_inc(exped, 1)
                    if u >= 1:
                        outputs(it, u - 1)
                outputs(it, per - 1)

        @block.vector
        def _(dve):
            link = Chain(dve, chain_s)
            for h in range(HEADS):
                link(nc.vector.memset(slope[:, h:h + 1], -(2.0 ** (-8.0 * (h + 1) / HEADS))))
            dve.wait_ge(dist_made, 2)
            with link.loop(rounds, 3 * per) as it:
                for u in range(per):
                    j, qt = divmod(u, TT)
                    b = u % 2
                    for c in range(2):
                        dve.wait_ge(scored, it * (2 * per) + (2 * u + c + 1))
                        nc.vector.scalar_tensor_tensor(out=s[:, b, c, :], in0=dist[:, qt, :],
                                                       scalar=slope[:, bass.ds(it * 2 + j, 1)],
                                                       in1=m.ps[:, 4 * b + c, :], op0=ALU.mult, op1=ALU.add
                                                       ).then_inc(biased, 1)
                    dve.wait_ge(biased, it * (2 * per) + (2 * u + 6))
                    nc.vector.tensor_reduce(neg_max[:, b, :], s[:, b, :, :], AX.X, ALU.max, negate=True
                                            ).then_inc(maxed, 1)
                    dve.wait_ge(exped, it * (2 * per) + (2 * u + 2))
                    link(nc.vector.reciprocal(z[:, b, :], z[:, b, :]))
                    link(nc.vector.tensor_tensor(z[:, b, 1:2], z[:, b, 1:2], m.neg_lam[:], ALU.mult))
                    dve.wait_ge(turned_out, it * per + (u + 1))
                    link(nc.vector.tensor_scalar(a[:, b, :], e[:, b, 1, :], z[:, b, 1:2], None, ALU.mult))
                    nc.vector.scalar_tensor_tensor(out=a[:, b, :], in0=e[:, b, 0, :], scalar=z[:, b, 0:1],
                                                   in1=a[:, b, :], op0=ALU.mult, op1=ALU.add).then_inc(mixed, 1)
                    dve.wait_ge(mixed, it * per + (u + 1))


def head_norm(nc, m, high, low):
    squared, summed, rooted, chain_s, highs = (m.sem("hn_" + n) for n in (
        "squared", "summed", "rooted", "chain", "highs"))
    with nc.Block() as block, ExitStack() as mem:
        sq = mem.enter_context(nc.sbuf_tensor("hn_sq", [P, HEADS, T], F32))
        gain = mem.enter_context(nc.sbuf_tensor("hn_gain", [P, 1], F32))

        @block.scalar
        def _(act):
            for h in range(HEADS):
                nc.scalar.activation(sq[:, h, :], m.oT[:, h, :], ACT.Square).then_inc(squared, 1)
            for h in range(HEADS):
                act.wait_ge(chain_s, 2 + h)
                nc.scalar.activation(sq[:, h, :], sq[:, h, :], ACT.Sqrt).then_inc(rooted, 1)
            for h in range(HEADS):
                act.wait_ge(chain_s, 1 + HEADS + 2 * (h + 1))
                nc.scalar.copy(high[:, h, :], m.oT[:, h, :]).then_inc(highs, 1)

        @block.tensor
        def _(pe):
            for h in range(HEADS):
                pe.wait_ge(squared, h + 1)
                nc.tensor.matmul(m.ps[:, h, :], m.ones[:], sq[:, h, :], start=True, stop=True).then_inc(summed, 1)

        @block.vector
        def _(dve):
            link = Chain(dve, chain_s)
            link(nc.vector.tensor_scalar(gain[:], m.v("subln"), 1.0 - LAM_INIT, None, ALU.mult))
            for h in range(HEADS):
                dve.wait_ge(summed, h + 1)
                link(nc.vector.tensor_scalar(sq[:, h, :], m.ps[:, h, :], 1.0 / P, EPS, ALU.mult, ALU.add))
            for h in range(HEADS):
                dve.wait_ge(rooted, h + 1)
                link(nc.vector.reciprocal(sq[:, h, :], sq[:, h, :]))
                link(nc.vector.scalar_tensor_tensor(out=m.oT[:, h, :], in0=m.oT[:, h, :], scalar=gain[:],
                                                    in1=sq[:, h, :], op0=ALU.mult, op1=ALU.mult))
            for h in range(HEADS):
                dve.wait_ge(highs, h + 1)
                nc.vector.tensor_tensor(low[:, h, :], m.oT[:, h, :], high[:, h, :].bitcast(F32), ALU.subtract)


def add_projection(nc, m, high, low):
    bank_free = m.sem("ap_bank_free")
    with nc.Block() as block:
        @block.sync
        def _(sp):
            m.stream.loads(sp, "attn_out")

        @block.tensor
        def _(pe):
            project(nc, m, pe, "attn_out", high, low, bank_free)

        @block.scalar
        def _(act):
            for n in range(KT):
                m.stream.done(act, "attn_out", n)
                m.stream.high(act, "attn_out", n)

        @block.vector
        def _(dve):
            for n in range(KT):
                m.stream.done(dve, "attn_out", n)
                nc.vector.scalar_tensor_tensor(out=m.xT[:, n, :], in0=m.ps[:, n, :],
                                               scalar=m.mod[:, 2 * KT + n:2 * KT + n + 1], in1=m.xT[:, n, :],
                                               op0=ALU.mult, op1=ALU.add).then_inc(bank_free, 1)
                m.stream.low(dve, "attn_out", n)


def first_of_equals(nc, link, out, eq, seen, width):
    link(nc.vector.memset(seen[:, :, 0:1], 0.0))
    for g in range(1, width):
        link(nc.vector.tensor_tensor(seen[:, :, g:g + 1], seen[:, :, g - 1:g], eq[:, :, g - 1:g], ALU.add))
    link(nc.vector.scalar_tensor_tensor(out=out, in0=seen[:], scalar=0.5, in1=eq, op0=ALU.is_lt, op1=ALU.mult))


def router(nc, m, high, low, gate_bc):
    G, E = EXPERT_GROUPS, EXPERTS // EXPERT_GROUPS
    logits_done, exps, chain_s, turned, gates_up, spread, spread_read = (m.sem("ro_" + n) for n in (
        "logits_done", "exps", "chain", "turned", "gates_up", "spread", "spread_read"))
    with nc.Block() as block, ExitStack() as mem:
        sb = lambda n, s: mem.enter_context(nc.sbuf_tensor("ro_" + n, s, F32))
        lg = sb("lg", [P, TT, G + EXPERTS])
        top, second, diff, ge, gs, w1 = (sb(n, [P, TT, 1]) for n in ("top", "second", "diff", "ge", "gs", "w1"))
        gx = sb("gx", [P, TT, G])
        eq, seen, oh_g, oh_1, oh_2, sel, ew = (sb(n, [P, TT, G]) for n in ("eq", "seen", "ohg", "oh1", "oh2", "sel", "ew"))
        prod = sb("prod", [P, TT, G, E])
        gates = sb("gates", [P, TT, G, E])
        gatesT = sb("gatesT", [EXPERTS, T])

        @block.tensor
        def _(pe):
            for tt in range(TT):
                for c in range(KT):
                    last = times(nc, m.ps[:, tt, 0:G + EXPERTS], [x[:, c, tt * P:(tt + 1) * P] for x in (high, low)],
                                 [m.router_h[:, c, :], m.router_l[:, c, :]], start=c == 0, stop=c == KT - 1)
                last.then_inc(logits_done, 1)
            pe.wait_ge(gates_up, 1)
            for tt in range(TT):
                nc.tensor.transpose(m.ps[0:EXPERTS, 4, tt * P:(tt + 1) * P],
                                    gates[:, tt, :, :].rearrange("p g e -> p (g e)"), m.ident[:]).then_inc(turned, 1)
            pe.wait_ge(gates_up, 2)
            for x in range(EXPERTS):
                if x >= 8:
                    pe.wait_ge(spread_read, x - 7)
                nc.tensor.matmul(m.ps[:, x % 8, :], m.ident[0:EXPERTS, x:x + 1].to_broadcast([EXPERTS, P]),
                                 gatesT[:], start=True, stop=True).then_inc(spread, 1)

        @block.scalar
        def _(act):
            act.wait_ge(exps, 1)
            nc.scalar.activation(gx[:], gx[:], ACT.Exp).then_inc(exps, 1)
            act.wait_ge(exps, 3)
            nc.scalar.activation(ge[:], diff[:], ACT.Exp).then_inc(exps, 1)
            for x in range(EXPERTS):
                act.wait_ge(spread, x + 1)
                nc.scalar.copy(gate_bc[:, x, :], m.ps[:, x % 8, :]).then_inc(spread_read, 1)

        @block.vector
        def _(dve):
            link = Chain(dve, chain_s)
            bc = lambda t, n: t[:].to_broadcast([P, TT, n])
            for tt in range(TT):
                dve.wait_ge(logits_done, tt + 1)
                link(nc.vector.tensor_tensor(lg[:, tt, :], m.ps[:, tt, 0:G + EXPERTS], m.router_b[:], ALU.add))
            link(nc.vector.tensor_reduce(top[:], lg[:, :, 0:G], AX.X, ALU.max))
            nc.vector.tensor_tensor(gx[:], lg[:, :, 0:G], bc(top, G), ALU.subtract).then_inc(exps, 1)
            link(nc.vector.tensor_tensor(eq[:], lg[:, :, 0:G], bc(top, G), ALU.is_equal))
            first_of_equals(nc, link, oh_g[:], eq[:], seen, G)
            dve.wait_ge(exps, 2)
            link(nc.vector.tensor_reduce(gs[:], gx[:], AX.X, ALU.add))
            link(nc.vector.reciprocal(gs[:], gs[:]))
            for g in range(G):
                link(nc.vector.tensor_tensor(prod[:, :, g, :], lg[:, :, G + g * E:G + (g + 1) * E],
                                             oh_g[:, :, g:g + 1].to_broadcast([P, TT, E]), ALU.mult))
            link(nc.vector.tensor_reduce(sel[:], prod[:].rearrange("p t g e -> p t e g"), AX.X, ALU.add))
            link(nc.vector.tensor_reduce(top[:], sel[:], AX.X, ALU.max))
            link(nc.vector.tensor_tensor(eq[:], sel[:], bc(top, E), ALU.is_equal))
            first_of_equals(nc, link, oh_1[:], eq[:], seen, E)
            link(nc.vector.scalar_tensor_tensor(out=ew[:], in0=oh_1[:], scalar=NEG, in1=sel[:], op0=ALU.mult, op1=ALU.add))
            link(nc.vector.tensor_reduce(second[:], ew[:], AX.X, ALU.max))
            link(nc.vector.tensor_tensor(eq[:], ew[:], bc(second, E), ALU.is_equal))
            first_of_equals(nc, link, oh_2[:], eq[:], seen, E)
            nc.vector.tensor_tensor(diff[:], second[:], top[:], ALU.subtract).then_inc(exps, 1)
            dve.wait_ge(exps, 4)
            link(nc.vector.tensor_scalar(w1[:], ge[:], 1.0, None, ALU.add))
            link(nc.vector.reciprocal(w1[:], w1[:]))
            link(nc.vector.tensor_tensor(w1[:], w1[:], gs[:], ALU.mult))
            link(nc.vector.tensor_tensor(ge[:], ge[:], w1[:], ALU.mult))
            link(nc.vector.tensor_tensor(oh_1[:], oh_1[:], bc(w1, E), ALU.mult))
            link(nc.vector.tensor_tensor(oh_2[:], oh_2[:], bc(ge, E), ALU.mult))
            link(nc.vector.tensor_tensor(ew[:], oh_1[:], oh_2[:], ALU.add))
            for g in range(G):
                ins = nc.vector.tensor_tensor(gates[:, :, g, :], ew[:], oh_g[:, :, g:g + 1].to_broadcast([P, TT, E]),
                                              ALU.mult)
                if g < G - 1:
                    link(ins)
            ins.then_inc(gates_up, 1)
            dve.wait_ge(turned, TT)
            nc.vector.tensor_copy(gatesT[:], m.ps[0:EXPERTS, 4, :]).then_inc(gates_up, 1)


def experts(nc, m, high, low, gate_bc):
    (gates_read, ups_read, ys_read, hid_made, hid_high, hid_low, ending, zeroed) = (m.sem("ex_" + n) for n in (
        "gates_read", "ups_read", "ys_read", "hid_made", "hid_high", "hid_low", "ending", "zeroed"))
    F = 4
    with nc.Block() as block, ExitStack() as mem:
        sb = lambda n, s, dt=F32: mem.enter_context(nc.sbuf_tensor("ex_" + n, s, dt))
        acc = sb("acc", [P, KT, T])
        hh, hl = sb("hh", [P, F, T], F32R), sb("hl", [P, F, T], F32R)
        sg, m1, hid = sb("sg", [P, 2, T]), sb("m1", [P, 2, T]), sb("hid", [P, 2, T])

        @block.sync
        def _(sp):
            m.stream.loads(sp, "experts")

        @block.tensor
        def _(pe):
            pe.sem_inc(ys_read, 8)
            pe.sem_inc(ups_read, 2)
            with pe.Fori(0, EXPERTS) as it:
                for k in range(2 * F):
                    w = [x.rearrange("p (c f) -> p c f", c=KT) for x in m.stream.weights(pe, "experts", k, it)]
                    pe.wait_ge(ys_read, it * 8 + (k + 1))
                    for c in range(KT):
                        last = times(nc, m.ps[:, k, :], [x[:, c, :] for x in w], [high[:, c, :], low[:, c, :]],
                                     start=c == 0, stop=c == KT - 1)
                    last.then_inc(m.chunk_done, 1)
                for k in range(F):
                    w = [x.rearrange("p (c f) -> p c f", c=F) for x in m.stream.weights(pe, "experts", 8 + k, it)]
                    if k == 0:
                        pe.wait_ge(hid_low, it * F + F)
                    for part in range(2):
                        for c in range(F):
                            last = times(nc, m.ps[:, 2 * k + part, :], [x[:, c, part * P:(part + 1) * P] for x in w],
                                         [hh[:, c, :], hl[:, c, :]], start=c == 0, stop=c == F - 1)
                    last.then_inc(m.chunk_done, 1)

        @block.scalar
        def _(act):
            with act.Fori(0, EXPERTS) as it:
                for f in range(F):
                    m.stream.done(act, "experts", 2 * f, it)
                    act.wait_ge(ups_read, it * F + (f + 1))
                    nc.scalar.activation(sg[:, f % 2, :], m.ps[:, 2 * f, :], ACT.Silu).then_inc(gates_read, 1)
                    m.stream.high(act, "experts", 2 * f, it)
                    act.wait_ge(hid_made, it * F + (f + 1))
                    nc.scalar.copy(hh[:, f, :], hid[:, f % 2, :]).then_inc(hid_high, 1)
                    m.stream.high(act, "experts", 2 * f + 1, it)
                for k in range(8, 12):
                    m.stream.done(act, "experts", k, it)
                    m.stream.high(act, "experts", k, it)

        @block.vector
        def _(dve):
            nc.vector.memset(acc[:], 0.0).then_inc(zeroed, 1)
            dve.wait_ge(zeroed, 1)
            with dve.Fori(0, EXPERTS) as it:
                for f in range(F):
                    m.stream.done(dve, "experts", 2 * f, it)
                    m.stream.low(dve, "experts", 2 * f, it)
                    m.stream.done(dve, "experts", 2 * f + 1, it)
                    dve.wait_ge(gates_read, it * F + (f + 1))
                    nc.vector.tensor_tensor(m1[:, f % 2, :], sg[:, f % 2, :], m.ps[:, 2 * f + 1, :], ALU.mult
                                            ).then_inc(ups_read, 1)
                    dve.wait_ge(ups_read, it * F + (f + 3))
                    nc.vector.tensor_tensor(hid[:, f % 2, :], m1[:, f % 2, :],
                                            gate_bc[:, bass.ds(it, 1), :].rearrange("p a t -> p (a t)"),
                                            ALU.mult).then_inc(hid_made, 1)
                    dve.wait_ge(hid_high, it * F + (f + 1))
                    nc.vector.tensor_tensor(hl[:, f, :], hid[:, f % 2, :], hh[:, f, :].bitcast(F32), ALU.subtract
                                            ).then_inc(hid_low, 1)
                    m.stream.low(dve, "experts", 2 * f + 1, it)
                dve.wait_ge(ys_read, it * 8 + 8)
                for k in range(F):
                    m.stream.done(dve, "experts", 8 + k, it)
                    for n in (2 * k, 2 * k + 1):
                        nc.vector.tensor_tensor(acc[:, n, :], acc[:, n, :], m.ps[:, n, :], ALU.add
                                                ).then_inc(ys_read, 1)
                    m.stream.low(dve, "experts", 8 + k, it)
            dve.wait_ge(ys_read, 8 + 8 * EXPERTS)
            for n in range(KT):
                nc.vector.scalar_tensor_tensor(out=m.xT[:, n, :], in0=acc[:, n, :],
                                               scalar=m.mod[:, 5 * KT + n:5 * KT + n + 1], in1=m.xT[:, n, :],
                                               op0=ALU.mult, op1=ALU.add).then_inc(ending, 1)


def second_projection(nc, m, high, low, fq, fk, fv, cols, negc, cq):
    bank_free, f_done, f_steps, f_chain, c_ready, c_turned, spread, spread_read, c_read = (m.sem("sp_" + n) for n in (
        "bank_free", "f_done", "f_steps", "f_chain", "c_ready", "c_turned", "spread", "spread_read", "c_read"))
    f_loaded = m.sem("sp_f_loaded")
    with nc.Block() as block, ExitStack() as mem:
        sb = lambda n, s: mem.enter_context(nc.sbuf_tensor("sp_" + n, s, F32))
        f_w, f_b = sb("f_w", [P, KT, HEADS]), sb("f_b", [HEADS, 1])
        fx, fa, fc, f1 = (sb(n, [HEADS, T]) for n in ("fx", "fa", "fc", "f1"))

        @block.sync
        def _(sp):
            sp.dma_start(f_w[:], m.i["f_w"].rearrange("(k p) f -> p k f", p=P)).then_inc(f_loaded, 16)
            sp.dma_start(f_b[:], m.i["f_b"]).then_inc(f_loaded, 16)
            m.stream.loads(sp, "fox_qk", "fox_v", "rwkv_in")

        @block.tensor
        def _(pe):
            pe.wait_ge(f_loaded, 32)
            for c in range(KT):
                last = nc.tensor.matmul(m.ps[0:HEADS, 7, :], f_w[:, c, :], m.xT[:, c, :], start=c == 0, stop=c == KT - 1)
            last.then_inc(f_done, 1)
            project(nc, m, pe, "fox_qk", high, low, bank_free, banks=7)
            token_major(nc, m, pe, "fox_v", high, low, bank_free, 2, 8, banks=7)
            project(nc, m, pe, "rwkv_in", high, low, bank_free, chunks=14, n0=16, banks=7)
            pe.wait_ge(c_ready, 1)
            pe.wait_ge(bank_free, 7 + 30)
            for tt in range(TT):
                nc.tensor.transpose(m.ps[:, 7, tt * HEADS:(tt + 1) * HEADS], fc[:, tt * P:(tt + 1) * P],
                                    m.ident[0:HEADS, 0:HEADS]).then_inc(c_turned, 1)
            pe.wait_ge(c_ready, 2)
            for h in range(HEADS):
                if h >= 6:
                    pe.wait_ge(spread_read, h - 5)
                nc.tensor.matmul(m.ps[:, h % 6, :], m.ident[0:HEADS, h:h + 1].to_broadcast([HEADS, P]), fx[:],
                                 start=True, stop=True).then_inc(spread, 1)

        @block.scalar
        def _(act):
            act.wait_ge(f_chain, 3)
            nc.scalar.activation(fa[:], fx[:], ACT.Abs).then_inc(f_steps, 1)
            act.wait_ge(f_steps, 1)
            nc.scalar.activation(fc[:], fa[:], ACT.Exp, scale=-1.0).then_inc(f_steps, 1)
            act.wait_ge(f_steps, 2)
            nc.scalar.activation(fa[:], fc[:], ACT.Ln, bias=1.0).then_inc(f_steps, 1)
            for n in range(8 + 4 + 14):
                m.stream.done(act, "fox_qk", n)
                bank = m.ps[:, (n if n < 8 else n + 4) % 7, :]
                if n < 4:
                    nc.scalar.mul(fq[:, n, :], bank, DH ** -0.5).then_inc(bank_free, 1)
                elif n < 8:
                    nc.scalar.copy(fk[:, n - 4, :], bank).then_inc(bank_free, 1)
                elif n < 12:
                    read_token_major(nc, bank_free, m.ps, fv, n - 8, 8, banks=7)
                else:
                    nc.scalar.copy(cols[:, n - 12, 1:T + 1], bank).then_inc(bank_free, 1)
                m.stream.high(act, "fox_qk", n)
            for h in range(HEADS):
                act.wait_ge(spread, h + 1)
                nc.scalar.copy(negc[:, h, :], m.ps[:, h % 6, :]).then_inc(spread_read, 1)

        @block.vector
        def _(dve):
            link = Chain(dve, f_chain)
            link(nc.vector.memset(cols[:, :, 0:1], 0.0))
            link(nc.vector.memset(f1[:], 1.0))
            dve.wait_ge(f_done, 1)
            dve.wait_ge(f_loaded, 32)
            link(nc.vector.tensor_scalar(fx[:], m.ps[0:HEADS, 7, :], f_b[:], None, ALU.add))
            dve.wait_ge(f_steps, 3)
            link(nc.vector.scalar_tensor_tensor(out=fx[:], in0=fx[:], scalar=0.0, in1=fa[:], op0=ALU.min,
                                                op1=ALU.subtract))
            nc.vector.tensor_tensor_scan(fc[:], f1[:], fx[:], 0.0, ALU.mult, ALU.add).then_inc(c_ready, 1)
            dve.wait_ge(c_ready, 1)
            nc.vector.tensor_scalar(fx[:], fc[:], -1.0, None, ALU.mult).then_inc(c_ready, 1)
            for n in range(8 + 4 + 14):
                m.stream.done(dve, "fox_qk", n)
                m.stream.low(dve, "fox_qk", n)
            dve.wait_ge(c_turned, TT)
            nc.vector.tensor_copy(cq[:], m.ps[:, 7, 0:TT * HEADS].rearrange("p (t h) -> p t h", h=HEADS)
                                  ).then_inc(c_read, 1)


def fox_attention(nc, m, fq, fk, fv, negc, cq, yf):
    (qk_staged, v_staged, scored, biased, masked, maxed, exped, mixed, turned, turned_out, unit_done, o_out,
     mask_made, chain_s) = (m.sem("fa_" + n) for n in (
         "qk_staged", "v_staged", "scored", "biased", "masked", "maxed", "exped", "mixed", "turned", "turned_out",
         "unit_done", "o_out", "mask_made", "chain"))
    tiles, per = 2, 2 * 2 * TT
    units = [(j, c, qt) for j in range(tiles) for c in range(2) for qt in range(TT)]
    with nc.Block() as block, ExitStack() as mem:
        sb = lambda n, s: mem.enter_context(nc.sbuf_tensor("fa_" + n, s, F32))
        causal = sb("causal", [P, P])
        q_st, k_st, v_st = sb("q_st", [P, 2, T]), sb("k_st", [P, 2, T]), sb("v_st", [P, 2, TT, P])
        s, e, a = sb("s", [P, 2, T]), sb("e", [P, 2, T]), sb("a", [P, 2, T])
        neg_max, z = sb("neg_max", [P, 2]), sb("z", [P, 2])
        aT = sb("aT", [P, 2, TT, P])

        @block.gpsimd
        def _(pool):
            nc.gpsimd.memset(causal[:], 0.0).then_inc(mask_made, 1)
            pool.wait_ge(mask_made, 1)
            nc.gpsimd.affine_select(out=causal[:], in_=causal[:], compare_op=ALU.is_ge, fill=NEG, base=0,
                                    pattern=[[-1, P]], channel_multiplier=1).then_inc(mask_made, 1)
            with pool.Fori(0, 2) as it:
                for j in range(tiles):
                    pool.wait_ge(unit_done, it * per + 8 * (j + 1))
                    for staged, whole in ((q_st, fq), (k_st, fk)):
                        nc.gpsimd.tensor_copy(staged[:, j, :], whole[:, bass.ds(it * 2 + j, 1), :].rearrange(
                            "p a t -> p (a t)")).then_inc(qk_staged, 1)
                    nc.gpsimd.tensor_copy(v_st[:, j, :, :], fv[:, :, bass.ds((it * 2 + j) * P, P)]
                                          ).then_inc(v_staged, 1)

        @block.tensor
        def _(pe):
            pe.sem_inc(unit_done, per)
            pe.sem_inc(biased, 2)
            pe.sem_inc(turned_out, 2)
            pe.sem_inc(o_out, 2)

            def values(it, u):
                j, c, qt = units[u]
                b = u % 2
                pe.wait_ge(mixed, it * per + (u + 1))
                pe.wait_ge(turned_out, it * per + (u + 1))
                for kt in range(qt + 1):
                    last = nc.tensor.transpose(m.ps[:, 3 * b + 1, kt * P:(kt + 1) * P],
                                               a[:, b, kt * P:(kt + 1) * P], m.ident[:])
                last.then_inc(turned, 1)
                if (c, qt) == (0, 0):
                    pe.wait_ge(v_staged, it * 2 + (j + 1))
                pe.wait_ge(turned_out, it * per + (u + 3))
                pe.wait_ge(o_out, it * per + (u + 1))
                for kt in range(qt + 1):
                    last = nc.tensor.matmul(m.ps[c * DH:(c + 1) * DH, 3 * b + 2, 0:P],
                                            v_st[:, j, kt, c * DH:(c + 1) * DH], aT[:, b, kt, :],
                                            start=kt == 0, stop=kt == qt)
                last.then_inc(unit_done, 1)

            with pe.Fori(0, 2) as it:
                for u, (j, c, qt) in enumerate(units):
                    if (c, qt) == (0, 0):
                        pe.wait_ge(qk_staged, it * 4 + 2 * (j + 1))
                    pe.wait_ge(biased, it * per + (u + 1))
                    rows = slice(c * DH, (c + 1) * DH)
                    nc.tensor.matmul(m.ps[:, 3 * (u % 2), 0:(qt + 1) * P], q_st[rows, j, qt * P:(qt + 1) * P],
                                     k_st[rows, j, 0:(qt + 1) * P], start=True, stop=True).then_inc(scored, 1)
                    if u >= 1:
                        values(it, u - 1)
                values(it, per - 1)

        @block.scalar
        def _(act):
            def outputs(it, u):
                j, c, qt = units[u]
                b, n = u % 2, (qt + 1) * P
                act.wait_ge(turned, it * per + (u + 1))
                nc.scalar.copy(aT[:, b, 0:qt + 1, :], m.ps[:, 3 * b + 1, 0:n].rearrange("p (k q) -> p k q", q=P)
                               ).then_inc(turned_out, 1)
                act.wait_ge(unit_done, it * per + (per + u + 1))
                nc.scalar.copy(yf[c * DH:(c + 1) * DH, bass.ds(it * 2 + j, 1), qt * P:(qt + 1) * P],
                               m.ps[c * DH:(c + 1) * DH, 3 * b + 2, 0:P].rearrange("p (a q) -> p a q", a=1)
                               ).then_inc(o_out, 1)

            with act.Fori(0, 2) as it:
                for u, (j, c, qt) in enumerate(units):
                    b, n = u % 2, (qt + 1) * P
                    act.wait_ge(maxed, it * per + (u + 1))
                    nc.scalar.activation(e[:, b, 0:n], s[:, b, 0:n], ACT.Exp, bias=neg_max[:, b:b + 1],
                                         accum_out=z[:, b:b + 1]).then_inc(exped, 1)
                    if u >= 1:
                        outputs(it, u - 1)
                outputs(it, per - 1)

        @block.vector
        def _(dve):
            dve.wait_ge(mask_made, 2)
            link = Chain(dve, chain_s)
            with link.loop(2, 2 * per) as it:
                for u, (j, c, qt) in enumerate(units):
                    b, n = u % 2, (qt + 1) * P
                    h = it * 4 + (2 * j + c)
                    dve.wait_ge(scored, it * per + (u + 1))
                    nc.vector.scalar_tensor_tensor(out=s[:, b, 0:n],
                                                   in0=negc[:, bass.ds(h, 1), 0:n].rearrange("p a t -> p (a t)"),
                                                   scalar=cq[:, qt, bass.ds(h, 1)], in1=m.ps[:, 3 * b, 0:n],
                                                   op0=ALU.add, op1=ALU.add).then_inc(biased, 1)
                    dve.wait_ge(biased, it * per + (u + 3))
                    link(nc.vector.tensor_tensor(s[:, b, n - P:n], s[:, b, n - P:n], causal[:], ALU.add))
                    nc.vector.tensor_reduce(neg_max[:, b:b + 1], s[:, b, 0:n], AX.X, ALU.max, negate=True
                                            ).then_inc(maxed, 1)
                    dve.wait_ge(exped, it * per + (u + 1))
                    link(nc.vector.reciprocal(z[:, b:b + 1], z[:, b:b + 1]))
                    dve.wait_ge(turned_out, it * per + (u + 1))
                    nc.vector.tensor_scalar(a[:, b, 0:n], e[:, b, 0:n], z[:, b:b + 1], None, ALU.mult
                                            ).then_inc(mixed, 1)
                    dve.wait_ge(mixed, it * per + (u + 1))


def time_mix_inputs(nc, m, cols, w):
    (loaded, acts, made, l_done, l_free, g_read, sum_done, rooted, centred, exps) = (m.sem("ti_" + n) for n in (
        "loaded", "acts", "made", "l_done", "l_free", "g_read", "sum_done", "rooted", "centred", "exps"))
    F = 4
    with nc.Block() as block, ExitStack() as mem:
        sb = lambda n, s: mem.enter_context(nc.sbuf_tensor("ti_" + n, s, F32))
        w2a2, g2 = sb("w2a2", [P, F * P]), sb("g2", [P, F * P])
        rw = cols[:, :, 1:T + 1]
        diff = sb("diff", [P, T])
        ta, tg = sb("ta", [P, T]), sb("tg", [P, T])
        lw, L, a, t1 = (sb(n, [P, F, T]) for n in ("lw", "L", "a", "t1"))
        ep, en, ex = a, t1, lw
        reset = sb("reset", [P, T])
        mid, omka = sb("mid", [P, F, NCHUNK]), sb("omka", [P, F])

        @block.sync
        def _(sp):
            sp.dma_start(w2a2[:], m.i["w2a2"]).then_inc(loaded, 16)
            sp.dma_start(g2[:], m.i["g2"]).then_inc(loaded, 16)

        @block.scalar
        def _(act):
            act.wait_ge(made, 4)
            nc.scalar.activation(ta[0:DH, :], rw[0:DH, 12, :], ACT.Tanh).then_inc(acts, 1)
            nc.scalar.copy(ta[DH:P, :], rw[DH:P, 12, :]).then_inc(acts, 1)
            nc.scalar.activation(tg[:], rw[:, 13, :], ACT.Sigmoid).then_inc(acts, 1)
            for f in range(F):
                act.wait_ge(l_done, f + 1)
                nc.scalar.activation(lw[:, f, :], m.ps[:, f, :], ACT.Sigmoid, bias=m.v("w0")[:, f:f + 1]
                                     ).then_inc(l_free, 1)
            for f in range(F):
                act.wait_ge(l_done, F + f + 1)
                nc.scalar.activation(a[:, f, :], m.ps[:, 4 + f, :], ACT.Sigmoid, bias=m.v("a0")[:, f:f + 1]
                                     ).then_inc(l_free, 1)
            for f in range(F):
                act.wait_ge(l_done, 2 * F + f + 1)
                nc.scalar.copy(w.g[:, f, :], m.ps[:, f, :]).then_inc(g_read, 1)
            act.wait_ge(rooted, 1)
            nc.scalar.activation(t1[:], t1[:], ACT.Sqrt).then_inc(rooted, 1)
            act.wait_ge(centred, 1)
            nc.scalar.activation(ep[:], L[:], ACT.Exp).then_inc(exps, 1)
            act.wait_ge(sum_done, 4)
            nc.scalar.activation(en[:], L[:], ACT.Exp, scale=-1.0).then_inc(exps, 1)
            act.wait_ge(centred, 3)
            nc.scalar.activation(ex[:], lw[:], ACT.Exp).then_inc(exps, 1)
            nc.scalar.activation(w.carry[:], w.carry[:], ACT.Exp).then_inc(exps, 1)

        @block.tensor
        def _(pe):
            pe.wait_ge(loaded, 32)
            pe.wait_ge(acts, 3)
            for f in range(F):
                nc.tensor.matmul(m.ps[:, f, :], w2a2[0:DH, f * P:(f + 1) * P], ta[0:DH, :], start=True, stop=True
                                 ).then_inc(l_done, 1)
            for f in range(F):
                nc.tensor.matmul(m.ps[:, 4 + f, :], w2a2[DH:P, f * P:(f + 1) * P], ta[DH:P, :], start=True, stop=True
                                 ).then_inc(l_done, 1)
            for f in range(F):
                pe.wait_ge(l_free, f + 1)
                nc.tensor.matmul(m.ps[:, f, :], g2[:, f * P:(f + 1) * P], tg[:], start=True, stop=True
                                 ).then_inc(l_done, 1)
            pe.wait_ge(l_free, 2 * F)
            pe.wait_ge(sum_done, 1)
            for f in range(F):
                last = nc.tensor.matmul(m.ps[:, 4 + f, :], m.halves[:], t1[:, f, :], start=True, stop=True)
            last.then_inc(sum_done, 1)
            pe.wait_ge(g_read, F)
            pe.wait_ge(sum_done, 3)
            for f in range(F):
                last = nc.tensor.matmul(m.ps[:, f, :], m.halves[:], t1[:, f, :], start=True, stop=True)
            last.then_inc(sum_done, 1)

        @block.vector
        def _(dve):
            link = Chain(dve, made)

            def per_tile(out, in0, name, in1=None, op0=ALU.mult, op1=ALU.mult):
                for f in range(F):
                    if in1 is None:
                        link(nc.vector.tensor_scalar(out[:, f, :], in0[:, f, :], m.v(name)[:, f:f + 1], None, op0))
                    else:
                        link(nc.vector.scalar_tensor_tensor(out=out[:, f, :], in0=in0[:, f, :],
                                                            scalar=m.v(name)[:, f:f + 1], in1=in1[:, f, :],
                                                            op0=op0, op1=op1))
            for n in [12, 13] + list(range(12)):
                link(nc.vector.tensor_tensor(diff[:], cols[:, n, 0:T], rw[:, n, :], ALU.subtract))
                link(nc.vector.scalar_tensor_tensor(out=rw[:, n, :], in0=diff[:], scalar=m.v("mu")[:, n:n + 1],
                                                    in1=rw[:, n, :], op0=ALU.mult, op1=ALU.add))
            k = rw[:, 4:8, :]
            per_tile(w.kk, k, "k_k")
            nc.vector.tensor_tensor(t1[:], w.kk[:], w.kk[:], ALU.mult).then_inc(sum_done, 1)
            dve.wait_ge(sum_done, 2)
            nc.vector.tensor_scalar(t1[:], m.ps[:, 4:8, :], 1e-30, None, ALU.max).then_inc(rooted, 1)
            dve.wait_ge(rooted, 2)
            link(nc.vector.tensor_scalar(t1[:], t1[:], 1e-12, None, ALU.max))
            link(nc.vector.reciprocal(t1[:], t1[:]))
            link(nc.vector.tensor_tensor(w.kk[:], w.kk[:], t1[:], ALU.mult))
            dve.wait_ge(l_free, 2 * F)
            link(nc.vector.tensor_tensor(w.b[:], w.kk[:], a[:], ALU.mult))
            link(nc.vector.tensor_scalar(omka[:], m.v("k_a"), -1.0, 1.0, ALU.mult, ALU.add))
            for f in range(F):
                link(nc.vector.tensor_scalar(t1[:, f, :], a[:, f, :], m.v("k_a")[:, f:f + 1], omka[:, f:f + 1],
                                             ALU.mult, ALU.add))
            link(nc.vector.tensor_tensor(w.k[:], t1[:], k, ALU.mult))
            for f in range(F):
                ins = nc.vector.scalar_tensor_tensor(out=t1[:, f, :], in0=w.r[:, f, :], scalar=m.v("r_k")[:, f:f + 1],
                                                     in1=w.k[:, f, :], op0=ALU.mult, op1=ALU.mult)
                if f < F - 1:
                    link(ins)
            ins.then_inc(sum_done, 1)
            link(nc.vector.tensor_scalar(lw[:], lw[:], -math.exp(-0.5), None, ALU.mult))
            link(nc.vector.memset(reset[:], 1.0))
            link(nc.vector.memset(reset[:].rearrange("p (c t) -> p c t", t=CHUNK)[:, :, 0:1], 0.0))
            for f in range(F):
                link(nc.vector.tensor_tensor_scan(L[:, f, :], reset[:], lw[:, f, :], 0.0, ALU.mult, ALU.add))
            ends = L[:].rearrange("p f (c t) -> p f c t", t=CHUNK)[:, :, :, CHUNK - 1:CHUNK].rearrange(
                "p f c o -> p f (c o)")
            link(nc.vector.tensor_scalar(mid[:], ends, 0.5, None, ALU.mult))
            Lc = L[:].rearrange("p f (c t) -> p (f c) t", t=CHUNK)
            nc.vector.tensor_tensor(Lc, Lc, mid[:].rearrange("p f (c o) -> p (f c) o", o=1).to_broadcast(
                [P, F * NCHUNK, CHUNK]), ALU.subtract).then_inc(centred, 1)
            dve.wait_ge(centred, 1)
            nc.vector.tensor_tensor(lw[:], L[:], lw[:], ALU.subtract).then_inc(centred, 1)
            link(nc.vector.memset(w.carry[:], 0.0))
            nc.vector.tensor_tensor(w.carry[:, :, 0:NCHUNK - 1], mid[:, :, 0:NCHUNK - 1], mid[:, :, 1:NCHUNK],
                                    ALU.add).then_inc(centred, 1)
            dve.wait_ge(sum_done, 4)
            link(nc.vector.tensor_tensor(w.bonus[:], m.ps[:, 0:4, :], w.v[:], ALU.mult))
            dve.wait_ge(exps, 3)
            for x, y in ((w.kk, ex), (w.r, ep), (w.b, en), (w.k, en)):
                link(nc.vector.tensor_tensor(x[:], x[:], y[:], ALU.mult))


def recurrence(nc, m, w, yr):
    names = ("masks", "made", "turned", "tm_read", "p1", "p2", "p1_read", "y_done", "y_read", "tu_done", "inv", "mv",
             "mv_read", "w_done", "w_read", "sa_done", "sa_read", "ds_done", "s_next", "yo_done", "yo_read", "slices", "made2", "w_half")
    s_ = {n: m.sem("rc_" + n) for n in names}
    F, LEVELS = 4, 5
    H2 = 4
    with nc.Block() as block, ExitStack() as mem:
        sb = lambda n, s, dt=F32: mem.enter_context(nc.sbuf_tensor("rc_" + n, s, dt))
        part = sb("part", [P, 4, P])
        low = sb("low", [P, P])
        pair, pairT = sb("pair", [P, P]), sb("pairT", [P, P])
        lev = sb("lev", [P, LEVELS, P])
        KR = sb("KR", [P, F, 2, P])
        B, C = sb("B", [P, F, P]), sb("C", [P, F, P])
        Bt, Ct, Vt = (sb(n, [P, T]) for n in ("Bt", "Ct", "Vt"))
        Vs = sb("Vs", [P, F, P])
        A = sb("A", [P, HEADS, 4, P])
        N = sb("N", [P, HEADS, P])
        Ti, U, Y = (sb(n, [P, HEADS, P]) for n in ("Ti", "U", "Y"))
        MV, W, SA = (sb(n, [P, HEADS, DH]) for n in ("MV", "W", "SA"))
        S = sb("S", [P, 3, F, DH])

        @block.gpsimd
        def _(pool):
            link = Chain(pool, s_["masks"])
            def triangle(out, strict, upper):
                link(nc.gpsimd.tensor_copy(out, m.halves[:]))
                sign = -1 if upper else 1
                link(nc.gpsimd.affine_select(out=out, in_=out, compare_op=ALU.is_ge, fill=0.0,
                                             base=-1 if strict else 0, pattern=[[-sign, P]], channel_multiplier=sign))
            for at, strict in ((0, True), (1, False), (2, True), (3, False)):
                triangle(part[:, at, :], strict, True)
            triangle(low[:], True, False)
            link(nc.gpsimd.memset(lev[:], 1.0))
            for l in range(LEVELS):
                size = 2 << l
                v = lev[:, l, :].rearrange("p (b h c) -> p b h c", h=2, c=size)
                link(nc.gpsimd.memset(v[:, :, 0, :], 0.0))
                link(nc.gpsimd.affine_select(out=v[:, :, 1, :], in_=v[:, :, 1, :], compare_op=ALU.is_ge, fill=0.0,
                                             base=0, pattern=[[-2 * size, P // (2 * size)], [0, size]],
                                             channel_multiplier=1))
                link(nc.gpsimd.affine_select(out=v[:, :, 1, :], in_=v[:, :, 1, :], compare_op=ALU.is_ge, fill=0.0,
                                             base=size - 1, pattern=[[2 * size, P // (2 * size)], [0, size]],
                                             channel_multiplier=-1))
            link(nc.gpsimd.memset(pair[:], 0.0))
            v = pair[:].rearrange("p (b h) -> p b h", h=2)
            link(nc.gpsimd.affine_select(out=v[:, :, 1:2], in_=v[:, :, 1:2], compare_op=ALU.not_equal, fill=1.0,
                                         base=0, pattern=[[-2, P // 2], [0, 1]], channel_multiplier=1))
            link(nc.gpsimd.memset(pairT[:], 0.0))
            v = pairT[:].rearrange("p (b h) -> p b h", h=2)
            link(nc.gpsimd.affine_select(out=v[:, :, 0:1], in_=v[:, :, 0:1], compare_op=ALU.not_equal, fill=1.0,
                                         base=-1, pattern=[[-2, P // 2], [0, 1]], channel_multiplier=1))

        masks_value = 2 * 5 + 1 + 3 * LEVELS + 4

        def heads_of(h):
            return slice(DH * (h % 2), DH * (h % 2) + DH), h // 2

        @block.tensor
        def _(pe):
            pe.sem_inc(s_["yo_read"], 1)
            with pe.Fori(0, TT) as it:
                pe.wait_ge(s_["yo_read"], it + 1)
                pe.wait_ge(s_["slices"], it * 5 + 5)
                for n, src in enumerate((B, C, Vs)):
                    for f in range(F):
                        last = nc.tensor.transpose(m.ps[:, n, f * P:(f + 1) * P], src[:, f, :], m.ident[:])
                    last.then_inc(s_["turned"], 1)
                for h in range(HEADS):
                    rows, f = heads_of(h)
                    if h >= 2:
                        pe.wait_ge(s_["p1_read"], it * 16 + 2 * (h - 1))
                    elif h == 0:
                        pe.wait_ge(s_["yo_read"], it + 1)
                    nc.tensor.matmul(m.ps[:, 4 + h % 2, 0:2 * P], B[rows, f, :], KR[rows, f, :, :].rearrange("p a t -> p (a t)"),
                                     start=True, stop=True)
                    nc.tensor.matmul(m.ps[:, 4 + h % 2, 2 * P:4 * P], C[rows, f, :], KR[rows, f, :, :].rearrange("p a t -> p (a t)"),
                                     start=True, stop=True).then_inc(s_["p1"], 1)
                    nc.tensor.matmul(m.ps[:, 6 + h % 2, 0:P], KR[rows, f, 0, :], B[rows, f, :],
                                     start=True, stop=True).then_inc(s_["p2"], 1)
                pe.wait_ge(s_["tm_read"], it * 3 + 3)
                pe.wait_ge(s_["p1_read"], it * 16 + 16)
                for h in range(HEADS):
                    last = nc.tensor.matmul(m.ps[:, 3, h * DH:(h + 1) * DH], A[:, h, 2, :], Vt[:, h * DH:(h + 1) * DH],
                                            start=True, stop=True)
                last.then_inc(s_["mv"], 1)
                for l in range(LEVELS):
                    for g in range(2):
                        pe.wait_ge(s_["inv"], it * (2 * LEVELS + 2) + (2 * l + g + 1))
                        for h in range(g * H2, g * H2 + H2):
                            last = nc.tensor.matmul(m.ps[:, g, (h % H2) * P:(h % H2 + 1) * P], N[:, h, :], U[:, h, :],
                                                    start=True, stop=True)
                        last.then_inc(s_["y_done"], 1)
                    for g in range(2):
                        pe.wait_ge(s_["y_read"], it * (2 * LEVELS) + (2 * l + g + 1))
                        for h in range(g * H2, g * H2 + H2):
                            at = slice((h % H2) * P, (h % H2 + 1) * P)
                            nc.tensor.matmul(m.ps[:, 4 + g, at], Y[:, h, :], Ti[:, h, :], start=True, stop=True)
                            last = nc.tensor.matmul(m.ps[:, 6 + g, at], Ti[:, h, :], Y[:, h, :], start=True, stop=True)
                        last.then_inc(s_["tu_done"], 1)
                pe.wait_ge(s_["inv"], it * (2 * LEVELS + 2) + (2 * LEVELS + 2))
                pe.wait_ge(s_["mv_read"], it + 1)
                for c in range(2):
                    toks = slice(DH * c, DH * c + DH)
                    settle(m, pe, s_["s_next"], it * 3 + (c + 1))
                    for par in range(2):
                        for h in range(par, HEADS, 2):
                            rows, f = heads_of(h)
                            last = nc.tensor.matmul(m.ps[toks, par, f * DH:(f + 1) * DH], KR[rows, f, 0, toks],
                                                    S[rows, c, f, :], start=True, stop=True)
                    last.then_inc(s_["w_done"], 1)
                    settle(m, pe, s_["w_read"], it * 2 + (c + 1))
                    for h in range(HEADS):
                        last = nc.tensor.matmul(m.ps[toks, 2, h * DH:(h + 1) * DH], U[toks, h, toks], W[toks, h, :],
                                                start=True, stop=True)
                    last.then_inc(s_["sa_done"], 1)
                    settle(m, pe, s_["sa_read"], it * 2 + (c + 1))
                    for h in range(HEADS):
                        rows, f = heads_of(h)
                        out = m.ps[rows, 3, f * DH:(f + 1) * DH]
                        nc.tensor.matmul(out, Ct[toks, h * DH:(h + 1) * DH], Vt[toks, h * DH:(h + 1) * DH],
                                         start=True, stop=False)
                        last = nc.tensor.matmul(out, Bt[toks, h * DH:(h + 1) * DH], SA[toks, h, :],
                                                start=False, stop=True)
                    last.then_inc(s_["ds_done"], 1)
                for h in range(HEADS):
                    rows, f = heads_of(h)
                    out = m.ps[rows, 4, f * P:(f + 1) * P]
                    nc.tensor.matmul(out, SA[:, h, :], A[:, h, 1, :], start=True, stop=False)
                    for c in range(2):
                        toks = slice(DH * c, DH * c + DH)
                        nc.tensor.matmul(m.ps[rows, 4, f * P + DH * c:f * P + DH * c + DH], S[rows, c, f, :],
                                         KR[rows, f, 1, toks], start=False, stop=False, skip_group_check=True)
                    last = nc.tensor.matmul(out, Vt[:, h * DH:(h + 1) * DH], A[:, h, 3, :], start=False, stop=True)
                last.then_inc(s_["yo_done"], 1)

        @block.scalar
        def _(act):
            with act.Fori(0, TT) as it:
                for n, dst in enumerate((Bt, Ct, Vt)):
                    act.wait_ge(s_["turned"], it * 3 + n + 1)
                    nc.scalar.copy(dst[:], m.ps[:, n, :]).then_inc(s_["tm_read"], 1)
                act.wait_ge(s_["mv"], it + 1)
                nc.scalar.copy(MV[:].rearrange("p h d -> p (h d)"), m.ps[:, 3, :]).then_inc(s_["mv_read"], 1)
                for c in range(2):
                    toks = slice(DH * c, DH * c + DH)
                    act.wait_ge(s_["sa_done"], it * 2 + (c + 1))
                    nc.scalar.mul(SA[toks, :, :].rearrange("p h d -> p (h d)"), m.ps[toks, 2, :], -1.0
                                  ).then_inc(s_["sa_read"], 1)
                act.wait_ge(s_["yo_done"], it + 1)
                nc.scalar.copy(yr[:, :, bass.ds(it * P, P)], m.ps[:, 4, :].rearrange("p (f t) -> p f t", f=F)
                               ).then_inc(s_["yo_read"], 1)

        @block.vector
        def _(dve):
            dve.wait_ge(s_["masks"], masks_value)
            link = Chain(dve, s_["made"])
            link(nc.vector.memset(S[:], 0.0))
            with link.loop(TT, 6) as it:
                toks = bass.ds(it * P, P)
                dve.wait_ge(s_["yo_read"], it + 1)
                for out, x in ((KR[:, :, 0, :], w.kk), (KR[:, :, 1, :], w.r), (B[:], w.b), (C[:], w.k), (Vs[:], w.v)):
                    nc.vector.tensor_copy(out, x[:, :, toks]).then_inc(s_["slices"], 1)
                nc.vector.tensor_copy(S[:, 0, :, :], S[:, 2, :, :]).then_inc(s_["s_next"], 1)
                for h in range(HEADS):
                    dve.wait_ge(s_["p1"], it * 8 + h + 1)
                    nc.vector.tensor_tensor(A[:, h, :, :].rearrange("p a t -> p (a t)"), m.ps[:, 4 + h % 2, :],
                                            part[:].rearrange("p a t -> p (a t)"), ALU.mult).then_inc(s_["p1_read"], 1)
                    dve.wait_ge(s_["p2"], it * 8 + h + 1)
                    nc.vector.tensor_tensor(N[:, h, :], m.ps[:, 6 + h % 2, 0:P], low[:], ALU.mult
                                            ).then_inc(s_["p1_read"], 1)
                dve.wait_ge(s_["p1_read"], it * 16 + 16)
                hb = lambda t: t.unsqueeze(1).to_broadcast([P, HEADS, P])
                link(nc.vector.tensor_tensor(U[:], A[:, :, 0, :], hb(pair[:]), ALU.mult))
                link(nc.vector.tensor_tensor(Ti[:], N[:], hb(pairT[:]), ALU.mult))
                for g in range(2):
                    hs = slice(g * H2, g * H2 + H2)
                    ib = m.ident[:].unsqueeze(1).to_broadcast([P, H2, P])
                    link(nc.vector.tensor_tensor(Ti[:, hs, :], ib, Ti[:, hs, :], ALU.subtract))
                    nc.vector.tensor_tensor(U[:, hs, :], ib, U[:, hs, :], ALU.subtract).then_inc(s_["inv"], 1)
                for l in range(LEVELS):
                    for g in range(2):
                        hs = slice(g * H2, g * H2 + H2)
                        dve.wait_ge(s_["y_done"], it * (2 * LEVELS) + (2 * l + g + 1))
                        nc.vector.tensor_tensor(Y[:, hs, :], m.ps[:, g, :].rearrange("p (h t) -> p h t", h=H2),
                                                lev[:, l, :].unsqueeze(1).to_broadcast([P, H2, P]), ALU.mult
                                                ).then_inc(s_["y_read"], 1)
                    for g in range(2):
                        hs = slice(g * H2, g * H2 + H2)
                        dve.wait_ge(s_["tu_done"], it * (2 * LEVELS) + (2 * l + g + 1))
                        dve.wait_ge(s_["inv"], it * (2 * LEVELS + 2) + (2 * l + g + 1))
                        nc.vector.tensor_tensor(Ti[:, hs, :], Ti[:, hs, :],
                                                m.ps[:, 4 + g, :].rearrange("p (h t) -> p h t", h=H2), ALU.subtract
                                                ).then_inc(s_["made2"], 1)
                        dve.wait_ge(s_["made2"], it * (2 * LEVELS) + (2 * l + g + 1))
                        nc.vector.tensor_tensor(U[:, hs, :], U[:, hs, :],
                                                m.ps[:, 6 + g, :].rearrange("p (h t) -> p h t", h=H2), ALU.subtract
                                                ).then_inc(s_["inv"], 1)
                dve.wait_ge(s_["mv_read"], it + 1)
                for c in range(2):
                    tk = slice(DH * c, DH * c + DH)
                    dve.wait_ge(s_["w_done"], it * 2 + (c + 1))
                    Wv, Mv = (x[tk, :, :].rearrange("p (f a) d -> p a f d", a=2) for x in (W, MV))
                    nc.vector.tensor_tensor(Wv[:, 0, :, :], m.ps[tk, 0, 0:F * DH].rearrange("p (f d) -> p f d", f=F),
                                            Mv[:, 0, :, :], ALU.add).then_inc(s_["w_half"], 1)
                    dve.wait_ge(s_["w_half"], it * 2 + (c + 1))
                    nc.vector.tensor_tensor(Wv[:, 1, :, :], m.ps[tk, 1, 0:F * DH].rearrange("p (f d) -> p f d", f=F),
                                            Mv[:, 1, :, :], ALU.add).then_inc(s_["w_read"], 1)
                    dve.wait_ge(s_["ds_done"], it * 2 + (c + 1))
                    nxt = S[:, c + 1, :, :]
                    link(nc.vector.tensor_tensor(nxt, S[:, c, :, :], m.ps[:, 3, 0:F * DH].rearrange(
                        "p (f d) -> p f d", f=F), ALU.add))
                    carry = w.carry[:, :, bass.ds(it * 2 + c, 1)].to_broadcast([P, F, DH])
                    nc.vector.tensor_tensor(nxt, nxt, carry, ALU.mult).then_inc(s_["s_next"], 1)
                    dve.wait_ge(s_["s_next"], it * 3 + (c + 2))


def time_mix_output(nc, m, w, yr):
    summed, squared, rooted, chain_s = (m.sem("to_" + n) for n in ("summed", "squared", "rooted", "chain"))
    F = 4
    with nc.Block() as block, ExitStack() as mem:
        t = mem.enter_context(nc.sbuf_tensor("to_t", [P, F, T], F32))

        @block.tensor
        def _(pe):
            for f in range(F):
                last = nc.tensor.matmul(m.ps[:, f, :], m.halves[:], yr[:, f, :], start=True, stop=True)
            last.then_inc(summed, 1)
            pe.wait_ge(squared, 1)
            for f in range(F):
                last = nc.tensor.matmul(m.ps[:, 4 + f, :], m.halves[:], t[:, f, :], start=True, stop=True)
            last.then_inc(summed, 1)

        @block.scalar
        def _(act):
            act.wait_ge(chain_s, 1)
            nc.scalar.activation(t[:], yr[:], ACT.Square).then_inc(squared, 1)
            act.wait_ge(chain_s, 2)
            nc.scalar.activation(t[:], t[:], ACT.Sqrt).then_inc(rooted, 1)

        @block.vector
        def _(dve):
            link = Chain(dve, chain_s)
            dve.wait_ge(summed, 1)
            link(nc.vector.scalar_tensor_tensor(out=yr[:], in0=m.ps[:, 0:4, :], scalar=-1.0 / DH, in1=yr[:],
                                                op0=ALU.mult, op1=ALU.add))
            dve.wait_ge(summed, 2)
            link(nc.vector.tensor_scalar(t[:], m.ps[:, 4:8, :], 1.0 / DH, GN_EPS, ALU.mult, ALU.add))
            dve.wait_ge(rooted, 1)
            link(nc.vector.reciprocal(t[:], t[:]))
            link(nc.vector.tensor_tensor(yr[:], yr[:], t[:], ALU.mult))
            for f in range(F):
                link(nc.vector.tensor_scalar(yr[:, f, :], yr[:, f, :], m.v("ln_g")[:, f:f + 1], m.v("ln_b")[:, f:f + 1],
                                             ALU.mult, ALU.add))
            link(nc.vector.tensor_tensor(yr[:], yr[:], w.bonus[:], ALU.add))
            link(nc.vector.tensor_tensor(yr[:], yr[:], w.g[:], ALU.mult))


def merge(nc, m, yf, yr, x_parts, yf_parts, yr_parts, merged):
    gates_read, both, added, highs, lows, m_high, m_low = (m.sem("me_" + n) for n in (
        "gates_read", "both", "added", "highs", "lows", "m_high", "m_low"))
    with nc.Block() as block, ExitStack() as mem:
        sg = mem.enter_context(nc.sbuf_tensor("me_sg", [P, 4, T], F32))
        t = mem.enter_context(nc.sbuf_tensor("me_t", [P, 2, T], F32))
        whole = [(m.xT, x_parts, k) for k in range(KT)] + [(y, y_parts, k) for y, y_parts in (
            (yf, yf_parts), (yr, yr_parts)) for k in range(4)]

        @block.sync
        def _(sp):
            m.stream.loads(sp, "merge")

        @block.tensor
        def _(pe):
            pe.sem_inc(gates_read, 4)
            pe.sem_inc(both, 4)
            pe.wait_ge(lows, KT)
            with pe.Fori(0, 2) as it:
                for g in range(2):
                    for k in range(6):
                        x, kt = [x_parts, x_parts, x_parts, x_parts, yf_parts, yr_parts][k], KT if k < 4 else 4
                        w = [v.rearrange("p (k f) -> p k f", k=kt) for v in m.stream.weights(pe, "merge", 6 * g + k, it)]
                        if k == 4:
                            pe.wait_ge(lows, KT + 8)
                        for half in range(1 if k < 4 else 2):
                            n = k if k < 4 else 2 * k - 4 + half
                            pe.wait_ge(gates_read if n < 4 else both, it * 8 + (4 * g + n % 4 + 1))
                            for c in range(kt):
                                last = times(nc, m.ps[:, n, :], [v[:, c, half * P:(half + 1) * P] for v in w],
                                             [v[:, c, :] for v in x], start=c == 0, stop=c == kt - 1)
                        last.then_inc(m.chunk_done, 1)

        @block.scalar
        def _(act):
            for x, parts, k in whole:
                nc.scalar.copy(parts[0][:, k, :], x[:, k, :]).then_inc(highs, 1)
            act.sem_inc(added, 1)
            with act.Fori(0, 2) as it:
                for g in range(2):
                    act.wait_ge(added, it * 2 + (g + 1))
                    for k in range(4):
                        m.stream.done(act, "merge", 6 * g + k, it)
                        nc.scalar.activation(sg[:, k, :], m.ps[:, k, :], ACT.Sigmoid).then_inc(gates_read, 1)
                        m.stream.high(act, "merge", 6 * g + k, it)
                    for k in range(4, 6):
                        m.stream.done(act, "merge", 6 * g + k, it)
                        m.stream.high(act, "merge", 6 * g + k, it)
                    act.wait_ge(added, it * 2 + (g + 2))
                    nc.scalar.copy(merged[0][:, bass.ds(it * 4 + 2 * g, 2), :], t[:]).then_inc(m_high, 1)

        @block.vector
        def _(dve):
            for n, (x, parts, k) in enumerate(whole):
                dve.wait_ge(highs, n + 1)
                nc.vector.tensor_tensor(parts[1][:, k, :], x[:, k, :], parts[0][:, k, :].bitcast(F32), ALU.subtract
                                        ).then_inc(lows, 1)
            with dve.Fori(0, 2) as it:
                for g in range(2):
                    for k in range(4):
                        m.stream.done(dve, "merge", 6 * g + k, it)
                        m.stream.low(dve, "merge", 6 * g + k, it)
                    dve.wait_ge(gates_read, it * 8 + (4 * g + 8))
                    for k in range(4, 6):
                        m.stream.done(dve, "merge", 6 * g + k, it)
                        for half in range(2):
                            n = 2 * k - 4 + half
                            out = t[:, half, :] if k == 4 else sg[:, 2 + half, :]
                            nc.vector.tensor_tensor(out, sg[:, n - 4, :], m.ps[:, n, :], ALU.mult).then_inc(both, 1)
                        m.stream.low(dve, "merge", 6 * g + k, it)
                    dve.wait_ge(both, it * 8 + (4 * g + 8))
                    nc.vector.tensor_tensor(t[:], t[:], sg[:, 2:4, :], ALU.add).then_inc(added, 1)
                    dve.wait_ge(m_high, it * 2 + (g + 1))
                    dve.wait_ge(added, it * 2 + (g + 2))
                    tiles = bass.ds(it * 4 + 2 * g, 2)
                    nc.vector.tensor_tensor(merged[1][:, tiles, :], t[:], merged[0][:, tiles, :].bitcast(F32),
                                            ALU.subtract).then_inc(m_low, 1)
                    dve.wait_ge(m_low, it * 2 + (g + 1))


def output_and_norm(nc, m, high, low):
    bank_free, summed, squared, rooted, chain_s = (m.sem("on_" + n) for n in (
        "bank_free", "summed", "squared", "rooted", "chain"))
    with nc.Block() as block, ExitStack() as mem:
        sb = lambda n, s: mem.enter_context(nc.sbuf_tensor("on_" + n, s, F32))
        sq, mean, rstd = sb("sq", [P, KT, T]), sb("mean", [P, T]), sb("rstd", [P, T])

        @block.sync
        def _(sp):
            m.stream.loads(sp, "w_o")

        @block.tensor
        def _(pe):
            project(nc, m, pe, "w_o", high, low, bank_free)
            pe.wait_ge(bank_free, 8 + 1)
            for k in range(KT):
                pe.wait_ge(bank_free, 8 + k + 1)
                last = nc.tensor.matmul(m.ps[:, 0, :], m.ones[:], m.xT[:, k, :], start=k == 0, stop=k == KT - 1)
            last.then_inc(summed, 1)
            for k in range(KT):
                pe.wait_ge(squared, k + 1)
                last = nc.tensor.matmul(m.ps[:, 1, :], m.ones[:], sq[:, k, :], start=k == 0, stop=k == KT - 1)
            last.then_inc(summed, 1)

        @block.scalar
        def _(act):
            for n in range(KT):
                m.stream.done(act, "w_o", n)
                m.stream.high(act, "w_o", n)
            for k in range(KT):
                act.wait_ge(chain_s, k + 2)
                nc.scalar.activation(sq[:, k, :], m.xT[:, k, :], ACT.Square).then_inc(squared, 1)
            act.wait_ge(chain_s, KT + 2)
            nc.scalar.activation(rstd[:], rstd[:], ACT.Sqrt).then_inc(rooted, 1)

        @block.vector
        def _(dve):
            for n in range(KT):
                m.stream.done(dve, "w_o", n)
                nc.vector.scalar_tensor_tensor(out=m.xT[:, n, :], in0=m.xT[:, n, :], scalar=ALPHA, in1=m.ps[:, n, :],
                                               op0=ALU.mult, op1=ALU.add).then_inc(bank_free, 1)
                m.stream.low(dve, "w_o", n)
            link = Chain(dve, chain_s)
            dve.wait_ge(summed, 1)
            link(nc.vector.tensor_scalar(mean[:], m.ps[:, 0, :], 1.0 / D, None, ALU.mult))
            for k in range(KT):
                link(nc.vector.tensor_tensor(m.xT[:, k, :], m.xT[:, k, :], mean[:], ALU.subtract))
            dve.wait_ge(summed, 2)
            link(nc.vector.tensor_scalar(rstd[:], m.ps[:, 1, :], 1.0 / D, LN_EPS, ALU.mult, ALU.add))
            dve.wait_ge(rooted, 1)
            link(nc.vector.reciprocal(rstd[:], rstd[:]))
            for k in range(KT):
                dve.wait_ge(squared, k + 1)
                link(nc.vector.scalar_tensor_tensor(out=m.xT[:, k, :], in0=m.xT[:, k, :], scalar=m.v("ln1_g")[:, k:k + 1],
                                                    in1=rstd[:], op0=ALU.mult, op1=ALU.mult))
                link(nc.vector.tensor_scalar(m.xT[:, k, :], m.xT[:, k, :], m.v("ln1_b")[:, k:k + 1], None, ALU.add))


def key_scores(nc, m, high, low, q, keys, x4, scores):
    bank_free, scored, highs, lows, spilled, keys_loaded = (m.sem("ks_" + n) for n in (
        "bank_free", "scored", "highs", "lows", "spilled", "keys_loaded"))
    HH = 2 * HEADS
    with nc.Block() as block:
        @block.sync
        def _(sp):
            sp.dma_start(keys[:], m.i["keys"].rearrange("p (h k) -> p h k", k=KEYS)).then_inc(keys_loaded, 16)
            sp.dma_start(x4.rearrange("(k p) t -> p k t", p=P), m.xT[:]).then_inc(spilled, 16)
            m.stream.loads(sp, "peer_q")
            sp.wait_ge(spilled, 16)

        @block.tensor
        def _(pe):
            pe.wait_ge(lows, KT)
            project(nc, m, pe, "peer_q", high, low, bank_free, chunks=HH)
            pe.wait_ge(keys_loaded, 16)
            for h in range(HH):
                pe.wait_ge(bank_free, HH + h + 1)
                for tt in range(TT):
                    toks = slice(tt * P, (tt + 1) * P)
                    last = nc.tensor.matmul(m.ps[:, h % 8, toks], q[:, h, toks], keys[:, h, :], start=True, stop=True)
                last.then_inc(scored, 1)

        @block.scalar
        def _(act):
            for k in range(KT):
                nc.scalar.copy(high[:, k, :], m.xT[:, k, :]).then_inc(highs, 1)
            for h in range(HH):
                m.stream.done(act, "peer_q", h)
                nc.scalar.copy(q[:, h, :], m.ps[:, h % 8, :]).then_inc(bank_free, 1)
                m.stream.high(act, "peer_q", h)
            for h in range(HH):
                act.wait_ge(scored, h + 1)
                nc.scalar.copy(scores[:, :, h * KEYS:(h + 1) * KEYS], m.ps[:, h % 8, :].rearrange(
                    "p (t k) -> p t k", t=TT)).then_inc(bank_free, 1)

        @block.vector
        def _(dve):
            for k in range(KT):
                dve.wait_ge(highs, k + 1)
                nc.vector.tensor_tensor(low[:, k, :], m.xT[:, k, :], high[:, k, :].bitcast(F32), ALU.subtract
                                        ).then_inc(lows, 1)
            for h in range(HH):
                m.stream.done(dve, "peer_q", h)
                m.stream.low(dve, "peer_q", h)


def choose(nc, m, scores, iT, jT, gT):
    chain_s, diffed, exped, chosen, turned, read = (m.sem("ch_" + n) for n in (
        "chain", "diffed", "exped", "chosen", "turned", "read"))
    iota_made = m.sem("ch_iota")
    HH, K = 2 * HEADS, TOPK
    with nc.Block() as block, ExitStack() as mem:
        sb = lambda n, s, dt=F32: mem.enter_context(nc.sbuf_tensor("ch_" + n, s, dt))
        sc, rest = sb("sc", [P, HH, KEYS]), sb("rest", [P, HH, KEYS])
        val, idx, idxf = sb("val", [P, HH, K]), sb("idx", [P, HH, K], U32), sb("idxf", [P, HH, K])
        cand, crest = sb("cand", [P, HEADS, K * K]), sb("crest", [P, HEADS, K * K])
        best, pos = sb("best", [P, HEADS, K]), sb("pos", [P, HEADS, K], U32)
        pa, pb = sb("pa", [P, HEADS, K], U32), sb("pb", [P, HEADS, K], U32)
        paf, pbf = sb("paf", [P, HEADS, K]), sb("pbf", [P, HEADS, K])
        eq = sb("eq", [P, HEADS, K, K])
        i_, j_, g_ = sb("i", [P, HEADS, K]), sb("j", [P, HEADS, K]), sb("g", [P, HEADS, K])
        gsum = sb("gsum", [P, HEADS, 1])

        @block.scalar
        def _(act):
            with act.Fori(0, TT) as it:
                act.wait_ge(diffed, it + 1)
                nc.scalar.activation(g_[:], g_[:], ACT.Exp).then_inc(exped, 1)
                act.wait_ge(turned, it + 1)
                for n, dst in enumerate((iT, jT, gT)):
                    nc.scalar.copy(dst[:, bass.ds(it * P, P)], m.ps[:, n, 0:P]).then_inc(read, 1)

        @block.tensor
        def _(pe):
            pe.sem_inc(read, 3)
            with pe.Fori(0, TT) as it:
                pe.wait_ge(read, it * 3 + 3)
                pe.wait_ge(chosen, it + 1)
                for n, src in enumerate((i_, j_, g_)):
                    last = nc.tensor.transpose(m.ps[:, n, 0:P], src[:].rearrange("p h k -> p (h k)"), m.ident[:])
                last.then_inc(turned, 1)

        @block.vector
        def _(dve):
            link = Chain(dve, chain_s)
            with link.fresh_loop(TT) as it:
                link(nc.vector.tensor_copy(sc[:].rearrange("p h k -> p (h k)"),
                                           scores[:, bass.ds(it, 1), :].rearrange("p a n -> p (a n)")))

                def every(n, one):
                    for h in range(n - 1):
                        one(h)
                    link(one(n - 1))

                def top16(n, values, index, x, left):
                    every(n, lambda h: nc.vector.max(values[:, h, 0:8], x[:, h, :]))
                    every(n, lambda h: nc.vector.match_replace(left[:, h, :], values[:, h, 0:8], x[:, h, :], NEG))
                    every(n, lambda h: nc.vector.max(values[:, h, 8:16], left[:, h, :]))
                    every(n, lambda h: nc.vector.max_index(index[:, h, 0:8], values[:, h, 0:8], x[:, h, :]))
                    every(n, lambda h: nc.vector.max_index(index[:, h, 8:16], values[:, h, 8:16], left[:, h, :]))

                top16(HH, val, idx, sc, rest)
                link(nc.vector.tensor_copy(idxf[:], idx[:]))
                v = val[:].rearrange("p (h c) k -> p h c k", c=2)
                link(nc.vector.tensor_tensor(cand[:].rearrange("p h (a b) -> p h a b", b=K),
                                             v[:, :, 0, :].unsqueeze(3).to_broadcast([P, HEADS, K, K]),
                                             v[:, :, 1, :].unsqueeze(2).to_broadcast([P, HEADS, K, K]), ALU.add))
                top16(HEADS, best, pos, cand, crest)
                nc.vector.tensor_tensor(g_[:], best[:], best[:, :, 0:1].to_broadcast([P, HEADS, K]), ALU.subtract
                                        ).then_inc(diffed, 1)
                link(nc.vector.tensor_scalar(pa[:], pos[:], 4, None, ALU.logical_shift_right))
                link(nc.vector.tensor_scalar(pb[:], pos[:], K - 1, None, ALU.bitwise_and))
                link(nc.vector.tensor_copy(paf[:], pa[:]))
                link(nc.vector.tensor_copy(pbf[:], pb[:]))
                ix = idxf[:].rearrange("p (h c) k -> p h c k", c=2)
                iota16 = m.iota[:, 0:K].unsqueeze(1).unsqueeze(1).to_broadcast([P, HEADS, K, K])
                for place, half, out in ((paf, 0, i_), (pbf, 1, j_)):
                    link(nc.vector.tensor_tensor(eq[:], place[:].unsqueeze(3).to_broadcast([P, HEADS, K, K]), iota16,
                                                 ALU.is_equal))
                    link(nc.vector.tensor_tensor(eq[:], eq[:], ix[:, :, half, :].unsqueeze(2).to_broadcast(
                        [P, HEADS, K, K]), ALU.mult))
                    link(nc.vector.tensor_reduce(out[:], eq[:], AX.X, ALU.add))
                dve.wait_ge(exped, it + 1)
                link(nc.vector.tensor_reduce(gsum[:], g_[:], AX.X, ALU.add))
                link(nc.vector.reciprocal(gsum[:], gsum[:]))
                nc.vector.tensor_tensor(g_[:], g_[:], gsum[:].to_broadcast([P, HEADS, K]), ALU.mult
                                        ).then_inc(chosen, 1)
                dve.wait_ge(turned, it + 1)


BLK = 256
PAIR = 4


def gate_matrices(nc, m, blk, G, iT, jT, gT, x4, x, high, low):
    made, done, read, x_loaded, highs = (m.sem(f"gm{blk}_{n}") for n in (
        "made", "done", "read", "x_loaded", "highs"))
    rounds = BLK // (2 * PAIR)
    with nc.Block() as block, ExitStack() as mem:
        A, B = (mem.enter_context(nc.sbuf_tensor(f"gm{blk}_{n}", [P, 2 * PAIR, P], F32)) for n in "AB")

        @block.sync
        def _(sp):
            sp.dma_start(x[:], x4.rearrange("(k p) t -> p k t", p=P)[:, :, blk * BLK:(blk + 1) * BLK]
                         ).then_inc(x_loaded, 16)
            sp.wait_ge(x_loaded, 16)

        @block.tensor
        def _(pe):
            pe.sem_inc(read, 2)
            with pe.Fori(0, rounds) as it:
                for g in range(2):
                    pe.wait_ge(made, it * (2 * (PAIR + 1)) + (PAIR + 1) * (g + 1))
                    pe.wait_ge(read, it * 2 + (g + 1))
                    for n in range(PAIR):
                        last = nc.tensor.matmul(m.ps[:, g, n * P:(n + 1) * P], B[:, g * PAIR + n, :],
                                                A[:, g * PAIR + n, :], start=True, stop=True)
                    last.then_inc(done, 1)

        @block.scalar
        def _(act):
            with act.Fori(0, rounds) as it:
                for g in range(2):
                    act.wait_ge(done, it * 2 + (g + 1))
                    nc.scalar.copy(G[:, bass.ds(it * (2 * PAIR) + PAIR * g, PAIR), :],
                                   m.ps[:, g, :].rearrange("p (t i) -> p t i", i=P)).then_inc(read, 1)
            act.wait_ge(x_loaded, 16)
            nc.scalar.copy(high[:], x[:]).then_inc(highs, 1)

        @block.vector
        def _(dve):
            with dve.Fori(0, rounds) as it:
                for g in range(2):
                    dve.wait_ge(read, it * 2 + (g + 1))
                    at = it * (2 * PAIR) + (blk * BLK + g * PAIR)
                    nc.vector.tensor_tensor(B[:, g * PAIR:(g + 1) * PAIR, :],
                                            m.iota[:].unsqueeze(1).to_broadcast([P, PAIR, P]),
                                            jT[:, bass.ds(at, PAIR)].unsqueeze(2).to_broadcast([P, PAIR, P]),
                                            ALU.is_equal).then_inc(made, 1)
                    for n in range(PAIR):
                        nc.vector.tensor_scalar(A[:, g * PAIR + n, :], m.iota[:], iT[:, bass.ds(at + n, 1)],
                                                gT[:, bass.ds(at + n, 1)], ALU.is_equal, ALU.mult).then_inc(made, 1)
            dve.wait_ge(highs, 1)
            nc.vector.tensor_tensor(low[:], x[:], high[:].bitcast(F32), ALU.subtract)


def key_experts(nc, m, blk, G, x, high, low):
    first, loop, last_tiles = (name + str(blk) for name in ("table_first", "table", "table_last"))
    hid, gelu, weighted, rounded, split = (m.sem(f"ke{blk}_{n}") for n in (
        "hid", "gelu", "weighted", "rounded", "split"))
    with nc.Block() as block, ExitStack() as mem:
        sb = lambda n, dt=F32: mem.enter_context(nc.sbuf_tensor(f"ke{blk}_{n}", [P, 2, BLK], dt))
        ge, gated, gated_high, gated_low = sb("ge"), sb("gated"), sb("gated_high", F32R), sb("gated_low", F32R)

        @block.sync
        def _(sp):
            m.stream.loads(sp, first, loop, last_tiles)

        @block.tensor
        def _(pe):
            pe.sem_inc(gelu, 2)
            pe.sem_inc(split, 2)

            def hidden(name, k, it, tile, b):
                u = [w.rearrange("p (c j) -> p c j", c=KT) for w in m.stream.weights(pe, name, k, it)]
                pe.wait_ge(gelu, tile + 1)
                for c in range(KT):
                    last = times(nc, m.ps[:, 4 + b, 0:BLK], [w[:, c, :] for w in u], [high[:, c, :], low[:, c, :]],
                                 start=c == 0, stop=c == KT - 1)
                last.then_inc(m.chunk_done, 1)

            def output(name, k, it, tile, b, stop=False):
                v = m.stream.weights(pe, name, k, it)
                pe.wait_ge(split, tile + 3)
                for tt in range(2):
                    for half in range(2):
                        last = times(nc, m.ps[:, 2 * tt + half, :],
                                     [w[:, b, tt * P:(tt + 1) * P] for w in (gated_high, gated_low)],
                                     [w[:, half * T:(half + 1) * T] for w in v], start=False, stop=stop,
                                     skip_group_check=True)
                last.then_inc(m.chunk_done, 1)

            for b in range(4):
                nc.tensor.matmul(m.ps[:, b, :], m.zeros[:], x[:, 0:2, :], start=True, stop=False,
                                 skip_group_check=True)
            hidden(first, 0, 0, 0, 0)
            with pe.Fori(0, (KEYS - 2) // STEP) as it:
                for j in range(STEP):
                    hidden(loop, 2 * j, it, it * STEP + (j + 1), (j + 1) % 2)
                    output(loop, 2 * j + 1, it, it * STEP + j, j % 2)
            hidden(last_tiles, 0, 0, KEYS - 1, 1)
            output(last_tiles, 1, 0, KEYS - 2, 0)
            output(last_tiles, 2, 0, KEYS - 1, 1, stop=True)

        @block.scalar
        def _(act):
            def activate(name, k, it, tile, b):
                m.stream.done(act, name, k, it)
                act.wait_ge(split, tile + 1)
                nc.scalar.activation(ge[:, b, :], m.ps[:, 4 + b, 0:BLK], ACT.Gelu).then_inc(gelu, 1)
                m.stream.high(act, name, k, it)

            def passing(name, k, it):
                m.stream.done(act, name, k, it)
                m.stream.high(act, name, k, it)

            activate(first, 0, 0, 0, 0)
            with act.Fori(0, (KEYS - 2) // STEP) as it:
                for j in range(STEP):
                    activate(loop, 2 * j, it, it * STEP + (j + 1), (j + 1) % 2)
                    passing(loop, 2 * j + 1, it)
            activate(last_tiles, 0, 0, KEYS - 1, 1)
            passing(last_tiles, 1, 0)
            passing(last_tiles, 2, 0)

        @block.vector
        def _(dve):
            def gate(name, k, it, tile, b):
                m.stream.done(dve, name, k, it)
                dve.wait_ge(gelu, tile + 3)
                g = G[:, :, bass.ds(tile, 1)].rearrange("p t o -> p (t o)")
                nc.vector.tensor_tensor(gated[:, b, :], ge[:, b, :], g, ALU.mult).then_inc(weighted, 1)
                nc.vector.tensor_tensor(gated_high[:, b, :], ge[:, b, :], g, ALU.mult).then_inc(rounded, 1)
                dve.wait_ge(weighted, tile + 1)
                dve.wait_ge(rounded, tile + 1)
                nc.vector.tensor_tensor(gated_low[:, b, :], gated[:, b, :], gated_high[:, b, :].bitcast(F32),
                                        ALU.subtract).then_inc(split, 1)
                m.stream.low(dve, name, k, it)

            def passing(name, k, it):
                m.stream.done(dve, name, k, it)
                m.stream.low(dve, name, k, it)

            gate(first, 0, 0, 0, 0)
            with dve.Fori(0, (KEYS - 2) // STEP) as it:
                for j in range(STEP):
                    gate(loop, 2 * j, it, it * STEP + (j + 1), (j + 1) % 2)
                    passing(loop, 2 * j + 1, it)
            gate(last_tiles, 0, 0, KEYS - 1, 1)
            passing(last_tiles, 1, 0)
            passing(last_tiles, 2, 0)


def last_norm(nc, m, blk, out, x):
    turned, scaled, loaded, steps, chain_s, stored = (m.sem(f"ln{blk}_{n}") for n in (
        "turned", "scaled", "loaded", "steps", "chain", "stored"))
    with nc.Block() as block, ExitStack() as mem:
        sb = lambda n, s: mem.enter_context(nc.sbuf_tensor(f"ln{blk}_{n}", s, F32))
        st, ln2 = sb("st", [P, 2, 2]), sb("ln2", [P, 2, D])
        y, sq = sb("y", [P, 2, D]), sb("sq", [P, 2, D])

        @block.sync
        def _(sp):
            sp.dma_start(ln2[:, 0, :], m.i["ln2"][0:1, :].broadcast_to([P, D])).then_inc(loaded, 16)
            sp.dma_start(ln2[:, 1, :], m.i["ln2"][1:2, :].broadcast_to([P, D])).then_inc(loaded, 16)
            for tt in range(2):
                sp.wait_ge(chain_s, 10 + tt)
                sp.dma_start(out[blk * BLK + tt * P:blk * BLK + (tt + 1) * P, :], y[:, tt, :]).then_inc(stored, 16)
            sp.wait_ge(stored, 32)

        @block.tensor
        def _(pe):
            for tt in range(2):
                for k in range(KT):
                    last = nc.tensor.transpose(m.ps[:, 4 + 2 * tt + k // 4, (k % 4) * P:(k % 4 + 1) * P],
                                               x[:, k, tt * P:(tt + 1) * P], m.ident[:])
                last.then_inc(turned, 1)

        @block.scalar
        def _(act):
            for tt in range(2):
                act.wait_ge(turned, tt + 1)
                nc.scalar.mul(sq[:, tt, :], m.ps[:, 4 + 2 * tt:6 + 2 * tt, :].rearrange("p a f -> p (a f)"), ALPHA
                              ).then_inc(scaled, 1)
            for tt in range(2):
                act.wait_ge(chain_s, tt + 1)
                nc.scalar.activation(sq[:, tt, :], y[:, tt, :], ACT.Copy, accum_out=st[:, 0, tt:tt + 1]
                                     ).then_inc(steps, 1)
            for tt in range(2):
                act.wait_ge(chain_s, tt + 4)
                nc.scalar.activation(sq[:, tt, :], y[:, tt, :], ACT.Square, accum_out=st[:, 1, tt:tt + 1]
                                     ).then_inc(steps, 1)
            act.wait_ge(chain_s, 6)
            nc.scalar.activation(st[:, 1, :], st[:, 1, :], ACT.Sqrt).then_inc(steps, 1)

        @block.vector
        def _(dve):
            link = Chain(dve, chain_s)
            for tt in range(2):
                dve.wait_ge(scaled, tt + 1)
                experts_y = m.ps[:, 2 * tt:2 * tt + 2, :].rearrange("p a f -> p (a f)")
                link(nc.vector.tensor_tensor(y[:, tt, :], sq[:, tt, :], experts_y, ALU.add))
            dve.wait_ge(steps, 2)
            link(nc.vector.tensor_scalar(st[:, 0, :], st[:, 0, :], -1.0 / D, None, ALU.mult))
            for tt in range(2):
                link(nc.vector.tensor_scalar(y[:, tt, :], y[:, tt, :], st[:, 0, tt:tt + 1], None, ALU.add))
            dve.wait_ge(steps, 4)
            link(nc.vector.tensor_scalar(st[:, 1, :], st[:, 1, :], 1.0 / D, LN_EPS, ALU.mult, ALU.add))
            dve.wait_ge(steps, 5)
            link(nc.vector.reciprocal(st[:, 1, :], st[:, 1, :]))
            dve.wait_ge(loaded, 32)
            for tt in range(2):
                link(nc.vector.scalar_tensor_tensor(out=y[:, tt, :], in0=y[:, tt, :], scalar=st[:, 1, tt:tt + 1],
                                                    in1=ln2[:, 0, :], op0=ALU.mult, op1=ALU.mult))
            for tt in range(2):
                link(nc.vector.tensor_tensor(y[:, tt, :], y[:, tt, :], ln2[:, 1, :], ALU.add))


def segments(i):
    w = i["w_in"]
    table = {
        "table_first": (1, 1, table_parts(i["u"], i["v"], [("u", 0)])),
        "table": ((KEYS - 2) // STEP, 2 * STEP, table_parts(i["u"], i["v"], [
            t for j in range(STEP) for t in (("u", j + 1), ("v", j))])),
        "table_last": (1, 3, table_parts(i["u"], i["v"], [("u", KEYS - 1), ("v", KEYS - 2), ("v", KEYS - 1)])),
    }
    return {
        "ada": (2, 3 * KT, wide_columns(i["ada_w"], 3 * KT)),
        "attn_qk": (1, 16, columns(i["attn_w_in"][:, 0:2 * D], 16)),
        "attn_v": (1, 8, wide_columns(i["attn_w_in"][:, 2 * D:3 * D], 8)),
        "attn_out": (1, 8, columns(i["attn_w_out"], 8)),
        "experts": (EXPERTS, 12, expert_parts(i["w_gate"], i["w_up"], i["w_down"])),
        "fox_qk": (1, 8, columns(w[:, 0:D], 8)),
        "fox_v": (1, 4, wide_columns(w[:, FOX_V:FOX_F], 4)),
        "rwkv_in": (1, 14, columns(w[:, RWKV_AT:GATE_AT], 14)),
        "merge": (2, 12, merge_parts(w, i["p_fox"], i["p_rwkv"])),
        "w_o": (1, 8, columns(i["w_o"], 8)),
        "peer_q": (1, 2 * HEADS, columns(i["peer_w_q"], 2 * HEADS)),
        **{name + str(blk): segment for blk in range(T // BLK) for name, segment in table.items()},
    }


def recycle(nc, sems):
    numbers = sorted(s.num for s in sems)
    with nc.Block() as block:
        @block.gpsimd
        def _(pool):
            at = 0
            while at < len(numbers):
                end = at
                while end + 1 < len(numbers) and numbers[end + 1] == numbers[end] + 1:
                    end += 1
                pool.sem_clear(range(numbers[at], numbers[end] + 1))
                at = end + 1
    for s in sems:
        nc.release_semaphore(s)
    sems.clear()


def build_program(nc, i, out):
    stage_sems = []

    def keep_sem(name):
        return ctx.enter_context(nc.semaphore(name))

    def sem(name):
        stage_sems.append(nc.alloc_semaphore(name))
        return stage_sems[-1]

    with ExitStack() as ctx:
        def allocate(scope, dt=F32):
            return lambda n, s, dt=dt: scope.enter_context(nc.sbuf_tensor(n, s, dt))

        def pair(scope, name, shape):
            return [allocate(scope)(name + part, shape, F32R) for part in ("_high", "_low")]

        sb = allocate(ctx)
        m = Shared()
        m.nc, m.i, m.sem = nc, i, sem
        m.raw = sb("raw", [P, RAW, CH])
        m.w_high, m.w_low = pair(ctx, "w", [P, AHEAD, CH])
        m.slot_full = [keep_sem(f"slot_full{n}") for n in range(RAW)]
        m.high_done, m.split_done, m.chunk_done, m.settled = (
            keep_sem(n) for n in ("high_done", "split_done", "chunk_done", "settled"))
        m.stream = Stream(m, segments(i))
        m.ps = ctx.enter_context(nc.psum_tensor("ps", [P, 8, T], F32))
        m.vec = sb("vec", [P, NVEC])
        m.v = lambda name: m.vec[:, VEC_AT[name][0]:VEC_AT[name][1]]
        m.ones, m.ident, m.zeros, m.iota = (sb(n, [P, P]) for n in ("ones", "ident", "zeros", "iota"))
        iT, jT, gT = sb("iT", [P, T]), sb("jT", [P, T]), sb("gT", [P, T])
        x4 = nc.dram_tensor("x4", (D, T), F32, kind="Internal").ap()
        with ExitStack() as early:
            sb = allocate(early)
            m.halves, m.iota_i = sb("halves", [P, P]), sb("iota_i", [P, P], I32)
            m.neg_lam, m.mod = sb("neg_lam", [P, 1]), sb("mod", [P, 6 * KT])
            m.norm1, m.norm2 = sb("norm1", [P, KT]), sb("norm2", [P, KT])
            m.router_w, m.router_b = sb("router_w", [P, KT, 20]), sb("router_b", [P, 20])
            m.router_h, m.router_l = pair(early, "router", [P, KT, 20])
            m.xT = sb("xT", [P, KT, T])

            with ExitStack() as mem:
                sb = allocate(mem)
                m.lam_row, m.lam_prod = sb("lam_row", [P, 4 * DH]), sb("lam_prod", [P, 2, DH])
                m.lam_dot, m.lam_e, m.cond = sb("lam_dot", [P, 2]), sb("lam_e", [P, 2]), sb("cond", [P, KT])
                m.cond_high, m.cond_low = pair(mem, "cond", [P, KT, P])
                setup(nc, m)
                modulation(nc, m)
            with ExitStack() as mem:
                m.oT = allocate(mem)("oT", [P, HEADS, T])
                with ExitStack() as inner:
                    sb = allocate(inner)
                    qT, kT, v = sb("qT", [P, HEADS, T]), sb("kT", [P, HEADS, T]), sb("v", [P, TT, D])
                    with ExitStack() as normed:
                        h = pair(normed, "h1", [P, KT, T])
                        rms_norm(nc, m, "norm_mix", m.norm1, m.mod[:, 0:KT], *h)
                        qkv_projection(nc, m, *h, qT, kT, v)
                    diff_attention(nc, m, qT, kT, v)
                o = pair(mem, "o", [P, HEADS, T])
                head_norm(nc, m, *o)
                add_projection(nc, m, *o)
            with ExitStack() as mem:
                h = pair(mem, "h2", [P, KT, T])
                rms_norm(nc, m, "norm_ffn", m.norm2, m.mod[:, 3 * KT:4 * KT], *h)
                gate_bc = allocate(mem)("gate_bc", [P, EXPERTS, T])
                router(nc, m, *h, gate_bc)
                experts(nc, m, *h, gate_bc)
            with ExitStack() as mem:
                sb = allocate(mem)
                yf, yr = sb("yf", [P, 4, T]), sb("yr", [P, 4, T])
                with ExitStack() as inner:
                    sb = allocate(inner)
                    cols = sb("cols", [P, 14, T + 1])
                    with ExitStack() as attn:
                        sb = allocate(attn)
                        fq, fk, fv = sb("fq", [P, 4, T]), sb("fk", [P, 4, T]), sb("fv", [P, TT, T])
                        negc, cq = sb("negc", [P, HEADS, T]), sb("cq", [P, TT, HEADS])
                        with ExitStack() as normed:
                            x3 = pair(normed, "x3", [P, KT, T])
                            rms_norm(nc, m, "norm_final", m.v("norm_final"), None, *x3, keep=True)
                            second_projection(nc, m, *x3, fq, fk, fv, cols, negc, cq)
                        fox_attention(nc, m, fq, fk, fv, negc, cq, yf)
                    w = Shared()
                    sb = allocate(inner)
                    w.kk, w.bonus, w.b, w.g = (sb("w_" + n, [P, 4, T]) for n in ("kk", "bonus", "b", "g"))
                    w.r, w.k, w.v = (cols[:, n:n + 4, 1:T + 1] for n in (0, 4, 8))
                    w.carry = sb("w_carry", [P, 4, NCHUNK])
                    time_mix_inputs(nc, m, cols, w)
                    recurrence(nc, m, w, yr)
                    time_mix_output(nc, m, w, yr)
                recycle(nc, stage_sems)
                merged = pair(mem, "merged", [P, KT, T])
                with ExitStack() as inner:
                    merge(nc, m, yf, yr, pair(inner, "x3m", [P, KT, T]), pair(inner, "yf", [P, 4, T]),
                          pair(inner, "yr", [P, 4, T]), merged)
                output_and_norm(nc, m, *merged)
            with ExitStack() as mem:
                scores = allocate(mem)("scores", [P, TT, 2 * HEADS * KEYS])
                with ExitStack() as inner:
                    sb = allocate(inner)
                    q, keys = sb("q", [P, 2 * HEADS, T]), sb("keys", [P, 2 * HEADS, KEYS])
                    key_scores(nc, m, *pair(inner, "x4", [P, KT, T]), q, keys, x4, scores)
                choose(nc, m, scores, iT, jT, gT)
        for blk in range(T // BLK):
            with ExitStack() as mem:
                sb = allocate(mem)
                x = sb(f"x{blk}", [P, KT, BLK])
                with ExitStack() as inner:
                    parts = pair(inner, f"x{blk}", [P, KT, BLK])
                    G = allocate(inner)(f"G{blk}", [P, BLK, KEYS])
                    gate_matrices(nc, m, blk, G, iT, jT, gT, x4, x, *parts)
                    key_experts(nc, m, blk, G, x, *parts)
                last_norm(nc, m, blk, out, x)


def lay_out(x):
    tile = lambda v: np.asarray(v).reshape(-1, P).T
    src = {"c": "c", "norm_mix": "norm_mix", "norm_ffn": "norm_ffn", "norm_final": "norm_final", "ln1_g": "ln1_g_2",
           "ln1_b": "ln1_b_2", "ada_b": "ada_b", "subln": "attn_subln", "mu": "rwkv_mu_2", "w0": "rwkv_w0_2",
           "a0": "rwkv_a0_2", "k_k": "rwkv_k_k_2", "k_a": "rwkv_k_a_2", "r_k": "rwkv_r_k_2", "ln_g": "rwkv_ln_g_2",
           "ln_b": "rwkv_ln_b_2"}
    a = {}
    a["vecs"] = np.concatenate([tile(x[src[n]]) for n, _ in VEC_NAMES], 1)
    a["lams"] = np.concatenate([np.asarray(x["attn_lam_" + n]) for n in ("q1", "k1", "q2", "k2")], 1)
    a["xT"] = np.asarray(x["x"])[0].T
    a["ada_w"] = np.asarray(x["ada_w"])[0]
    a["attn_w_in"] = np.asarray(x["attn_w_in"])[0]
    a["attn_w_out"] = np.asarray(x["attn_w_out"])[0]
    a["router_w"] = np.concatenate([np.asarray(x["router_group_w"])[0],
                                    np.asarray(x["router_expert_w"])[0].reshape(D, EXPERTS)], 1)
    a["router_b"] = np.concatenate([np.asarray(x["router_group_b"]),
                                    np.asarray(x["router_expert_b"]).reshape(1, EXPERTS)], 1)
    for n in ("gate", "up", "down"):
        a["w_" + n] = np.asarray(x["expert_w_" + n])[0]
    a["w_in"] = np.asarray(x["w_in_2"])[0]
    a["f_w"] = a["w_in"][:, FOX_F:RWKV_AT]
    a["f_b"] = np.asarray(x["fox_f_bias_2"]).reshape(HEADS, 1)
    a["w2a2"] = np.concatenate([np.asarray(x["rwkv_w2_2"])[0], np.asarray(x["rwkv_a2_2"])[0]], 0)
    a["g2"] = np.asarray(x["rwkv_g2_2"])[0]
    for n in ("p_fox", "p_rwkv", "w_o", "peer_w_q"):
        a[n] = np.asarray(x[n + "_2"])[0]
    a["keys"] = np.asarray(x["peer_sub_keys_2"])[0].transpose(3, 0, 1, 2).reshape(P, 2 * HEADS * KEYS)
    a["u"] = np.asarray(x["peer_u_2"])[0].reshape(KEYS, KEYS, KT, P).transpose(0, 3, 2, 1).reshape(KEYS, P, D)
    a["v"] = np.asarray(x["peer_v_2"])[0].reshape(KEYS, KEYS, D)
    a["ln2"] = np.concatenate([np.asarray(x["ln2_g_2"]), np.asarray(x["ln2_b_2"])], 0)
    return {n: np.ascontiguousarray(v) for n, v in a.items()}


def kernel(**inputs):
    import concourse.bacc as bacc
    from concourse.bass_utils import run_bass_kernel_spmd

    nc = bacc.Bacc("TRN2", target_bir_lowering=False, num_devices=1)
    arrays = lay_out(inputs)
    i = {n: nc.dram_tensor("in_" + n, a.shape, mybir.dt.from_np(a.dtype), kind="ExternalInput").ap()
         for n, a in arrays.items()}
    out = nc.dram_tensor("out", (T, D), F32, kind="ExternalOutput").ap()
    build_program(nc, i, out)
    r = run_bass_kernel_spmd(nc, [{"in_" + n: a for n, a in arrays.items()}], core_ids=[0])
    return r.results[0]["out"].reshape(1, T, D)
```

```python
import math
from contextlib import ExitStack, contextmanager

import numpy as np

import concourse.bass as bass
from concourse import mybir

F32 = mybir.dt.float32
F32R = mybir.dt.float32r
I32 = mybir.dt.int32
U32 = mybir.dt.uint32
ALU = mybir.AluOpType
ACT = mybir.ActivationFunctionType
AX = mybir.AxisListType

P = 128
D = 1024
T = 512
KT = D // P
TT = T // P
HEADS = 8
DH = 64
EXPERTS = 16
EXPERT_GROUPS = 4
EPS = 1e-6
LN_EPS = 1e-5
GN_EPS = 64e-5
ALPHA = 2.0 ** 0.25
LAM_INIT = 0.8 - 0.6 * math.exp(0.0)
CHUNK = 64
NCHUNK = T // CHUNK
KEYS = 128
TOPK = 16
NEG = -1e30

VEC_NAMES = [("c", 8), ("norm_mix", 8), ("norm_ffn", 8), ("norm_final", 8), ("ln1_g", 8), ("ln1_b", 8),
             ("ada_b", 48), ("subln", 1), ("mu", 14), ("w0", 4), ("a0", 4), ("k_k", 4), ("k_a", 4),
             ("r_k", 4), ("ln_g", 4), ("ln_b", 4)]
VEC_AT, _n = {}, 0
for _name, _w in VEC_NAMES:
    VEC_AT[_name] = (_n, _n + _w)
    _n += _w
NVEC = _n

FOX_Q, FOX_V, FOX_F, RWKV_AT, GATE_AT = 0, 1024, 1536, 1544, 3336


class Shared:
    pass


class Chain:

    def __init__(self, eng, sem):
        self.eng, self.sem, self.base, self.k, self.reg, self.per = eng, sem, 0, 0, None, 0

    def value(self):
        v = self.base + self.k
        return v if self.reg is None else self.reg * self.per + v

    def __call__(self, ins):
        ins.then_inc(self.sem, 1)
        self.k += 1
        self.eng.wait_ge(self.sem, self.value())

    @contextmanager
    def loop(self, n, per):
        self.base, self.k = self.base + self.k, 0
        with self.eng.Fori(0, n) as i:
            self.reg, self.per = i, per
            yield i
        assert self.k == per, (self.k, per)
        self.reg, self.base, self.k = None, self.base + n * per, 0

    @contextmanager
    def fresh_loop(self, n):
        with self.eng.Fori(0, n) as i:
            self.eng.sem_clear(self.sem)
            self.base = self.k = 0
            yield i


def settle(m, eng, sem, value):
    eng.wait_ge(sem, value)
    eng.sem_inc(m.settled, 1)


RAW = 3
AHEAD = 3
CH = 1024


class Stream:

    def __init__(self, m, segments):
        self.m, self.start, self.segments = m, {}, segments
        n = 0
        for name, (rounds, period, parts) in segments.items():
            self.start[name] = n
            n += rounds * period
        self.total = n

    def count(self, name, k, it, per_chunk=1, more=0):
        n = per_chunk * (self.start[name] + k) + more
        return n if isinstance(it, int) and it == 0 else it * (per_chunk * self.segments[name][1]) + n

    def full(self, name, k, it):
        n = self.start[name] + k
        value = 16 * (n // RAW + 1)
        period = self.segments[name][1]
        if isinstance(it, int) and it == 0:
            return value
        assert period % RAW == 0
        return it * (16 * period // RAW) + value

    def done(self, eng, name, k, it=0):
        eng.wait_ge(self.m.chunk_done, self.count(name, k, it, more=1))

    def weights(self, pe, name, k, it=0):
        pe.wait_ge(self.m.split_done, self.count(name, k, it, more=1))
        slot = (self.start[name] + k) % AHEAD
        return self.m.w_high[:, slot, :], self.m.w_low[:, slot, :]

    def high(self, act, name, k, it=0):
        n = self.start[name] + k + AHEAD
        if n >= self.total:
            return
        act.wait_ge(self.m.slot_full[n % RAW], self.full(name, k + AHEAD, it))
        self.m.nc.scalar.copy(self.m.w_high[:, n % AHEAD, :], self.m.raw[:, n % RAW, :]
                              ).then_inc(self.m.high_done, 1)

    def low(self, dve, name, k, it=0):
        n = self.start[name] + k + AHEAD
        if n >= self.total:
            return
        dve.wait_ge(self.m.high_done, self.count(name, k, it, more=AHEAD + 1))
        self.m.nc.vector.tensor_tensor(self.m.w_low[:, n % AHEAD, :], self.m.raw[:, n % RAW, :],
                                       self.m.w_high[:, n % AHEAD, :].bitcast(F32), ALU.subtract
                                       ).then_inc(self.m.split_done, 1)

    def load(self, sp, name, k, it=0, first=False):
        rounds, period, parts = self.segments[name]
        slot = (self.start[name] + k) % RAW
        if not first:
            settle(self.m, sp, self.m.split_done, self.count(name, k, it, more=1 - RAW))
        dst, src = parts(self.m.raw[:, slot, :], k, it)
        sp.dma_start(dst, src).then_inc(self.m.slot_full[slot], 16)

    def loads(self, sp, *names):
        rounds, period, _ = self.segments[names[-1]]
        lo = self.start[names[0]] + RAW + AHEAD
        hi = min(self.start[names[-1]] + rounds * period + RAW + AHEAD, self.total)
        for name, (rounds, period, _) in self.segments.items():
            at = self.start[name]
            a, b = max(lo, at), min(hi, at + rounds * period)
            if a >= b:
                continue
            off, whole = a - at, (b - a) // period
            if rounds > 1 and whole > 1:
                with sp.Fori(0, whole) as it:
                    for j in range(off, off + period):
                        self.load(sp, name, j % period, it + j // period)
                off += whole * period
            for j in range(off, b - at):
                self.load(sp, name, j % period, j // period)


def columns(w, period):
    kt = w.shape[0] // P
    width = CH // kt
    src = w.rearrange("(k p) f -> p k f", p=P)

    def parts(slot, k, it):
        return slot.rearrange("p (k f) -> p k f", k=kt), src[:, :, bass.ds(it * (period * width) + k * width, width)]
    return parts


def wide_columns(w, period):
    src = w.rearrange("(k p) f -> p k f", p=P)

    def parts(slot, k, it):
        return (slot.rearrange("p (k f) -> p k f", f=256),
                src[:, (k % 2) * 4:(k % 2) * 4 + 4, bass.ds(it * (period * P) + (k // 2) * 256, 256)])
    return parts


def expert_parts(gate, up, down):
    views = [w.rearrange("e (k p) f -> p e k f", p=P) for w in (gate, up, down)]

    def parts(slot, k, it):
        which, at = (k % 2, k // 2) if k < 8 else (2, k - 8)
        kt = KT if k < 8 else 4
        width = CH // kt
        src = views[which][:, bass.ds(it, 1), :, at * width:(at + 1) * width].rearrange("p e k f -> p (e k) f")
        return slot.rearrange("p (k f) -> p k f", k=kt), src
    return parts


STEP = 6


def table_parts(u, v, tiles):
    def parts(slot, k, it):
        which, first = tiles[k]
        return slot, (v if which == "v" else u)[bass.ds(it * STEP + first, 1)].rearrange("a p f -> p (a f)")
    return parts


def merge_parts(w_in, p_fox, p_rwkv):
    gates, fox, rwkv = (w.rearrange("(k p) f -> p k f", p=P) for w in (w_in, p_fox, p_rwkv))

    def parts(slot, k, it):
        group, k = divmod(k, 6)
        at = it * 512 + group * 256
        if k < 4:
            return (slot.rearrange("p (k f) -> p k f", k=KT),
                    gates[:, :, bass.ds(at + (GATE_AT + (k // 2) * D + (k % 2) * P), P)])
        return slot.rearrange("p (k f) -> p k f", k=4), (fox, rwkv)[k - 4][:, :, bass.ds(at, 256)]
    return parts


def inverse_root(nc, act, x, steps, at):
    nc.scalar.activation(x, x, ACT.Ln).then_inc(steps, 1)
    act.wait_ge(steps, at + 1)
    nc.scalar.activation(x, x, ACT.Exp, scale=-0.5).then_inc(steps, 1)


def times(nc, out, w, a, start, stop, **more):
    nc.tensor.matmul(out, w[0], a[0], start=start, stop=False, **more)
    nc.tensor.matmul(out, w[0], a[1], start=False, stop=False, **more)
    return nc.tensor.matmul(out, w[1], a[0], start=False, stop=stop, **more)


def setup(nc, m):
    vec_loaded, lam_loaded, x_loaded, made, chain_s, silu_done = (
        m.sem(n) for n in ("vec_loaded", "lam_loaded", "x_loaded", "made", "setup_chain", "silu_done"))
    with nc.Block() as block:
        @block.sync
        def _(sp):
            sp.dma_start(m.vec[:], m.i["vecs"]).then_inc(vec_loaded, 16)
            for n in range(RAW):
                m.stream.load(sp, "ada", n, first=True)
            sp.dma_start(m.lam_row[:], m.i["lams"].broadcast_to([P, 4 * DH])).then_inc(lam_loaded, 16)
            sp.dma_start(m.xT[:], m.i["xT"].rearrange("(k p) t -> p k t", p=P)).then_inc(x_loaded, 16)
            sp.dma_start(m.router_w[:], m.i["router_w"].rearrange("(k p) f -> p k f", p=P)).then_inc(x_loaded, 16)
            sp.dma_start(m.router_b[:], m.i["router_b"].broadcast_to([P, 20])).then_inc(x_loaded, 16)
            for n in range(RAW, RAW + AHEAD):
                m.stream.load(sp, "ada", n)
            sp.wait_ge(x_loaded, 48)

        @block.gpsimd
        def _(pool):
            link = Chain(pool, chain_s)
            link(nc.gpsimd.memset(m.ones[:], 1.0))
            link(nc.gpsimd.memset(m.zeros[:], 0.0))
            link(nc.gpsimd.memset(m.ident[:], 0.0))
            link(nc.gpsimd.affine_select(out=m.ident[:], in_=m.ident[:], compare_op=ALU.not_equal, fill=1.0,
                                         base=0, pattern=[[-1, P]], channel_multiplier=1))
            link(nc.gpsimd.memset(m.halves[:], 0.0))
            link(nc.gpsimd.memset(m.halves[0:DH, 0:DH], 1.0))
            link(nc.gpsimd.memset(m.halves[DH:P, DH:P], 1.0))
            link(nc.gpsimd.iota(m.iota_i[:], pattern=[[1, P]], base=0, channel_multiplier=0))
            link(nc.gpsimd.tensor_copy(m.iota[:], m.iota_i[:]))

        @block.scalar
        def _(act):
            act.wait_ge(vec_loaded, 16)
            nc.scalar.activation(m.cond[:], m.v("c"), ACT.Silu).then_inc(silu_done, 1)
            for n in range(AHEAD):
                m.stream.high(act, "ada", n - AHEAD)
            act.wait_ge(silu_done, 1)
            nc.scalar.copy(m.cond_high[:], m.cond[:].unsqueeze(2).to_broadcast([P, KT, P])).then_inc(silu_done, 1)
            act.wait_ge(x_loaded, 48)
            nc.scalar.copy(m.router_h[:], m.router_w[:]).then_inc(silu_done, 1)

        @block.vector
        def _(dve):
            link = Chain(dve, made)
            dve.wait_ge(lam_loaded, 16)
            link(nc.vector.tensor_tensor(m.lam_prod[:], m.lam_row[:].rearrange("p (a b d) -> p a b d", a=2, b=2)[:, :, 0, :],
                                         m.lam_row[:].rearrange("p (a b d) -> p a b d", a=2, b=2)[:, :, 1, :], ALU.mult))
            link(nc.vector.tensor_reduce(m.lam_dot[:], m.lam_prod[:], AX.X, ALU.add))
            for n in range(AHEAD):
                m.stream.low(dve, "ada", n - AHEAD)
            dve.wait_ge(silu_done, 3)
            link(nc.vector.tensor_tensor(m.cond_low[:], m.cond[:].unsqueeze(2).to_broadcast([P, KT, P]),
                                         m.cond_high[:].bitcast(F32), ALU.subtract))
            link(nc.vector.tensor_tensor(m.router_l[:], m.router_w[:], m.router_h[:].bitcast(F32), ALU.subtract))


def modulation(nc, m):
    mod_free, mod_chain, lam_exp, steps = (m.sem(n) for n in ("mod_free", "mod_chain", "lam_exp", "mod_steps"))
    with nc.Block() as block, ExitStack() as mem:
        own = mem.enter_context(nc.sbuf_tensor("mod_own", [P, KT, P], F32))

        @block.sync
        def _(sp):
            m.stream.loads(sp, "ada")

        @block.tensor
        def _(pe):
            pe.sem_inc(mod_free, 3)
            with pe.Fori(0, 2) as it:
                for v in range(3):
                    pe.wait_ge(mod_free, it * 3 + (v + 1))
                    for k in range(KT):
                        w = m.stream.weights(pe, "ada", v * KT + k, it)
                        for j in range(4):
                            c = 4 * (k % 2) + j
                            last = times(nc, m.ps[:, 2 * v + k // 4, (k // 2 % 2) * 256:(k // 2 % 2 + 1) * 256],
                                         [m.cond_high[:, c, :], m.cond_low[:, c, :]],
                                         [x[:, j * 256:(j + 1) * 256] for x in w], start=c == 0, stop=c == KT - 1)
                        last.then_inc(m.chunk_done, 1)

        @block.scalar
        def _(act):
            nc.scalar.activation(m.lam_e[:], m.lam_dot[:], ACT.Exp).then_inc(lam_exp, 1)
            with act.Fori(0, 2) as it:
                for k in range(3 * KT):
                    m.stream.done(act, "ada", k, it)
                    m.stream.high(act, "ada", k, it)

        @block.vector
        def _(dve):
            link = Chain(dve, steps)
            with link.loop(2, 6) as it:
                for v in range(3):
                    for k in range(KT):
                        m.stream.done(dve, "ada", v * KT + k, it)
                        m.stream.low(dve, "ada", v * KT + k, it)
                    link(nc.vector.tensor_tensor(own[:], m.ps[:, 2 * v:2 * v + 2, :].rearrange(
                        "p b (k c) -> p (b k) c", c=P), m.ident[:].unsqueeze(1).to_broadcast([P, KT, P]), ALU.mult))
                    tiles = bass.ds(it * (3 * KT) + v * KT, KT)
                    link(nc.vector.tensor_reduce(m.mod[:, tiles], own[:], AX.X, ALU.add))
                    nc.vector.tensor_tensor(m.mod[:, tiles], m.mod[:, tiles], m.v("ada_b")[:, tiles], ALU.add
                                            ).then_inc(mod_free, 1)
            dve.wait_ge(mod_free, 9)
            link = Chain(dve, mod_chain)
            for out, scale, norm in ((m.norm1, 1, "norm_mix"), (m.norm2, 4, "norm_ffn")):
                link(nc.vector.tensor_scalar(out[:], m.mod[:, scale * KT:(scale + 1) * KT], 1.0, None, ALU.add))
                link(nc.vector.tensor_tensor(out[:], out[:], m.v(norm), ALU.mult))
            dve.wait_ge(lam_exp, 1)
            link(nc.vector.tensor_tensor(m.neg_lam[:], m.lam_e[:, 1:2], m.lam_e[:, 0:1], ALU.subtract))
            link(nc.vector.tensor_scalar(m.neg_lam[:], m.neg_lam[:], -LAM_INIT, None, ALU.add))


def rms_norm(nc, m, name, scale, shift, high, low, keep=False):
    squared, summed, rooted, chain_s, scaled, highs = (m.sem(f"{name}_{n}") for n in (
        "squared", "summed", "rooted", "chain", "scaled", "highs"))
    with nc.Block() as block, ExitStack() as mem:
        sq = mem.enter_context(nc.sbuf_tensor(f"{name}_sq", [P, KT, T], F32))
        inv_rms = mem.enter_context(nc.sbuf_tensor(f"{name}_rms", [P, T], F32))
        out = m.xT if keep else sq
        shifts = [0.0 if shift is None else shift[:, k:k + 1] for k in range(KT)]

        @block.scalar
        def _(act):
            for k in range(KT):
                nc.scalar.activation(sq[:, k, :], m.xT[:, k, :], ACT.Square).then_inc(squared, 1)
            act.wait_ge(chain_s, KT)
            inverse_root(nc, act, inv_rms[:], rooted, 0)
            for k in range(KT):
                act.wait_ge(scaled, k + 1)
                nc.scalar.activation(high[:, k, :], out[:, k, :], ACT.Identity, bias=shifts[k]).then_inc(highs, 1)

        @block.tensor
        def _(pe):
            pe.wait_ge(chain_s, KT - 1)
            nc.tensor.matmul(m.ps[:, 0, :], m.ones[:], sq[:, 0, :], start=True, stop=True).then_inc(summed, 1)

        @block.vector
        def _(dve):
            link = Chain(dve, chain_s)
            for k in range(1, KT):
                dve.wait_ge(squared, k + 1)
                link(nc.vector.tensor_tensor(sq[:, 0, :], sq[:, 0, :], sq[:, k, :], ALU.add))
            dve.wait_ge(summed, 1)
            link(nc.vector.tensor_scalar(inv_rms[:], m.ps[:, 0, :], 1.0 / D, EPS, ALU.mult, ALU.add))
            dve.wait_ge(rooted, 2)

            def rest(k):
                dve.wait_ge(highs, k + 1)
                nc.vector.scalar_tensor_tensor(out=low[:, k, :], in0=out[:, k, :], scalar=shifts[k],
                                               in1=high[:, k, :].bitcast(F32), op0=ALU.add, op1=ALU.subtract)

            for k in range(KT):
                nc.vector.scalar_tensor_tensor(out=out[:, k, :], in0=m.xT[:, k, :], scalar=scale[:, k:k + 1],
                                               in1=inv_rms[:], op0=ALU.mult, op1=ALU.mult).then_inc(scaled, 1)
                if k >= 2:
                    rest(k - 2)
            rest(KT - 2)
            rest(KT - 1)


def project(nc, m, pe, name, high, low, bank_free, chunks=8, n0=0, banks=8):
    if n0 == 0:
        pe.sem_inc(bank_free, banks)
    for k in range(chunks):
        w = [x.rearrange("p (c f) -> p c f", c=KT) for x in m.stream.weights(pe, name, k)]
        n = n0 + k
        pe.wait_ge(bank_free, n + 1)
        for c in range(KT):
            last = times(nc, m.ps[:, n % banks, :], [x[:, c, :] for x in w], [high[:, c, :], low[:, c, :]],
                         start=c == 0, stop=c == KT - 1)
        last.then_inc(m.chunk_done, 1)


def token_major(nc, m, pe, name, high, low, bank_free, groups, n0, banks=8):
    for k in range(2 * groups):
        w = m.stream.weights(pe, name, k)
        n = n0 + 4 * (k // 2)
        for tt in range(TT):
            if k % 2 == 0:
                pe.wait_ge(bank_free, n + tt + 1)
            toks = slice(tt * P, (tt + 1) * P)
            for j in range(4):
                c = 4 * (k % 2) + j
                last = times(nc, m.ps[:, (n + tt) % banks, 0:256], [high[:, c, toks], low[:, c, toks]],
                             [x[:, j * 256:(j + 1) * 256] for x in w], start=c == 0, stop=c == KT - 1)
        last.then_inc(m.chunk_done, 1)


def read_token_major(nc, bank_free, ps, out, k, n0, banks=8):
    if k % 2:
        for tt in range(TT):
            nc.scalar.copy(out[:, tt, (k // 2) * 256:(k // 2 + 1) * 256], ps[:, (n0 + 4 * (k // 2) + tt) % banks, 0:256]
                           ).then_inc(bank_free, 1)


def qkv_projection(nc, m, high, low, qT, kT, v):
    bank_free = m.sem("qkv_bank_free")
    with nc.Block() as block:
        @block.sync
        def _(sp):
            m.stream.loads(sp, "attn_qk", "attn_v")

        @block.tensor
        def _(pe):
            project(nc, m, pe, "attn_qk", high, low, bank_free, chunks=16)
            token_major(nc, m, pe, "attn_v", high, low, bank_free, 4, 16)

        @block.scalar
        def _(act):
            for n in range(16):
                m.stream.done(act, "attn_qk", n)
                if n < HEADS:
                    nc.scalar.mul(qT[:, n, :], m.ps[:, n % 8, :], DH ** -0.5).then_inc(bank_free, 1)
                else:
                    nc.scalar.copy(kT[:, n - HEADS, :], m.ps[:, n % 8, :]).then_inc(bank_free, 1)
                m.stream.high(act, "attn_qk", n)
            for n in range(8):
                m.stream.done(act, "attn_v", n)
                read_token_major(nc, bank_free, m.ps, v, n, 16)
                m.stream.high(act, "attn_v", n)

        @block.vector
        def _(dve):
            for n in range(16 + 8):
                m.stream.done(dve, "attn_qk", n)
                m.stream.low(dve, "attn_qk", n)


def diff_attention(nc, m, qT, kT, v):
    (qk_staged, v_staged, scored, biased, maxed, exped, mixed, turned, turned_out, unit_done, o_out, dist_made,
     chain_s) = (m.sem("da_" + n) for n in (
         "qk_staged", "v_staged", "scored", "biased", "maxed", "exped", "mixed", "turned", "turned_out",
         "unit_done", "o_out", "dist_made", "chain"))
    rounds, per = HEADS // 2, 2 * TT
    with nc.Block() as block, ExitStack() as mem:
        sb = lambda n, s, dt=F32: mem.enter_context(nc.sbuf_tensor("da_" + n, s, dt))
        dist_i = sb("dist_i", [P, TT, T], I32)
        dist = sb("dist", [P, TT, T])
        slope = sb("slope", [P, HEADS])
        q_st = sb("q_st", [P, 2, T])
        k_st = sb("k_st", [P, 2, T])
        v_st = sb("v_st", [P, 2, TT, P])
        s = sb("s", [P, 2, 2, T])
        e = sb("e", [P, 2, 2, T])
        neg_max = sb("neg_max", [P, 2, 2])
        z = sb("z", [P, 2, 2])
        a = sb("a", [P, 2, T])
        aT = sb("aT", [P, 2, TT, P])

        @block.gpsimd
        def _(pool):
            nc.gpsimd.iota(dist_i[:], pattern=[[P, TT], [-1, T]], base=0, channel_multiplier=1).then_inc(dist_made, 1)
            with pool.Fori(0, rounds) as it:
                for j in range(2):
                    pool.wait_ge(unit_done, it * per + TT * (j + 1))
                    for staged, whole in ((q_st, qT), (k_st, kT)):
                        nc.gpsimd.tensor_copy(staged[:, j, :], whole[:, bass.ds(it * 2 + j, 1), :].rearrange(
                            "p a t -> p (a t)")).then_inc(qk_staged, 1)
                    nc.gpsimd.tensor_copy(v_st[:, j, :, :], v[:, :, bass.ds((it * 2 + j) * P, P)]
                                          ).then_inc(v_staged, 1)

        @block.tensor
        def _(pe):
            pe.sem_inc(unit_done, per)
            pe.sem_inc(biased, 4)
            pe.sem_inc(turned_out, 2)
            pe.sem_inc(o_out, 2)

            def turn(it, u):
                b = u % 2
                pe.wait_ge(mixed, it * per + (u + 1))
                pe.wait_ge(turned_out, it * per + (u + 1))
                for kt in range(TT):
                    last = nc.tensor.transpose(m.ps[:, 4 * b + 2, kt * P:(kt + 1) * P],
                                               a[:, b, kt * P:(kt + 1) * P], m.ident[:])
                last.then_inc(turned, 1)

            def values(it, u):
                j, b = u // TT, u % 2
                if u % TT == 0:
                    pe.wait_ge(v_staged, it * 2 + (j + 1))
                pe.wait_ge(turned_out, it * per + (u + 3))
                pe.wait_ge(o_out, it * per + (u + 1))
                for kt in range(TT):
                    last = nc.tensor.matmul(m.ps[:, 4 * b + 3, 0:P], v_st[:, j % 2, kt, :], aT[:, b, kt, :],
                                            start=kt == 0, stop=kt == TT - 1)
                last.then_inc(unit_done, 1)

            def scores(it, u):
                j, qt = divmod(u, TT)
                if qt == 0:
                    pe.wait_ge(qk_staged, it * 4 + 2 * (j + 1))
                pe.wait_ge(biased, it * (2 * per) + (2 * u + 2))
                for c in range(2):
                    rows = slice(c * DH, (c + 1) * DH)
                    nc.tensor.matmul(m.ps[:, 4 * (u % 2) + c, :], q_st[rows, j % 2, qt * P:(qt + 1) * P],
                                     k_st[rows, j % 2, :], start=True, stop=True).then_inc(scored, 1)

            def steps(it, first, end, units):
                for u in range(first, end):
                    for lag, part in ((0, scores), (2, turn), (3, values)):
                        if 0 <= u - lag < units:
                            part(it, u - lag)

            steps(0, 0, 3, per)
            with pe.Fori(0, rounds - 1) as it:
                steps(it, 3, per + 3, 2 * per)
            steps(rounds - 1, 3, per + 3, per)

        @block.scalar
        def _(act):
            def transposed(it, u):
                act.wait_ge(turned, it * per + (u + 1))
                nc.scalar.copy(aT[:, u % 2, :, :], m.ps[:, 4 * (u % 2) + 2, :].rearrange("p (k q) -> p k q", k=TT)
                               ).then_inc(turned_out, 1)

            def output(it, u):
                act.wait_ge(unit_done, it * per + (per + u + 1))
                nc.scalar.copy(m.oT[:, bass.ds(it * 2 + u // TT, 1), (u % TT) * P:(u % TT + 1) * P],
                               m.ps[:, 4 * (u % 2) + 3, 0:P].rearrange("p (a q) -> p a q", a=1)).then_inc(o_out, 1)

            act.wait_ge(dist_made, 1)
            nc.scalar.activation(dist[:], dist_i[:], ACT.Abs).then_inc(dist_made, 1)
            def exponentials(it, u):
                b = u % 2
                act.wait_ge(maxed, it * per + (u + 1))
                for c in range(2):
                    nc.scalar.activation(e[:, b, c, :], s[:, b, c, :], ACT.Exp, bias=neg_max[:, b, c:c + 1],
                                         accum_out=z[:, b, c:c + 1]).then_inc(exped, 1)

            def steps(it, first, end, units):
                for u in range(first, end):
                    for lag, part in ((2, transposed), (3, output), (0, exponentials)):
                        if 0 <= u - lag < units:
                            part(it, u - lag)

            steps(0, 0, 3, per)
            with act.Fori(0, rounds - 1) as it:
                steps(it, 3, per + 3, 2 * per)
            steps(rounds - 1, 3, per + 3, per)

        @block.vector
        def _(dve):
            link = Chain(dve, chain_s)
            for h in range(HEADS):
                link(nc.vector.memset(slope[:, h:h + 1], -(2.0 ** (-8.0 * (h + 1) / HEADS))))
            dve.wait_ge(dist_made, 2)

            def mix(it, u):
                b = u % 2
                dve.wait_ge(exped, it * (2 * per) + (2 * u + 2))
                link(nc.vector.reciprocal(z[:, b, :], z[:, b, :]))
                link(nc.vector.tensor_tensor(z[:, b, 1:2], z[:, b, 1:2], m.neg_lam[:], ALU.mult))
                dve.wait_ge(turned_out, it * per + (u + 1))
                link(nc.vector.tensor_scalar(a[:, b, :], e[:, b, 1, :], z[:, b, 1:2], None, ALU.mult))
                nc.vector.scalar_tensor_tensor(out=a[:, b, :], in0=e[:, b, 0, :], scalar=z[:, b, 0:1],
                                               in1=a[:, b, :], op0=ALU.mult, op1=ALU.add).then_inc(mixed, 1)
                dve.wait_ge(mixed, it * per + (u + 1))

            def biased_scores(it, u):
                j, qt = divmod(u, TT)
                b = u % 2
                for c in range(2):
                    dve.wait_ge(scored, it * (2 * per) + (2 * u + c + 1))
                    nc.vector.scalar_tensor_tensor(out=s[:, b, c, :], in0=dist[:, qt, :],
                                                   scalar=slope[:, bass.ds(it * 2 + j, 1)],
                                                   in1=m.ps[:, 4 * b + c, :], op0=ALU.mult, op1=ALU.add
                                                   ).then_inc(biased, 1)
                dve.wait_ge(biased, it * (2 * per) + (2 * u + 6))
                nc.vector.tensor_reduce(neg_max[:, b, :], s[:, b, :, :], AX.X, ALU.max, negate=True
                                        ).then_inc(maxed, 1)

            def steps(it, first, end, units):
                for u in range(first, end):
                    if u < units:
                        biased_scores(it, u)
                    if u >= 1:
                        mix(it, u - 1)

            steps(0, 0, 1, per)
            with link.loop(rounds - 1, 3 * per) as it:
                steps(it, 1, per + 1, 2 * per)
            steps(rounds - 1, 1, per + 1, per)


def head_norm(nc, m, high, low):
    squared, summed, logged, rooted, chain_s, scaled, highs = (m.sem("hn_" + n) for n in (
        "squared", "summed", "logged", "rooted", "chain", "scaled", "highs"))
    with nc.Block() as block, ExitStack() as mem:
        sb = lambda n, s: mem.enter_context(nc.sbuf_tensor("hn_" + n, s, F32))
        sq, gain, eps = sb("sq", [P, HEADS, T]), sb("gain", [P, 1]), sb("eps", [P, 1])

        @block.scalar
        def _(act):
            for h in range(HEADS):
                nc.scalar.activation(sq[:, h, :], m.oT[:, h, :], ACT.Square).then_inc(squared, 1)
            act.wait_ge(chain_s, 2)
            for h in range(HEADS):
                act.wait_ge(summed, h + 1)
                nc.scalar.activation(sq[:, h, :], m.ps[:, h, :], ACT.Ln, bias=eps[:], scale=1.0 / P).then_inc(logged, 1)
            for h in range(HEADS):
                act.wait_ge(logged, h + 1)
                nc.scalar.activation(sq[:, h, :], sq[:, h, :], ACT.Exp, scale=-0.5).then_inc(rooted, 1)
            for h in range(HEADS):
                act.wait_ge(scaled, h + 1)
                nc.scalar.copy(high[:, h, :], m.oT[:, h, :]).then_inc(highs, 1)

        @block.tensor
        def _(pe):
            for h in range(HEADS):
                pe.wait_ge(squared, h + 1)
                nc.tensor.matmul(m.ps[:, h, :], m.ones[:], sq[:, h, :], start=True, stop=True).then_inc(summed, 1)

        @block.vector
        def _(dve):
            link = Chain(dve, chain_s)
            link(nc.vector.tensor_scalar(gain[:], m.v("subln"), 1.0 - LAM_INIT, None, ALU.mult))
            link(nc.vector.memset(eps[:], EPS))
            for h in range(HEADS):
                dve.wait_ge(rooted, h + 1)
                nc.vector.scalar_tensor_tensor(out=m.oT[:, h, :], in0=m.oT[:, h, :], scalar=gain[:],
                                               in1=sq[:, h, :], op0=ALU.mult, op1=ALU.mult).then_inc(scaled, 1)
            for h in range(HEADS):
                dve.wait_ge(highs, h + 1)
                nc.vector.tensor_tensor(low[:, h, :], m.oT[:, h, :], high[:, h, :].bitcast(F32), ALU.subtract)


def add_projection(nc, m, high, low):
    bank_free = m.sem("ap_bank_free")
    with nc.Block() as block:
        @block.sync
        def _(sp):
            m.stream.loads(sp, "attn_out")

        @block.tensor
        def _(pe):
            project(nc, m, pe, "attn_out", high, low, bank_free)

        @block.scalar
        def _(act):
            for n in range(KT):
                m.stream.done(act, "attn_out", n)
                m.stream.high(act, "attn_out", n)

        @block.vector
        def _(dve):
            for n in range(KT):
                m.stream.done(dve, "attn_out", n)
                nc.vector.scalar_tensor_tensor(out=m.xT[:, n, :], in0=m.ps[:, n, :],
                                               scalar=m.mod[:, 2 * KT + n:2 * KT + n + 1], in1=m.xT[:, n, :],
                                               op0=ALU.mult, op1=ALU.add).then_inc(bank_free, 1)
                m.stream.low(dve, "attn_out", n)


def first_of_equals(nc, link, out, eq, seen, width):
    link(nc.vector.memset(seen[:, :, 0:1], 0.0))
    for g in range(1, width):
        link(nc.vector.tensor_tensor(seen[:, :, g:g + 1], seen[:, :, g - 1:g], eq[:, :, g - 1:g], ALU.add))
    link(nc.vector.scalar_tensor_tensor(out=out, in0=seen[:], scalar=0.5, in1=eq, op0=ALU.is_lt, op1=ALU.mult))


def router(nc, m, high, low, gate_bc):
    G, E = EXPERT_GROUPS, EXPERTS // EXPERT_GROUPS
    logits_done, exps, chain_s, turned, gates_up, spread, spread_read = (m.sem("ro_" + n) for n in (
        "logits_done", "exps", "chain", "turned", "gates_up", "spread", "spread_read"))
    with nc.Block() as block, ExitStack() as mem:
        sb = lambda n, s: mem.enter_context(nc.sbuf_tensor("ro_" + n, s, F32))
        lg = sb("lg", [P, TT, G + EXPERTS])
        top, second, diff, ge, gs, w1 = (sb(n, [P, TT, 1]) for n in ("top", "second", "diff", "ge", "gs", "w1"))
        gx = sb("gx", [P, TT, G])
        eq, seen, oh_g, oh_1, oh_2, sel, ew = (sb(n, [P, TT, G]) for n in ("eq", "seen", "ohg", "oh1", "oh2", "sel", "ew"))
        prod = sb("prod", [P, TT, G, E])
        gates = sb("gates", [P, TT, G, E])
        gatesT = sb("gatesT", [EXPERTS, T])

        @block.tensor
        def _(pe):
            for tt in range(TT):
                for c in range(KT):
                    last = times(nc, m.ps[:, tt, 0:G + EXPERTS], [x[:, c, tt * P:(tt + 1) * P] for x in (high, low)],
                                 [m.router_h[:, c, :], m.router_l[:, c, :]], start=c == 0, stop=c == KT - 1)
                last.then_inc(logits_done, 1)
            pe.wait_ge(gates_up, 1)
            for tt in range(TT):
                nc.tensor.transpose(m.ps[0:EXPERTS, 4, tt * P:(tt + 1) * P],
                                    gates[:, tt, :, :].rearrange("p g e -> p (g e)"), m.ident[:]).then_inc(turned, 1)
            pe.wait_ge(gates_up, 2)
            for x in range(EXPERTS):
                if x >= 8:
                    pe.wait_ge(spread_read, x - 7)
                nc.tensor.matmul(m.ps[:, x % 8, :], m.ident[0:EXPERTS, x:x + 1].to_broadcast([EXPERTS, P]),
                                 gatesT[:], start=True, stop=True).then_inc(spread, 1)

        @block.scalar
        def _(act):
            act.wait_ge(exps, 1)
            nc.scalar.activation(gx[:], gx[:], ACT.Exp).then_inc(exps, 1)
            act.wait_ge(exps, 3)
            nc.scalar.activation(ge[:], diff[:], ACT.Exp).then_inc(exps, 1)
            for x in range(EXPERTS):
                act.wait_ge(spread, x + 1)
                nc.scalar.copy(gate_bc[:, x, :], m.ps[:, x % 8, :]).then_inc(spread_read, 1)

        @block.vector
        def _(dve):
            link = Chain(dve, chain_s)
            bc = lambda t, n: t[:].to_broadcast([P, TT, n])
            for tt in range(TT):
                dve.wait_ge(logits_done, tt + 1)
                link(nc.vector.tensor_tensor(lg[:, tt, :], m.ps[:, tt, 0:G + EXPERTS], m.router_b[:], ALU.add))
            link(nc.vector.tensor_reduce(top[:], lg[:, :, 0:G], AX.X, ALU.max))
            nc.vector.tensor_tensor(gx[:], lg[:, :, 0:G], bc(top, G), ALU.subtract).then_inc(exps, 1)
            link(nc.vector.tensor_tensor(eq[:], lg[:, :, 0:G], bc(top, G), ALU.is_equal))
            first_of_equals(nc, link, oh_g[:], eq[:], seen, G)
            dve.wait_ge(exps, 2)
            link(nc.vector.tensor_reduce(gs[:], gx[:], AX.X, ALU.add))
            link(nc.vector.reciprocal(gs[:], gs[:]))
            for g in range(G):
                link(nc.vector.tensor_tensor(prod[:, :, g, :], lg[:, :, G + g * E:G + (g + 1) * E],
                                             oh_g[:, :, g:g + 1].to_broadcast([P, TT, E]), ALU.mult))
            link(nc.vector.tensor_reduce(sel[:], prod[:].rearrange("p t g e -> p t e g"), AX.X, ALU.add))
            link(nc.vector.tensor_reduce(top[:], sel[:], AX.X, ALU.max))
            link(nc.vector.tensor_tensor(eq[:], sel[:], bc(top, E), ALU.is_equal))
            first_of_equals(nc, link, oh_1[:], eq[:], seen, E)
            link(nc.vector.scalar_tensor_tensor(out=ew[:], in0=oh_1[:], scalar=NEG, in1=sel[:], op0=ALU.mult, op1=ALU.add))
            link(nc.vector.tensor_reduce(second[:], ew[:], AX.X, ALU.max))
            link(nc.vector.tensor_tensor(eq[:], ew[:], bc(second, E), ALU.is_equal))
            first_of_equals(nc, link, oh_2[:], eq[:], seen, E)
            nc.vector.tensor_tensor(diff[:], second[:], top[:], ALU.subtract).then_inc(exps, 1)
            dve.wait_ge(exps, 4)
            link(nc.vector.tensor_scalar(w1[:], ge[:], 1.0, None, ALU.add))
            link(nc.vector.reciprocal(w1[:], w1[:]))
            link(nc.vector.tensor_tensor(w1[:], w1[:], gs[:], ALU.mult))
            link(nc.vector.tensor_tensor(ge[:], ge[:], w1[:], ALU.mult))
            link(nc.vector.tensor_tensor(oh_1[:], oh_1[:], bc(w1, E), ALU.mult))
            link(nc.vector.tensor_tensor(oh_2[:], oh_2[:], bc(ge, E), ALU.mult))
            link(nc.vector.tensor_tensor(ew[:], oh_1[:], oh_2[:], ALU.add))
            for g in range(G):
                ins = nc.vector.tensor_tensor(gates[:, :, g, :], ew[:], oh_g[:, :, g:g + 1].to_broadcast([P, TT, E]),
                                              ALU.mult)
                if g < G - 1:
                    link(ins)
            ins.then_inc(gates_up, 1)
            dve.wait_ge(turned, TT)
            nc.vector.tensor_copy(gatesT[:], m.ps[0:EXPERTS, 4, :]).then_inc(gates_up, 1)


def experts(nc, m, high, low, gate_bc):
    (gates_read, ups_read, ys_read, hid_made, hid_high, hid_low, ending, zeroed) = (m.sem("ex_" + n) for n in (
        "gates_read", "ups_read", "ys_read", "hid_made", "hid_high", "hid_low", "ending", "zeroed"))
    F = 4
    with nc.Block() as block, ExitStack() as mem:
        sb = lambda n, s, dt=F32: mem.enter_context(nc.sbuf_tensor("ex_" + n, s, dt))
        acc = sb("acc", [P, KT, T])
        hh, hl = sb("hh", [P, F, T], F32R), sb("hl", [P, F, T], F32R)
        sg, m1, hid = sb("sg", [P, 2, T]), sb("m1", [P, 2, T]), sb("hid", [P, 2, T])

        @block.sync
        def _(sp):
            m.stream.loads(sp, "experts")

        @block.tensor
        def _(pe):
            pe.sem_inc(ys_read, 8)
            pe.sem_inc(ups_read, 2)
            with pe.Fori(0, EXPERTS) as it:
                for k in range(2 * F):
                    w = [x.rearrange("p (c f) -> p c f", c=KT) for x in m.stream.weights(pe, "experts", k, it)]
                    pe.wait_ge(ys_read, it * 8 + (k + 1))
                    for c in range(KT):
                        last = times(nc, m.ps[:, k, :], [x[:, c, :] for x in w], [high[:, c, :], low[:, c, :]],
                                     start=c == 0, stop=c == KT - 1)
                    last.then_inc(m.chunk_done, 1)
                for k in range(F):
                    w = [x.rearrange("p (c f) -> p c f", c=F) for x in m.stream.weights(pe, "experts", 8 + k, it)]
                    for c, part in [(c, part) for c in range(F) for part in range(2)]:
                        if (k, part) == (0, 0):
                            pe.wait_ge(hid_low, it * F + (c + 1))
                        last = times(nc, m.ps[:, 2 * k + part, :], [x[:, c, part * P:(part + 1) * P] for x in w],
                                     [hh[:, c, :], hl[:, c, :]], start=c == 0, stop=c == F - 1)
                    last.then_inc(m.chunk_done, 1)

        @block.scalar
        def _(act):
            with act.Fori(0, EXPERTS) as it:
                for f in range(F):
                    m.stream.done(act, "experts", 2 * f, it)
                    act.wait_ge(ups_read, it * F + (f + 1))
                    nc.scalar.activation(sg[:, f % 2, :], m.ps[:, 2 * f, :], ACT.Silu).then_inc(gates_read, 1)
                    m.stream.high(act, "experts", 2 * f, it)
                    act.wait_ge(hid_made, it * F + (f + 1))
                    nc.scalar.copy(hh[:, f, :], hid[:, f % 2, :]).then_inc(hid_high, 1)
                    m.stream.high(act, "experts", 2 * f + 1, it)
                for k in range(8, 12):
                    m.stream.done(act, "experts", k, it)
                    m.stream.high(act, "experts", k, it)

        @block.vector
        def _(dve):
            nc.vector.memset(acc[:], 0.0).then_inc(zeroed, 1)
            dve.wait_ge(zeroed, 1)
            with dve.Fori(0, EXPERTS) as it:
                for f in range(F):
                    m.stream.done(dve, "experts", 2 * f, it)
                    m.stream.low(dve, "experts", 2 * f, it)
                    m.stream.done(dve, "experts", 2 * f + 1, it)
                    dve.wait_ge(gates_read, it * F + (f + 1))
                    nc.vector.tensor_tensor(m1[:, f % 2, :], sg[:, f % 2, :], m.ps[:, 2 * f + 1, :], ALU.mult
                                            ).then_inc(ups_read, 1)
                    dve.wait_ge(ups_read, it * F + (f + 3))
                    nc.vector.tensor_tensor(hid[:, f % 2, :], m1[:, f % 2, :],
                                            gate_bc[:, bass.ds(it, 1), :].rearrange("p a t -> p (a t)"),
                                            ALU.mult).then_inc(hid_made, 1)
                    dve.wait_ge(hid_high, it * F + (f + 1))
                    nc.vector.tensor_tensor(hl[:, f, :], hid[:, f % 2, :], hh[:, f, :].bitcast(F32), ALU.subtract
                                            ).then_inc(hid_low, 1)
                    m.stream.low(dve, "experts", 2 * f + 1, it)
                dve.wait_ge(ys_read, it * 8 + 8)
                for k in range(F):
                    m.stream.done(dve, "experts", 8 + k, it)
                    for n in (2 * k, 2 * k + 1):
                        nc.vector.tensor_tensor(acc[:, n, :], acc[:, n, :], m.ps[:, n, :], ALU.add
                                                ).then_inc(ys_read, 1)
                    m.stream.low(dve, "experts", 8 + k, it)
            dve.wait_ge(ys_read, 8 + 8 * EXPERTS)
            for n in range(KT):
                nc.vector.scalar_tensor_tensor(out=m.xT[:, n, :], in0=acc[:, n, :],
                                               scalar=m.mod[:, 5 * KT + n:5 * KT + n + 1], in1=m.xT[:, n, :],
                                               op0=ALU.mult, op1=ALU.add).then_inc(ending, 1)


def second_projection(nc, m, high, low, fq, fk, fv, cols, negc, cq):
    bank_free, f_done, f_steps, f_chain, c_ready, c_turned, spread, spread_read, c_read = (m.sem("sp_" + n) for n in (
        "bank_free", "f_done", "f_steps", "f_chain", "c_ready", "c_turned", "spread", "spread_read", "c_read"))
    f_loaded = m.sem("sp_f_loaded")
    with nc.Block() as block, ExitStack() as mem:
        sb = lambda n, s: mem.enter_context(nc.sbuf_tensor("sp_" + n, s, F32))
        f_w, f_b = sb("f_w", [P, KT, HEADS]), sb("f_b", [HEADS, 1])
        fx, fa, fc, f1 = (sb(n, [HEADS, T]) for n in ("fx", "fa", "fc", "f1"))

        @block.sync
        def _(sp):
            sp.dma_start(f_w[:], m.i["f_w"].rearrange("(k p) f -> p k f", p=P)).then_inc(f_loaded, 16)
            sp.dma_start(f_b[:], m.i["f_b"]).then_inc(f_loaded, 16)
            m.stream.loads(sp, "fox_qk", "fox_v", "rwkv_in")

        @block.tensor
        def _(pe):
            pe.wait_ge(f_loaded, 32)
            for c in range(KT):
                last = nc.tensor.matmul(m.ps[0:HEADS, 7, :], f_w[:, c, :], m.xT[:, c, :], start=c == 0, stop=c == KT - 1)
            last.then_inc(f_done, 1)
            project(nc, m, pe, "fox_qk", high, low, bank_free, banks=7)
            token_major(nc, m, pe, "fox_v", high, low, bank_free, 2, 8, banks=7)
            project(nc, m, pe, "rwkv_in", high, low, bank_free, chunks=14, n0=16, banks=7)
            pe.wait_ge(c_ready, 1)
            pe.wait_ge(bank_free, 7 + 30)
            for tt in range(TT):
                nc.tensor.transpose(m.ps[:, 7, tt * HEADS:(tt + 1) * HEADS], fc[:, tt * P:(tt + 1) * P],
                                    m.ident[0:HEADS, 0:HEADS]).then_inc(c_turned, 1)
            pe.wait_ge(c_ready, 2)
            for h in range(HEADS):
                if h >= 6:
                    pe.wait_ge(spread_read, h - 5)
                nc.tensor.matmul(m.ps[:, h % 6, :], m.ident[0:HEADS, h:h + 1].to_broadcast([HEADS, P]), fx[:],
                                 start=True, stop=True).then_inc(spread, 1)

        @block.scalar
        def _(act):
            act.wait_ge(f_chain, 3)
            nc.scalar.activation(fa[:], fx[:], ACT.Abs).then_inc(f_steps, 1)
            act.wait_ge(f_steps, 1)
            nc.scalar.activation(fc[:], fa[:], ACT.Exp, scale=-1.0).then_inc(f_steps, 1)
            act.wait_ge(f_steps, 2)
            nc.scalar.activation(fa[:], fc[:], ACT.Ln, bias=1.0).then_inc(f_steps, 1)
            for n in range(8 + 4 + 14):
                m.stream.done(act, "fox_qk", n)
                bank = m.ps[:, (n if n < 8 else n + 4) % 7, :]
                if n < 4:
                    nc.scalar.mul(fq[:, n, :], bank, DH ** -0.5).then_inc(bank_free, 1)
                elif n < 8:
                    nc.scalar.copy(fk[:, n - 4, :], bank).then_inc(bank_free, 1)
                elif n < 12:
                    read_token_major(nc, bank_free, m.ps, fv, n - 8, 8, banks=7)
                else:
                    nc.scalar.copy(cols[:, n - 12, 1:T + 1], bank).then_inc(bank_free, 1)
                m.stream.high(act, "fox_qk", n)
            for h in range(HEADS):
                act.wait_ge(spread, h + 1)
                nc.scalar.copy(negc[:, h, :], m.ps[:, h % 6, :]).then_inc(spread_read, 1)

        @block.vector
        def _(dve):
            link = Chain(dve, f_chain)
            link(nc.vector.memset(cols[:, :, 0:1], 0.0))
            link(nc.vector.memset(f1[:], 1.0))
            dve.wait_ge(f_done, 1)
            dve.wait_ge(f_loaded, 32)
            link(nc.vector.tensor_scalar(fx[:], m.ps[0:HEADS, 7, :], f_b[:], None, ALU.add))
            dve.wait_ge(f_steps, 3)
            link(nc.vector.scalar_tensor_tensor(out=fx[:], in0=fx[:], scalar=0.0, in1=fa[:], op0=ALU.min,
                                                op1=ALU.subtract))
            nc.vector.tensor_tensor_scan(fc[:], f1[:], fx[:], 0.0, ALU.mult, ALU.add).then_inc(c_ready, 1)
            dve.wait_ge(c_ready, 1)
            nc.vector.tensor_scalar(fx[:], fc[:], -1.0, None, ALU.mult).then_inc(c_ready, 1)
            for n in range(8 + 4 + 14):
                m.stream.done(dve, "fox_qk", n)
                m.stream.low(dve, "fox_qk", n)
            dve.wait_ge(c_turned, TT)
            nc.vector.tensor_copy(cq[:], m.ps[:, 7, 0:TT * HEADS].rearrange("p (t h) -> p t h", h=HEADS)
                                  ).then_inc(c_read, 1)


def fox_attention(nc, m, fq, fk, fv, negc, cq, yf):
    (qk_staged, v_staged, scored, biased, masked, maxed, exped, mixed, turned, turned_out, unit_done, o_out,
     mask_made, chain_s) = (m.sem("fa_" + n) for n in (
         "qk_staged", "v_staged", "scored", "biased", "masked", "maxed", "exped", "mixed", "turned", "turned_out",
         "unit_done", "o_out", "mask_made", "chain"))
    tiles, per = 2, 2 * 2 * TT
    units = [(j, c, qt) for j in range(tiles) for c in range(2) for qt in range(TT)]
    with nc.Block() as block, ExitStack() as mem:
        sb = lambda n, s: mem.enter_context(nc.sbuf_tensor("fa_" + n, s, F32))
        causal = sb("causal", [P, P])
        q_st, k_st, v_st = sb("q_st", [P, 2, T]), sb("k_st", [P, 2, T]), sb("v_st", [P, 2, TT, P])
        s, e, a = sb("s", [P, 2, T]), sb("e", [P, 2, T]), sb("a", [P, 2, T])
        neg_max, z = sb("neg_max", [P, 2]), sb("z", [P, 2])
        aT = sb("aT", [P, 2, TT, P])

        @block.gpsimd
        def _(pool):
            nc.gpsimd.memset(causal[:], 0.0).then_inc(mask_made, 1)
            pool.wait_ge(mask_made, 1)
            nc.gpsimd.affine_select(out=causal[:], in_=causal[:], compare_op=ALU.is_ge, fill=NEG, base=0,
                                    pattern=[[-1, P]], channel_multiplier=1).then_inc(mask_made, 1)
            with pool.Fori(0, 2) as it:
                for j in range(tiles):
                    pool.wait_ge(unit_done, it * per + 8 * (j + 1))
                    for staged, whole in ((q_st, fq), (k_st, fk)):
                        nc.gpsimd.tensor_copy(staged[:, j, :], whole[:, bass.ds(it * 2 + j, 1), :].rearrange(
                            "p a t -> p (a t)")).then_inc(qk_staged, 1)
                    nc.gpsimd.tensor_copy(v_st[:, j, :, :], fv[:, :, bass.ds((it * 2 + j) * P, P)]
                                          ).then_inc(v_staged, 1)

        @block.tensor
        def _(pe):
            pe.sem_inc(unit_done, per)
            pe.sem_inc(biased, 2)
            pe.sem_inc(turned_out, 2)
            pe.sem_inc(o_out, 2)

            def turn(it, u):
                j, c, qt = units[u]
                b = u % 2
                pe.wait_ge(mixed, it * per + (u + 1))
                pe.wait_ge(turned_out, it * per + (u + 1))
                for kt in range(qt + 1):
                    last = nc.tensor.transpose(m.ps[:, 3 * b + 1, kt * P:(kt + 1) * P],
                                               a[:, b, kt * P:(kt + 1) * P], m.ident[:])
                last.then_inc(turned, 1)

            def values(it, u):
                j, c, qt = units[u]
                b = u % 2
                if (c, qt) == (0, 0):
                    pe.wait_ge(v_staged, it * 2 + (j + 1))
                pe.wait_ge(turned_out, it * per + (u + 3))
                pe.wait_ge(o_out, it * per + (u + 1))
                for kt in range(qt + 1):
                    last = nc.tensor.matmul(m.ps[c * DH:(c + 1) * DH, 3 * b + 2, 0:P],
                                            v_st[:, j, kt, c * DH:(c + 1) * DH], aT[:, b, kt, :],
                                            start=kt == 0, stop=kt == qt)
                last.then_inc(unit_done, 1)

            with pe.Fori(0, 2) as it:
                for u, (j, c, qt) in enumerate(units):
                    if (c, qt) == (0, 0):
                        pe.wait_ge(qk_staged, it * 4 + 2 * (j + 1))
                    pe.wait_ge(biased, it * per + (u + 1))
                    rows = slice(c * DH, (c + 1) * DH)
                    nc.tensor.matmul(m.ps[:, 3 * (u % 2), 0:(qt + 1) * P], q_st[rows, j, qt * P:(qt + 1) * P],
                                     k_st[rows, j, 0:(qt + 1) * P], start=True, stop=True).then_inc(scored, 1)
                    if u >= 2:
                        turn(it, u - 2)
                    if u >= 3:
                        values(it, u - 3)
                turn(it, per - 2)
                values(it, per - 3)
                turn(it, per - 1)
                values(it, per - 2)
                values(it, per - 1)

        @block.scalar
        def _(act):
            def transposed(it, u):
                j, c, qt = units[u]
                b, n = u % 2, (qt + 1) * P
                act.wait_ge(turned, it * per + (u + 1))
                nc.scalar.copy(aT[:, b, 0:qt + 1, :], m.ps[:, 3 * b + 1, 0:n].rearrange("p (k q) -> p k q", q=P)
                               ).then_inc(turned_out, 1)

            def output(it, u):
                j, c, qt = units[u]
                b = u % 2
                act.wait_ge(unit_done, it * per + (per + u + 1))
                nc.scalar.copy(yf[c * DH:(c + 1) * DH, bass.ds(it * 2 + j, 1), qt * P:(qt + 1) * P],
                               m.ps[c * DH:(c + 1) * DH, 3 * b + 2, 0:P].rearrange("p (a q) -> p a q", a=1)
                               ).then_inc(o_out, 1)

            with act.Fori(0, 2) as it:
                for u, (j, c, qt) in enumerate(units):
                    b, n = u % 2, (qt + 1) * P
                    if u >= 2:
                        transposed(it, u - 2)
                    if u >= 3:
                        output(it, u - 3)
                    act.wait_ge(maxed, it * per + (u + 1))
                    nc.scalar.activation(e[:, b, 0:n], s[:, b, 0:n], ACT.Exp, bias=neg_max[:, b:b + 1],
                                         accum_out=z[:, b:b + 1]).then_inc(exped, 1)
                transposed(it, per - 2)
                output(it, per - 3)
                transposed(it, per - 1)
                output(it, per - 2)
                output(it, per - 1)

        @block.vector
        def _(dve):
            dve.wait_ge(mask_made, 2)
            link = Chain(dve, chain_s)

            def divide(it, u):
                b, n = u % 2, (units[u][2] + 1) * P
                dve.wait_ge(exped, it * per + (u + 1))
                link(nc.vector.reciprocal(z[:, b:b + 1], z[:, b:b + 1]))
                dve.wait_ge(turned_out, it * per + (u + 1))
                nc.vector.tensor_scalar(a[:, b, 0:n], e[:, b, 0:n], z[:, b:b + 1], None, ALU.mult).then_inc(mixed, 1)
                dve.wait_ge(mixed, it * per + (u + 1))

            with link.loop(2, 2 * per) as it:
                for u, (j, c, qt) in enumerate(units):
                    b, n = u % 2, (qt + 1) * P
                    h = it * 4 + (2 * j + c)
                    dve.wait_ge(scored, it * per + (u + 1))
                    nc.vector.scalar_tensor_tensor(out=s[:, b, 0:n],
                                                   in0=negc[:, bass.ds(h, 1), 0:n].rearrange("p a t -> p (a t)"),
                                                   scalar=cq[:, qt, bass.ds(h, 1)], in1=m.ps[:, 3 * b, 0:n],
                                                   op0=ALU.add, op1=ALU.add).then_inc(biased, 1)
                    dve.wait_ge(biased, it * per + (u + 3))
                    link(nc.vector.tensor_tensor(s[:, b, n - P:n], s[:, b, n - P:n], causal[:], ALU.add))
                    nc.vector.tensor_reduce(neg_max[:, b:b + 1], s[:, b, 0:n], AX.X, ALU.max, negate=True
                                            ).then_inc(maxed, 1)
                    if u >= 1:
                        divide(it, u - 1)
                divide(it, per - 1)


LEVELS = 5


def allocate_masks(sb):
    masks = Shared()
    masks.part = sb("mask_part", [P, 4, P])
    masks.low = sb("mask_low", [P, P])
    masks.pair, masks.pairT = sb("mask_pair", [P, P]), sb("mask_pairT", [P, P])
    masks.lev = sb("mask_lev", [P, LEVELS, P])
    return masks


def make_masks(nc, m, pool, done, masks):
    link = Chain(pool, done)
    def triangle(out, strict, upper):
        link(nc.gpsimd.tensor_copy(out, m.halves[:]))
        sign = -1 if upper else 1
        link(nc.gpsimd.affine_select(out=out, in_=out, compare_op=ALU.is_ge, fill=0.0,
                                     base=-1 if strict else 0, pattern=[[-sign, P]], channel_multiplier=sign))
    for at, strict in ((0, True), (1, False), (2, True), (3, False)):
        triangle(masks.part[:, at, :], strict, True)
    triangle(masks.low[:], True, False)
    link(nc.gpsimd.memset(masks.lev[:], 1.0))
    for l in range(LEVELS):
        size = 2 << l
        v = masks.lev[:, l, :].rearrange("p (b h c) -> p b h c", h=2, c=size)
        link(nc.gpsimd.memset(v[:, :, 0, :], 0.0))
        link(nc.gpsimd.affine_select(out=v[:, :, 1, :], in_=v[:, :, 1, :], compare_op=ALU.is_ge, fill=0.0,
                                     base=0, pattern=[[-2 * size, P // (2 * size)], [0, size]],
                                     channel_multiplier=1))
        link(nc.gpsimd.affine_select(out=v[:, :, 1, :], in_=v[:, :, 1, :], compare_op=ALU.is_ge, fill=0.0,
                                     base=size - 1, pattern=[[2 * size, P // (2 * size)], [0, size]],
                                     channel_multiplier=-1))
    link(nc.gpsimd.memset(masks.pair[:], 0.0))
    v = masks.pair[:].rearrange("p (b h) -> p b h", h=2)
    link(nc.gpsimd.affine_select(out=v[:, :, 1:2], in_=v[:, :, 1:2], compare_op=ALU.not_equal, fill=1.0,
                                 base=0, pattern=[[-2, P // 2], [0, 1]], channel_multiplier=1))
    link(nc.gpsimd.memset(masks.pairT[:], 0.0))
    v = masks.pairT[:].rearrange("p (b h) -> p b h", h=2)
    link(nc.gpsimd.affine_select(out=v[:, :, 0:1], in_=v[:, :, 0:1], compare_op=ALU.not_equal, fill=1.0,
                                 base=-1, pattern=[[-2, P // 2], [0, 1]], channel_multiplier=1))


def time_mix_inputs(nc, m, cols, w, masks):
    masks_made = m.sem("ti_masks_made")
    (loaded, acts, made, l_done, l_free, g_read, sum_done, rooted, centred, exps) = (m.sem("ti_" + n) for n in (
        "loaded", "acts", "made", "l_done", "l_free", "g_read", "sum_done", "rooted", "centred", "exps"))
    F = 4
    with nc.Block() as block, ExitStack() as mem:
        sb = lambda n, s: mem.enter_context(nc.sbuf_tensor("ti_" + n, s, F32))
        w2a2, g2 = sb("w2a2", [P, F * P]), sb("g2", [P, F * P])
        rw = cols[:, :, 1:T + 1]
        diff = sb("diff", [P, T])
        ta, tg = sb("ta", [P, T]), sb("tg", [P, T])
        lw, L, a, t1 = (sb(n, [P, F, T]) for n in ("lw", "L", "a", "t1"))
        ep, en, ex = a, t1, lw
        reset = sb("reset", [P, T])
        mid, omka = sb("mid", [P, F, NCHUNK]), sb("omka", [P, F])

        @block.gpsimd
        def _(pool):
            make_masks(nc, m, pool, masks_made, masks)

        @block.sync
        def _(sp):
            sp.dma_start(w2a2[:], m.i["w2a2"]).then_inc(loaded, 16)
            sp.dma_start(g2[:], m.i["g2"]).then_inc(loaded, 16)

        @block.scalar
        def _(act):
            act.wait_ge(made, 4)
            nc.scalar.activation(ta[0:DH, :], rw[0:DH, 12, :], ACT.Tanh).then_inc(acts, 1)
            nc.scalar.copy(ta[DH:P, :], rw[DH:P, 12, :]).then_inc(acts, 1)
            nc.scalar.activation(tg[:], rw[:, 13, :], ACT.Sigmoid).then_inc(acts, 1)
            for f in range(F):
                act.wait_ge(l_done, f + 1)
                nc.scalar.activation(lw[:, f, :], m.ps[:, f, :], ACT.Sigmoid, bias=m.v("w0")[:, f:f + 1]
                                     ).then_inc(l_free, 1)
            for f in range(F):
                act.wait_ge(l_done, F + f + 1)
                nc.scalar.activation(a[:, f, :], m.ps[:, 4 + f, :], ACT.Sigmoid, bias=m.v("a0")[:, f:f + 1]
                                     ).then_inc(l_free, 1)
            for f in range(F):
                act.wait_ge(l_done, 2 * F + f + 1)
                nc.scalar.copy(w.g[:, f, :], m.ps[:, f, :]).then_inc(g_read, 1)
            act.wait_ge(rooted, 1)
            inverse_root(nc, act, t1[:], rooted, 1)
            act.wait_ge(centred, 1)
            nc.scalar.activation(ep[:], L[:], ACT.Exp).then_inc(exps, 1)
            act.wait_ge(sum_done, 4)
            nc.scalar.activation(en[:], L[:], ACT.Exp, scale=-1.0).then_inc(exps, 1)
            act.wait_ge(centred, 3)
            nc.scalar.activation(ex[:], lw[:], ACT.Exp).then_inc(exps, 1)
            nc.scalar.activation(w.carry[:], w.carry[:], ACT.Exp).then_inc(exps, 1)

        @block.tensor
        def _(pe):
            pe.wait_ge(loaded, 32)
            pe.wait_ge(acts, 3)
            for f in range(F):
                nc.tensor.matmul(m.ps[:, f, :], w2a2[0:DH, f * P:(f + 1) * P], ta[0:DH, :], start=True, stop=True
                                 ).then_inc(l_done, 1)
            for f in range(F):
                nc.tensor.matmul(m.ps[:, 4 + f, :], w2a2[DH:P, f * P:(f + 1) * P], ta[DH:P, :], start=True, stop=True
                                 ).then_inc(l_done, 1)
            for f in range(F):
                pe.wait_ge(l_free, f + 1)
                nc.tensor.matmul(m.ps[:, f, :], g2[:, f * P:(f + 1) * P], tg[:], start=True, stop=True
                                 ).then_inc(l_done, 1)
            pe.wait_ge(l_free, 2 * F)
            pe.wait_ge(sum_done, 1)
            for f in range(F):
                last = nc.tensor.matmul(m.ps[:, 4 + f, :], m.halves[:], t1[:, f, :], start=True, stop=True)
            last.then_inc(sum_done, 1)
            pe.wait_ge(g_read, F)
            pe.wait_ge(sum_done, 3)
            for f in range(F):
                last = nc.tensor.matmul(m.ps[:, f, :], m.halves[:], t1[:, f, :], start=True, stop=True)
            last.then_inc(sum_done, 1)

        @block.vector
        def _(dve):
            link = Chain(dve, made)

            def per_tile(out, in0, name, in1=None, op0=ALU.mult, op1=ALU.mult):
                for f in range(F):
                    if in1 is None:
                        link(nc.vector.tensor_scalar(out[:, f, :], in0[:, f, :], m.v(name)[:, f:f + 1], None, op0))
                    else:
                        link(nc.vector.scalar_tensor_tensor(out=out[:, f, :], in0=in0[:, f, :],
                                                            scalar=m.v(name)[:, f:f + 1], in1=in1[:, f, :],
                                                            op0=op0, op1=op1))
            for n in [12, 13] + list(range(12)):
                link(nc.vector.tensor_tensor(diff[:], cols[:, n, 0:T], rw[:, n, :], ALU.subtract))
                link(nc.vector.scalar_tensor_tensor(out=rw[:, n, :], in0=diff[:], scalar=m.v("mu")[:, n:n + 1],
                                                    in1=rw[:, n, :], op0=ALU.mult, op1=ALU.add))
            k = rw[:, 4:8, :]
            per_tile(w.kk, k, "k_k")
            nc.vector.tensor_tensor(t1[:], w.kk[:], w.kk[:], ALU.mult).then_inc(sum_done, 1)
            dve.wait_ge(sum_done, 2)
            nc.vector.tensor_scalar(t1[:], m.ps[:, 4:8, :], 1e-24, None, ALU.max).then_inc(rooted, 1)
            dve.wait_ge(rooted, 3)
            link(nc.vector.tensor_tensor(w.kk[:], w.kk[:], t1[:], ALU.mult))
            dve.wait_ge(l_free, 2 * F)
            link(nc.vector.tensor_tensor(w.b[:], w.kk[:], a[:], ALU.mult))
            link(nc.vector.tensor_scalar(omka[:], m.v("k_a"), -1.0, 1.0, ALU.mult, ALU.add))
            for f in range(F):
                link(nc.vector.tensor_scalar(t1[:, f, :], a[:, f, :], m.v("k_a")[:, f:f + 1], omka[:, f:f + 1],
                                             ALU.mult, ALU.add))
            link(nc.vector.tensor_tensor(w.k[:], t1[:], k, ALU.mult))
            for f in range(F):
                ins = nc.vector.scalar_tensor_tensor(out=t1[:, f, :], in0=w.r[:, f, :], scalar=m.v("r_k")[:, f:f + 1],
                                                     in1=w.k[:, f, :], op0=ALU.mult, op1=ALU.mult)
                if f < F - 1:
                    link(ins)
            ins.then_inc(sum_done, 1)
            link(nc.vector.tensor_scalar(lw[:], lw[:], -math.exp(-0.5), None, ALU.mult))
            link(nc.vector.memset(reset[:], 1.0))
            link(nc.vector.memset(reset[:].rearrange("p (c t) -> p c t", t=CHUNK)[:, :, 0:1], 0.0))
            for f in range(F):
                link(nc.vector.tensor_tensor_scan(L[:, f, :], reset[:], lw[:, f, :], 0.0, ALU.mult, ALU.add))
            ends = L[:].rearrange("p f (c t) -> p f c t", t=CHUNK)[:, :, :, CHUNK - 1:CHUNK].rearrange(
                "p f c o -> p f (c o)")
            link(nc.vector.tensor_scalar(mid[:], ends, 0.5, None, ALU.mult))
            Lc = L[:].rearrange("p f (c t) -> p (f c) t", t=CHUNK)
            nc.vector.tensor_tensor(Lc, Lc, mid[:].rearrange("p f (c o) -> p (f c) o", o=1).to_broadcast(
                [P, F * NCHUNK, CHUNK]), ALU.subtract).then_inc(centred, 1)
            dve.wait_ge(centred, 1)
            nc.vector.tensor_tensor(lw[:], L[:], lw[:], ALU.subtract).then_inc(centred, 1)
            link(nc.vector.memset(w.carry[:], 0.0))
            nc.vector.tensor_tensor(w.carry[:, :, 0:NCHUNK - 1], mid[:, :, 0:NCHUNK - 1], mid[:, :, 1:NCHUNK],
                                    ALU.add).then_inc(centred, 1)
            dve.wait_ge(sum_done, 4)
            link(nc.vector.tensor_tensor(w.bonus[:], m.ps[:, 0:4, :], w.v[:], ALU.mult))
            dve.wait_ge(exps, 3)
            for x, y in ((w.kk, ex), (w.r, ep), (w.b, en), (w.k, en)):
                link(nc.vector.tensor_tensor(x[:], x[:], y[:], ALU.mult))


def recurrence(nc, m, w, masks, yr):
    names = ("made", "turned", "tm_read", "p1", "p2", "p1_read", "y_done", "y_read", "tu_done", "inv", "mv",
             "mv_read", "w_done", "w_read", "sa_done", "sa_read", "ds_done", "s_next", "yo_done", "yo_read", "slices", "made2", "w_half")
    s_ = {n: m.sem("rc_" + n) for n in names}
    F = 4
    H2 = 4
    with nc.Block() as block, ExitStack() as mem:
        sb = lambda n, s, dt=F32: mem.enter_context(nc.sbuf_tensor("rc_" + n, s, dt))
        part, low, pair, pairT, lev = masks.part, masks.low, masks.pair, masks.pairT, masks.lev
        KR = sb("KR", [P, F, 2, P])
        B, C = sb("B", [P, F, P]), sb("C", [P, F, P])
        Bt, Ct, Vt = (sb(n, [P, T]) for n in ("Bt", "Ct", "Vt"))
        Vs = sb("Vs", [P, F, P])
        A = sb("A", [P, HEADS, 4, P])
        N = sb("N", [P, HEADS, P])
        Ti, U, Y = (sb(n, [P, HEADS, P]) for n in ("Ti", "U", "Y"))
        MV, W, SA = (sb(n, [P, HEADS, DH]) for n in ("MV", "W", "SA"))
        S = sb("S", [P, 3, F, DH])

        def heads_of(h):
            return slice(DH * (h % 2), DH * (h % 2) + DH), h // 2

        @block.tensor
        def _(pe):
            pe.sem_inc(s_["yo_read"], 1)
            with pe.Fori(0, TT) as it:
                pe.wait_ge(s_["yo_read"], it + 1)
                pe.wait_ge(s_["slices"], it * 5 + 5)
                for n, src in enumerate((B, C, Vs)):
                    for f in range(F):
                        last = nc.tensor.transpose(m.ps[:, n, f * P:(f + 1) * P], src[:, f, :], m.ident[:])
                    last.then_inc(s_["turned"], 1)
                for h in range(HEADS):
                    rows, f = heads_of(h)
                    if h >= 2:
                        pe.wait_ge(s_["p1_read"], it * 16 + 2 * (h - 1))
                    elif h == 0:
                        pe.wait_ge(s_["yo_read"], it + 1)
                    nc.tensor.matmul(m.ps[:, 4 + h % 2, 0:2 * P], B[rows, f, :], KR[rows, f, :, :].rearrange("p a t -> p (a t)"),
                                     start=True, stop=True)
                    nc.tensor.matmul(m.ps[:, 4 + h % 2, 2 * P:4 * P], C[rows, f, :], KR[rows, f, :, :].rearrange("p a t -> p (a t)"),
                                     start=True, stop=True).then_inc(s_["p1"], 1)
                    nc.tensor.matmul(m.ps[:, 6 + h % 2, 0:P], KR[rows, f, 0, :], B[rows, f, :],
                                     start=True, stop=True).then_inc(s_["p2"], 1)
                pe.wait_ge(s_["tm_read"], it * 3 + 3)
                pe.wait_ge(s_["p1_read"], it * 16 + 16)
                for h in range(HEADS):
                    last = nc.tensor.matmul(m.ps[:, 3, h * DH:(h + 1) * DH], A[:, h, 2, :], Vt[:, h * DH:(h + 1) * DH],
                                            start=True, stop=True)
                last.then_inc(s_["mv"], 1)
                for l in range(LEVELS):
                    for g in range(2):
                        pe.wait_ge(s_["inv"], it * (2 * LEVELS + 2) + (2 * l + g + 1))
                        for h in range(g * H2, g * H2 + H2):
                            last = nc.tensor.matmul(m.ps[:, g, (h % H2) * P:(h % H2 + 1) * P], N[:, h, :], U[:, h, :],
                                                    start=True, stop=True)
                        last.then_inc(s_["y_done"], 1)
                    for g in range(2):
                        pe.wait_ge(s_["y_read"], it * (2 * LEVELS) + (2 * l + g + 1))
                        if l >= 1:
                            pe.wait_ge(s_["made2"], it * (2 * LEVELS - 2) + (2 * l + g - 1))
                        for h in range(g * H2, g * H2 + H2):
                            at = slice((h % H2) * P, (h % H2 + 1) * P)
                            if l < LEVELS - 1:
                                nc.tensor.matmul(m.ps[:, 4 + g, at], Y[:, h, :], Ti[:, h, :], start=True, stop=True)
                            last = nc.tensor.matmul(m.ps[:, 6 + g, at], Ti[:, h, :], Y[:, h, :], start=True, stop=True)
                        last.then_inc(s_["tu_done"], 1)
                pe.wait_ge(s_["inv"], it * (2 * LEVELS + 2) + (2 * LEVELS + 2))
                pe.wait_ge(s_["mv_read"], it + 1)
                for c in range(2):
                    toks = slice(DH * c, DH * c + DH)
                    settle(m, pe, s_["s_next"], it * 3 + (c + 1))
                    for par in range(2):
                        for h in range(par, HEADS, 2):
                            rows, f = heads_of(h)
                            last = nc.tensor.matmul(m.ps[toks, par, f * DH:(f + 1) * DH], KR[rows, f, 0, toks],
                                                    S[rows, c, f, :], start=True, stop=True)
                    last.then_inc(s_["w_done"], 1)
                    settle(m, pe, s_["w_read"], it * 2 + (c + 1))
                    for h in range(HEADS):
                        last = nc.tensor.matmul(m.ps[toks, 2, h * DH:(h + 1) * DH], U[toks, h, toks], W[toks, h, :],
                                                start=True, stop=True)
                    last.then_inc(s_["sa_done"], 1)
                    settle(m, pe, s_["sa_read"], it * 2 + (c + 1))
                    for h in range(HEADS):
                        rows, f = heads_of(h)
                        out = m.ps[rows, 3, f * DH:(f + 1) * DH]
                        nc.tensor.matmul(out, Ct[toks, h * DH:(h + 1) * DH], Vt[toks, h * DH:(h + 1) * DH],
                                         start=True, stop=False)
                        last = nc.tensor.matmul(out, Bt[toks, h * DH:(h + 1) * DH], SA[toks, h, :],
                                                start=False, stop=True)
                    last.then_inc(s_["ds_done"], 1)
                for h in range(HEADS):
                    rows, f = heads_of(h)
                    out = m.ps[rows, 4, f * P:(f + 1) * P]
                    nc.tensor.matmul(out, SA[:, h, :], A[:, h, 1, :], start=True, stop=False)
                    for c in range(2):
                        toks = slice(DH * c, DH * c + DH)
                        nc.tensor.matmul(m.ps[rows, 4, f * P + DH * c:f * P + DH * c + DH], S[rows, c, f, :],
                                         KR[rows, f, 1, toks], start=False, stop=False, skip_group_check=True)
                    last = nc.tensor.matmul(out, Vt[:, h * DH:(h + 1) * DH], A[:, h, 3, :], start=False, stop=True)
                last.then_inc(s_["yo_done"], 1)

        @block.scalar
        def _(act):
            with act.Fori(0, TT) as it:
                for n, dst in enumerate((Bt, Ct, Vt)):
                    act.wait_ge(s_["turned"], it * 3 + n + 1)
                    nc.scalar.copy(dst[:], m.ps[:, n, :]).then_inc(s_["tm_read"], 1)
                act.wait_ge(s_["mv"], it + 1)
                nc.scalar.copy(MV[:].rearrange("p h d -> p (h d)"), m.ps[:, 3, :]).then_inc(s_["mv_read"], 1)
                for c in range(2):
                    toks = slice(DH * c, DH * c + DH)
                    act.wait_ge(s_["sa_done"], it * 2 + (c + 1))
                    nc.scalar.mul(SA[toks, :, :].rearrange("p h d -> p (h d)"), m.ps[toks, 2, :], -1.0
                                  ).then_inc(s_["sa_read"], 1)
                act.wait_ge(s_["yo_done"], it + 1)
                nc.scalar.copy(yr[:, :, bass.ds(it * P, P)], m.ps[:, 4, :].rearrange("p (f t) -> p f t", f=F)
                               ).then_inc(s_["yo_read"], 1)

        @block.vector
        def _(dve):
            link = Chain(dve, s_["made"])
            link(nc.vector.memset(S[:], 0.0))
            with link.loop(TT, 6) as it:
                toks = bass.ds(it * P, P)
                dve.wait_ge(s_["yo_read"], it + 1)
                for out, x in ((KR[:, :, 0, :], w.kk), (KR[:, :, 1, :], w.r), (B[:], w.b), (C[:], w.k), (Vs[:], w.v)):
                    nc.vector.tensor_copy(out, x[:, :, toks]).then_inc(s_["slices"], 1)
                nc.vector.tensor_copy(S[:, 0, :, :], S[:, 2, :, :]).then_inc(s_["s_next"], 1)
                for h in range(HEADS):
                    dve.wait_ge(s_["p1"], it * 8 + h + 1)
                    nc.vector.tensor_tensor(A[:, h, :, :].rearrange("p a t -> p (a t)"), m.ps[:, 4 + h % 2, :],
                                            part[:].rearrange("p a t -> p (a t)"), ALU.mult).then_inc(s_["p1_read"], 1)
                    dve.wait_ge(s_["p2"], it * 8 + h + 1)
                    nc.vector.tensor_tensor(N[:, h, :], m.ps[:, 6 + h % 2, 0:P], low[:], ALU.mult
                                            ).then_inc(s_["p1_read"], 1)
                dve.wait_ge(s_["p1_read"], it * 16 + 16)
                hb = lambda t: t.unsqueeze(1).to_broadcast([P, HEADS, P])
                link(nc.vector.tensor_tensor(U[:], A[:, :, 0, :], hb(pair[:]), ALU.mult))
                link(nc.vector.tensor_tensor(Ti[:], N[:], hb(pairT[:]), ALU.mult))
                for g in range(2):
                    hs = slice(g * H2, g * H2 + H2)
                    ib = m.ident[:].unsqueeze(1).to_broadcast([P, H2, P])
                    link(nc.vector.tensor_tensor(Ti[:, hs, :], ib, Ti[:, hs, :], ALU.subtract))
                    nc.vector.tensor_tensor(U[:, hs, :], ib, U[:, hs, :], ALU.subtract).then_inc(s_["inv"], 1)
                for l in range(LEVELS):
                    for g in range(2):
                        hs = slice(g * H2, g * H2 + H2)
                        dve.wait_ge(s_["y_done"], it * (2 * LEVELS) + (2 * l + g + 1))
                        nc.vector.tensor_tensor(Y[:, hs, :], m.ps[:, g, :].rearrange("p (h t) -> p h t", h=H2),
                                                lev[:, l, :].unsqueeze(1).to_broadcast([P, H2, P]), ALU.mult
                                                ).then_inc(s_["y_read"], 1)
                    for g in range(2):
                        hs = slice(g * H2, g * H2 + H2)
                        dve.wait_ge(s_["tu_done"], it * (2 * LEVELS) + (2 * l + g + 1))
                        dve.wait_ge(s_["inv"], it * (2 * LEVELS + 2) + (2 * l + g + 1))
                        nc.vector.tensor_tensor(U[:, hs, :], U[:, hs, :],
                                                m.ps[:, 6 + g, :].rearrange("p (h t) -> p h t", h=H2), ALU.subtract
                                                ).then_inc(s_["inv"], 1)
                    for g in range(2 if l < LEVELS - 1 else 0):
                        hs = slice(g * H2, g * H2 + H2)
                        if l >= 1:
                            dve.wait_ge(s_["made2"], it * (2 * LEVELS - 2) + (2 * l + g - 1))
                        nc.vector.tensor_tensor(Ti[:, hs, :], Ti[:, hs, :],
                                                m.ps[:, 4 + g, :].rearrange("p (h t) -> p h t", h=H2), ALU.subtract
                                                ).then_inc(s_["made2"], 1)
                dve.wait_ge(s_["mv_read"], it + 1)
                for c in range(2):
                    tk = slice(DH * c, DH * c + DH)
                    dve.wait_ge(s_["w_done"], it * 2 + (c + 1))
                    Wv, Mv = (x[tk, :, :].rearrange("p (f a) d -> p a f d", a=2) for x in (W, MV))
                    nc.vector.tensor_tensor(Wv[:, 0, :, :], m.ps[tk, 0, 0:F * DH].rearrange("p (f d) -> p f d", f=F),
                                            Mv[:, 0, :, :], ALU.add).then_inc(s_["w_half"], 1)
                    dve.wait_ge(s_["w_half"], it * 2 + (c + 1))
                    nc.vector.tensor_tensor(Wv[:, 1, :, :], m.ps[tk, 1, 0:F * DH].rearrange("p (f d) -> p f d", f=F),
                                            Mv[:, 1, :, :], ALU.add).then_inc(s_["w_read"], 1)
                    dve.wait_ge(s_["ds_done"], it * 2 + (c + 1))
                    nxt = S[:, c + 1, :, :]
                    link(nc.vector.tensor_tensor(nxt, S[:, c, :, :], m.ps[:, 3, 0:F * DH].rearrange(
                        "p (f d) -> p f d", f=F), ALU.add))
                    carry = w.carry[:, :, bass.ds(it * 2 + c, 1)].to_broadcast([P, F, DH])
                    nc.vector.tensor_tensor(nxt, nxt, carry, ALU.mult).then_inc(s_["s_next"], 1)
                    dve.wait_ge(s_["s_next"], it * 3 + (c + 2))


def time_mix_output(nc, m, w, yr):
    summed, squared, rooted, chain_s = (m.sem("to_" + n) for n in ("summed", "squared", "rooted", "chain"))
    F = 4
    with nc.Block() as block, ExitStack() as mem:
        t = mem.enter_context(nc.sbuf_tensor("to_t", [P, F, T], F32))

        @block.tensor
        def _(pe):
            for f in range(F):
                last = nc.tensor.matmul(m.ps[:, f, :], m.halves[:], yr[:, f, :], start=True, stop=True)
            last.then_inc(summed, 1)
            pe.wait_ge(squared, 1)
            for f in range(F):
                last = nc.tensor.matmul(m.ps[:, 4 + f, :], m.halves[:], t[:, f, :], start=True, stop=True)
            last.then_inc(summed, 1)

        @block.scalar
        def _(act):
            act.wait_ge(chain_s, 1)
            nc.scalar.activation(t[:], yr[:], ACT.Square).then_inc(squared, 1)
            act.wait_ge(chain_s, 2)
            inverse_root(nc, act, t[:], rooted, 0)

        @block.vector
        def _(dve):
            link = Chain(dve, chain_s)
            dve.wait_ge(summed, 1)
            link(nc.vector.scalar_tensor_tensor(out=yr[:], in0=m.ps[:, 0:4, :], scalar=-1.0 / DH, in1=yr[:],
                                                op0=ALU.mult, op1=ALU.add))
            dve.wait_ge(summed, 2)
            link(nc.vector.tensor_scalar(t[:], m.ps[:, 4:8, :], 1.0 / DH, GN_EPS, ALU.mult, ALU.add))
            dve.wait_ge(rooted, 2)
            link(nc.vector.tensor_tensor(yr[:], yr[:], t[:], ALU.mult))
            for f in range(F):
                link(nc.vector.tensor_scalar(yr[:, f, :], yr[:, f, :], m.v("ln_g")[:, f:f + 1], m.v("ln_b")[:, f:f + 1],
                                             ALU.mult, ALU.add))
            link(nc.vector.tensor_tensor(yr[:], yr[:], w.bonus[:], ALU.add))
            link(nc.vector.tensor_tensor(yr[:], yr[:], w.g[:], ALU.mult))


def merge(nc, m, yf, yr, x_parts, yf_parts, yr_parts, merged):
    gates_read, both, added, highs, lows, m_high, m_low = (m.sem("me_" + n) for n in (
        "gates_read", "both", "added", "highs", "lows", "m_high", "m_low"))
    with nc.Block() as block, ExitStack() as mem:
        sg = mem.enter_context(nc.sbuf_tensor("me_sg", [P, 4, T], F32))
        t = mem.enter_context(nc.sbuf_tensor("me_t", [P, 2, T], F32))
        whole = [(m.xT, x_parts, k) for k in range(KT)] + [(y, y_parts, k) for y, y_parts in (
            (yf, yf_parts), (yr, yr_parts)) for k in range(4)]

        @block.sync
        def _(sp):
            m.stream.loads(sp, "merge")

        @block.tensor
        def _(pe):
            pe.sem_inc(gates_read, 4)
            pe.sem_inc(both, 4)
            pe.wait_ge(lows, KT)
            with pe.Fori(0, 2) as it:
                for g in range(2):
                    for k in range(6):
                        x, kt = [x_parts, x_parts, x_parts, x_parts, yf_parts, yr_parts][k], KT if k < 4 else 4
                        w = [v.rearrange("p (k f) -> p k f", k=kt) for v in m.stream.weights(pe, "merge", 6 * g + k, it)]
                        if k == 4:
                            pe.wait_ge(lows, KT + 8)
                        for half in range(1 if k < 4 else 2):
                            n = k if k < 4 else 2 * k - 4 + half
                            pe.wait_ge(gates_read if n < 4 else both, it * 8 + (4 * g + n % 4 + 1))
                            for c in range(kt):
                                last = times(nc, m.ps[:, n, :], [v[:, c, half * P:(half + 1) * P] for v in w],
                                             [v[:, c, :] for v in x], start=c == 0, stop=c == kt - 1)
                        last.then_inc(m.chunk_done, 1)

        @block.scalar
        def _(act):
            for x, parts, k in whole:
                nc.scalar.copy(parts[0][:, k, :], x[:, k, :]).then_inc(highs, 1)
            act.sem_inc(added, 1)
            with act.Fori(0, 2) as it:
                for g in range(2):
                    act.wait_ge(added, it * 2 + (g + 1))
                    for k in range(4):
                        m.stream.done(act, "merge", 6 * g + k, it)
                        nc.scalar.activation(sg[:, k, :], m.ps[:, k, :], ACT.Sigmoid).then_inc(gates_read, 1)
                        m.stream.high(act, "merge", 6 * g + k, it)
                    for k in range(4, 6):
                        m.stream.done(act, "merge", 6 * g + k, it)
                        m.stream.high(act, "merge", 6 * g + k, it)
                    act.wait_ge(added, it * 2 + (g + 2))
                    nc.scalar.copy(merged[0][:, bass.ds(it * 4 + 2 * g, 2), :], t[:]).then_inc(m_high, 1)

        @block.vector
        def _(dve):
            for n, (x, parts, k) in enumerate(whole):
                dve.wait_ge(highs, n + 1)
                nc.vector.tensor_tensor(parts[1][:, k, :], x[:, k, :], parts[0][:, k, :].bitcast(F32), ALU.subtract
                                        ).then_inc(lows, 1)
            with dve.Fori(0, 2) as it:
                for g in range(2):
                    for k in range(4):
                        m.stream.done(dve, "merge", 6 * g + k, it)
                        m.stream.low(dve, "merge", 6 * g + k, it)
                    dve.wait_ge(gates_read, it * 8 + (4 * g + 8))
                    for k in range(4, 6):
                        m.stream.done(dve, "merge", 6 * g + k, it)
                        for half in range(2):
                            n = 2 * k - 4 + half
                            out = t[:, half, :] if k == 4 else sg[:, 2 + half, :]
                            nc.vector.tensor_tensor(out, sg[:, n - 4, :], m.ps[:, n, :], ALU.mult).then_inc(both, 1)
                        m.stream.low(dve, "merge", 6 * g + k, it)
                    dve.wait_ge(both, it * 8 + (4 * g + 8))
                    nc.vector.tensor_tensor(t[:], t[:], sg[:, 2:4, :], ALU.add).then_inc(added, 1)
                    dve.wait_ge(m_high, it * 2 + (g + 1))
                    dve.wait_ge(added, it * 2 + (g + 2))
                    tiles = bass.ds(it * 4 + 2 * g, 2)
                    nc.vector.tensor_tensor(merged[1][:, tiles, :], t[:], merged[0][:, tiles, :].bitcast(F32),
                                            ALU.subtract).then_inc(m_low, 1)
                    dve.wait_ge(m_low, it * 2 + (g + 1))


def output_and_norm(nc, m, high, low):
    bank_free, summed, squared, added, scaled, rooted, chain_s = (m.sem("on_" + n) for n in (
        "bank_free", "summed", "squared", "added", "scaled", "rooted", "chain"))
    with nc.Block() as block, ExitStack() as mem:
        sb = lambda n, s: mem.enter_context(nc.sbuf_tensor("on_" + n, s, F32))
        sq, mean, rstd = sb("sq", [P, KT, T]), sb("mean", [P, T]), sb("rstd", [P, T])

        @block.sync
        def _(sp):
            m.stream.loads(sp, "w_o")

        @block.tensor
        def _(pe):
            project(nc, m, pe, "w_o", high, low, bank_free)
            pe.wait_ge(bank_free, 8 + 1)
            for k in range(KT):
                pe.wait_ge(bank_free, 8 + k + 1)
                last = nc.tensor.matmul(m.ps[:, 0, :], m.ones[:], m.xT[:, k, :], start=k == 0, stop=k == KT - 1)
            last.then_inc(summed, 1)
            pe.wait_ge(added, KT - 1)
            nc.tensor.matmul(m.ps[:, 1, :], m.ones[:], sq[:, 0, :], start=True, stop=True).then_inc(summed, 1)

        @block.scalar
        def _(act):
            for n in range(KT):
                m.stream.done(act, "w_o", n)
                m.stream.high(act, "w_o", n)
            for k in range(KT):
                act.wait_ge(chain_s, k + 2)
                nc.scalar.activation(sq[:, k, :], m.xT[:, k, :], ACT.Square).then_inc(squared, 1)
            act.wait_ge(chain_s, KT + 2)
            inverse_root(nc, act, rstd[:], rooted, 0)
            for k in range(KT):
                act.wait_ge(scaled, k + 1)
                nc.scalar.activation(m.xT[:, k, :], m.xT[:, k, :], ACT.Identity, bias=m.v("ln1_b")[:, k:k + 1])

        @block.vector
        def _(dve):
            for n in range(KT):
                m.stream.done(dve, "w_o", n)
                nc.vector.scalar_tensor_tensor(out=m.xT[:, n, :], in0=m.xT[:, n, :], scalar=ALPHA, in1=m.ps[:, n, :],
                                               op0=ALU.mult, op1=ALU.add).then_inc(bank_free, 1)
                m.stream.low(dve, "w_o", n)
            link = Chain(dve, chain_s)
            dve.wait_ge(summed, 1)
            link(nc.vector.tensor_scalar(mean[:], m.ps[:, 0, :], 1.0 / D, None, ALU.mult))
            for k in range(KT):
                link(nc.vector.tensor_tensor(m.xT[:, k, :], m.xT[:, k, :], mean[:], ALU.subtract))
            for k in range(1, KT):
                dve.wait_ge(squared, k + 1)
                if k >= 2:
                    dve.wait_ge(added, k - 1)
                nc.vector.tensor_tensor(sq[:, 0, :], sq[:, 0, :], sq[:, k, :], ALU.add).then_inc(added, 1)
            dve.wait_ge(summed, 2)
            link(nc.vector.tensor_scalar(rstd[:], m.ps[:, 1, :], 1.0 / D, LN_EPS, ALU.mult, ALU.add))
            dve.wait_ge(rooted, 2)
            for k in range(KT):
                nc.vector.scalar_tensor_tensor(out=m.xT[:, k, :], in0=m.xT[:, k, :], scalar=m.v("ln1_g")[:, k:k + 1],
                                               in1=rstd[:], op0=ALU.mult, op1=ALU.mult).then_inc(scaled, 1)


def choose_experts(nc, m, high, low, x4, iT, jT, gT):
    names = ("q_read", "scored", "copied", "highs", "lows", "spilled", "keys_loaded", "chain", "used", "diffed", "exped",
             "chosen", "turned", "turned_read", "found", "picked")
    (q_read, scored, copied, highs, lows, spilled, keys_loaded, chain_s, used, diffed, exped, chosen, turned,
     turned_read, found, picked) = (m.sem("ch_" + n) for n in names)
    HH, K = 2 * HEADS, TOPK
    with nc.Block() as block, ExitStack() as mem:
        sb = lambda n, s, dt=F32: mem.enter_context(nc.sbuf_tensor("ch_" + n, s, dt))
        q, keys = sb("q", [P, 4, T]), sb("keys", [P, HH, KEYS])
        sc, rest = sb("sc", [P, 2, 2 * TT, KEYS]), sb("rest", [P, 2 * TT, KEYS])
        val, idx, idxf = sb("val", [P, 2 * TT, K]), sb("idx", [P, 2 * TT, K], U32), sb("idxf", [P, 2 * TT, K])
        cand, crest = sb("cand", [P, TT, K * K]), sb("crest", [P, TT, K * K])
        best, pos = sb("best", [P, TT, K]), sb("pos", [P, TT, K], U32)
        pa, pb = sb("pa", [P, TT, K], U32), sb("pb", [P, TT, K], U32)
        paf, pbf = sb("paf", [P, TT, K]), sb("pbf", [P, TT, K])
        eq = sb("eq", [P, 2, TT, K, K])
        i_, j_, g_ = (sb(n, [P, TT, HEADS, K]) for n in "ijg")
        gsum = sb("gsum", [P, TT * HEADS, 1])

        @block.sync
        def _(sp):
            sp.dma_start(keys[:], m.i["keys"].rearrange("p (h k) -> p h k", k=KEYS)).then_inc(keys_loaded, 16)
            sp.dma_start(x4.rearrange("(k p) t -> p k t", p=P), m.xT[:]).then_inc(spilled, 16)
            m.stream.loads(sp, "peer_q")
            sp.wait_ge(spilled, 16)

        @block.tensor
        def _(pe):
            def queries(n):
                w = [x.rearrange("p (c f) -> p c f", c=KT) for x in m.stream.weights(pe, "peer_q", n)]
                if n >= 4:
                    pe.wait_ge(q_read, n - 3)
                for c in range(KT):
                    if n == 0:
                        pe.wait_ge(lows, c + 1)
                    last = times(nc, m.ps[:, n % 4, :], [x[:, c, :] for x in w], [high[:, c, :], low[:, c, :]],
                                 start=c == 0, stop=c == KT - 1)
                last.then_inc(m.chunk_done, 1)

            def score(n):
                pe.wait_ge(q_read, n + 1)
                if n >= 4:
                    pe.wait_ge(copied, n - 3)
                for tt in range(TT):
                    toks = slice(tt * P, (tt + 1) * P)
                    last = nc.tensor.matmul(m.ps[:, 4 + n % 4, toks], q[:, n % 4, toks], keys[:, n, :],
                                            start=True, stop=True)
                last.then_inc(scored, 1)

            for h in range(HEADS + 1):
                for n in (2 * h, 2 * h + 1):
                    if h < HEADS:
                        queries(n)
                if h == 1:
                    pe.wait_ge(keys_loaded, 16)
                for n in (2 * h - 2, 2 * h - 1):
                    if h >= 1:
                        score(n)
            pe.wait_ge(chosen, HEADS + 1)
            for n, src in enumerate((i_, j_, g_)):
                for tt in range(TT):
                    last = nc.tensor.transpose(m.ps[:, n, tt * P:(tt + 1) * P], src[:, tt, :, :].rearrange("p h k -> p (h k)"),
                                               m.ident[:])
                last.then_inc(turned, 1)

        @block.scalar
        def _(act):
            for k in range(KT):
                nc.scalar.copy(high[:, k, :], m.xT[:, k, :]).then_inc(highs, 1)
            for h in range(HEADS + 1):
                if h < HEADS:
                    for n in (2 * h, 2 * h + 1):
                        m.stream.done(act, "peer_q", n)
                        if n >= 4:
                            act.wait_ge(scored, n - 3)
                        nc.scalar.copy(q[:, n % 4, :], m.ps[:, n % 4, :]).then_inc(q_read, 1)
                        m.stream.high(act, "peer_q", n)
                if h >= 1:
                    if h >= 3:
                        act.wait_ge(used, h - 2)
                    for n in (2 * h - 2, 2 * h - 1):
                        act.wait_ge(scored, n + 1)
                        nc.scalar.copy(sc[:, (h - 1) % 2, (n % 2) * TT:(n % 2 + 1) * TT, :], m.ps[:, 4 + n % 4, :].rearrange(
                            "p (t k) -> p t k", t=TT)).then_inc(copied, 1)
            act.wait_ge(diffed, HEADS)
            nc.scalar.activation(g_[:], g_[:], ACT.Exp).then_inc(exped, 1)
            for n, dst in enumerate((iT, jT, gT)):
                act.wait_ge(turned, n + 1)
                nc.scalar.copy(dst[:], m.ps[:, n, :]).then_inc(turned_read, 1)

        @block.gpsimd
        def _(pool):
            for n in range(HH):
                pool.wait_ge(found, n + 1)
                half = n % 2
                nc.gpsimd.tensor_tensor(eq[:, half], eq[:, half], idxf[:, half * TT:(half + 1) * TT, :].unsqueeze(2
                                        ).to_broadcast([P, TT, K, K]), ALU.mult).then_inc(picked, 1)

        @block.vector
        def _(dve):
            link = Chain(dve, chain_s)

            def every(n, one):
                for row in range(n - 1):
                    one(row)
                link(one(n - 1))

            def top16(n, values, index, x, left):
                every(n, lambda a: nc.vector.max(values[:, a, 0:8], x[:, a, :]))
                every(n, lambda a: nc.vector.match_replace(left[:, a, :], values[:, a, 0:8], x[:, a, :], NEG))
                every(n, lambda a: nc.vector.max(values[:, a, 8:16], left[:, a, :]))
                every(n, lambda a: nc.vector.max_index(index[:, a, 0:8], values[:, a, 0:8], x[:, a, :]))
                every(n, lambda a: nc.vector.max_index(index[:, a, 8:16], values[:, a, 8:16], left[:, a, :]))

            def choose(h):
                dve.wait_ge(copied, 2 * h + 2)
                top16(2 * TT, val, idx, sc[:, h % 2, :, :], rest)
                nc.vector.sem_inc(used, 1)
                if h >= 1:
                    collect(h - 1)
                link(nc.vector.tensor_copy(idxf[:], idx[:]))
                link(nc.vector.tensor_tensor(cand[:].rearrange("p t (a b) -> p t a b", b=K),
                                             val[:, 0:TT, :].unsqueeze(3).to_broadcast([P, TT, K, K]),
                                             val[:, TT:2 * TT, :].unsqueeze(2).to_broadcast([P, TT, K, K]), ALU.add))
                top16(TT, best, pos, cand, crest)
                nc.vector.tensor_tensor(g_[:, :, h, :], best[:], best[:, :, 0:1].to_broadcast([P, TT, K]), ALU.subtract
                                        ).then_inc(diffed, 1)
                nc.vector.tensor_scalar(pa[:], pos[:], 4, None, ALU.logical_shift_right)
                link(nc.vector.tensor_scalar(pb[:], pos[:], K - 1, None, ALU.bitwise_and))
                nc.vector.tensor_copy(paf[:], pa[:])
                link(nc.vector.tensor_copy(pbf[:], pb[:]))
                iota16 = m.iota[:, 0:K].unsqueeze(1).unsqueeze(1).to_broadcast([P, TT, K, K])
                for half, place in enumerate((paf, pbf)):
                    nc.vector.tensor_tensor(eq[:, half], place[:].unsqueeze(3).to_broadcast([P, TT, K, K]), iota16,
                                            ALU.is_equal).then_inc(found, 1)

            def collect(h):
                dve.wait_ge(picked, 2 * h + 2)
                for half, out in enumerate((i_, j_)):
                    ins = nc.vector.tensor_reduce(out[:, :, h, :], eq[:, half], AX.X, ALU.add)
                ins.then_inc(chosen, 1)

            for k in range(KT):
                dve.wait_ge(highs, k + 1)
                nc.vector.tensor_tensor(low[:, k, :], m.xT[:, k, :], high[:, k, :].bitcast(F32), ALU.subtract
                                        ).then_inc(lows, 1)
            for h in range(HEADS + 1):
                if h < HEADS:
                    for n in (2 * h, 2 * h + 1):
                        m.stream.done(dve, "peer_q", n)
                        m.stream.low(dve, "peer_q", n)
                if h >= 1:
                    choose(h - 1)
            collect(HEADS - 1)
            g = g_[:].rearrange("p t h k -> p (t h) k")
            dve.wait_ge(exped, 1)
            link(nc.vector.tensor_reduce(gsum[:], g, AX.X, ALU.add))
            link(nc.vector.reciprocal(gsum[:], gsum[:]))
            nc.vector.tensor_tensor(g, g, gsum[:].to_broadcast([P, TT * HEADS, K]), ALU.mult).then_inc(chosen, 1)


BLK = 256
PAIR = 4


def gate_matrices(nc, m, blk, G, iT, jT, gT, x4, x, high, low):
    made, weighted, done, read, x_loaded, highs = (m.sem(f"gm{blk}_{n}") for n in (
        "made", "weighted", "done", "read", "x_loaded", "highs"))
    groups = 4
    per = groups * PAIR
    rounds = BLK // per
    A = x[:].rearrange("p k t -> p (k t)").rearrange("p (n i) -> p n i", i=P)
    with nc.Block() as block, ExitStack() as mem:
        B = mem.enter_context(nc.sbuf_tensor(f"gm{blk}_B", [P, per, P], F32))

        @block.sync
        def _(sp):
            sp.wait_ge(done, groups * rounds)
            sp.dma_start(x[:], x4.rearrange("(k p) t -> p k t", p=P)[:, :, blk * BLK:(blk + 1) * BLK]
                         ).then_inc(x_loaded, 16)
            sp.wait_ge(x_loaded, 16)

        @block.tensor
        def _(pe):
            pe.sem_inc(read, groups)
            with pe.Fori(0, rounds) as it:
                for g in range(groups):
                    pe.wait_ge(made, it * (2 * groups) + 2 * (g + 1))
                    pe.wait_ge(weighted, it * groups + (g + 1))
                    pe.wait_ge(read, it * groups + (g + 1))
                    for n in range(PAIR):
                        last = nc.tensor.matmul(m.ps[:, g, n * P:(n + 1) * P], B[:, g * PAIR + n, :],
                                                A[:, g * PAIR + n, :], start=True, stop=True)
                    last.then_inc(done, 1)

        @block.scalar
        def _(act):
            with act.Fori(0, rounds) as it:
                for g in range(groups):
                    act.wait_ge(done, it * groups + (g + 1))
                    nc.scalar.copy(G[:, bass.ds(it * per + PAIR * g, PAIR), :],
                                   m.ps[:, g, :].rearrange("p (t i) -> p t i", i=P)).then_inc(read, 1)
            act.wait_ge(x_loaded, 16)
            nc.scalar.copy(high[:], x[:]).then_inc(highs, 1)

        @block.gpsimd
        def _(pool):
            with pool.Fori(0, rounds) as it:
                for g in range(groups):
                    pool.wait_ge(made, it * (2 * groups) + (2 * g + 1))
                    rows = A[:, g * PAIR:(g + 1) * PAIR, :]
                    nc.gpsimd.tensor_tensor(rows, rows, gT[:, bass.ds(it * per + (blk * BLK + g * PAIR), PAIR)]
                                            .unsqueeze(2).to_broadcast([P, PAIR, P]), ALU.mult).then_inc(weighted, 1)

        @block.vector
        def _(dve):
            with dve.Fori(0, rounds) as it:
                for g in range(groups):
                    dve.wait_ge(read, it * groups + (g + 1))
                    at = it * per + (blk * BLK + g * PAIR)
                    for onehot, place in ((A, iT), (B, jT)):
                        nc.vector.tensor_tensor(onehot[:, g * PAIR:(g + 1) * PAIR, :],
                                                m.iota[:].unsqueeze(1).to_broadcast([P, PAIR, P]),
                                                place[:, bass.ds(at, PAIR)].unsqueeze(2).to_broadcast([P, PAIR, P]),
                                                ALU.is_equal).then_inc(made, 1)
            dve.wait_ge(highs, 1)
            nc.vector.tensor_tensor(low[:], x[:], high[:].bitcast(F32), ALU.subtract)


def key_experts(nc, m, blk, G, x, high, low):
    first, loop, last_tiles = (name + str(blk) for name in ("table_first", "table", "table_last"))
    hid, gelu, weighted, rounded, split = (m.sem(f"ke{blk}_{n}") for n in (
        "hid", "gelu", "weighted", "rounded", "split"))
    with nc.Block() as block, ExitStack() as mem:
        sb = lambda n, dt=F32: mem.enter_context(nc.sbuf_tensor(f"ke{blk}_{n}", [P, 2, BLK], dt))
        ge, gated, gated_high, gated_low = sb("ge"), sb("gated"), sb("gated_high", F32R), sb("gated_low", F32R)

        @block.sync
        def _(sp):
            m.stream.loads(sp, first, loop, last_tiles)

        @block.tensor
        def _(pe):
            pe.sem_inc(gelu, 2)
            pe.sem_inc(split, 2)

            def hidden(name, k, it, tile, b):
                u = [w.rearrange("p (c j) -> p c j", c=KT) for w in m.stream.weights(pe, name, k, it)]
                pe.wait_ge(gelu, tile + 1)
                for c in range(KT):
                    last = times(nc, m.ps[:, 4 + b, 0:BLK], [w[:, c, :] for w in u], [high[:, c, :], low[:, c, :]],
                                 start=c == 0, stop=c == KT - 1)
                last.then_inc(m.chunk_done, 1)

            def output(name, k, it, tile, b, stop=False):
                v = m.stream.weights(pe, name, k, it)
                pe.wait_ge(split, tile + 3)
                for tt in range(2):
                    for half in range(2):
                        last = times(nc, m.ps[:, 2 * tt + half, :],
                                     [w[:, b, tt * P:(tt + 1) * P] for w in (gated_high, gated_low)],
                                     [w[:, half * T:(half + 1) * T] for w in v], start=False, stop=stop,
                                     skip_group_check=True)
                last.then_inc(m.chunk_done, 1)

            for b in range(4):
                nc.tensor.matmul(m.ps[:, b, :], m.zeros[:], x[:, 0:2, :], start=True, stop=False,
                                 skip_group_check=True)
            hidden(first, 0, 0, 0, 0)
            with pe.Fori(0, (KEYS - 2) // STEP) as it:
                for j in range(STEP):
                    hidden(loop, 2 * j, it, it * STEP + (j + 1), (j + 1) % 2)
                    output(loop, 2 * j + 1, it, it * STEP + j, j % 2)
            hidden(last_tiles, 0, 0, KEYS - 1, 1)
            output(last_tiles, 1, 0, KEYS - 2, 0)
            output(last_tiles, 2, 0, KEYS - 1, 1, stop=True)

        @block.scalar
        def _(act):
            def activate(name, k, it, tile, b):
                m.stream.done(act, name, k, it)
                act.wait_ge(split, tile + 1)
                nc.scalar.activation(ge[:, b, :], m.ps[:, 4 + b, 0:BLK], ACT.Gelu).then_inc(gelu, 1)
                m.stream.high(act, name, k, it)

            def passing(name, k, it):
                m.stream.done(act, name, k, it)
                m.stream.high(act, name, k, it)

            activate(first, 0, 0, 0, 0)
            with act.Fori(0, (KEYS - 2) // STEP) as it:
                for j in range(STEP):
                    activate(loop, 2 * j, it, it * STEP + (j + 1), (j + 1) % 2)
                    passing(loop, 2 * j + 1, it)
            activate(last_tiles, 0, 0, KEYS - 1, 1)
            passing(last_tiles, 1, 0)
            passing(last_tiles, 2, 0)

        @block.vector
        def _(dve):
            def gate(name, k, it, tile, b):
                m.stream.done(dve, name, k, it)
                dve.wait_ge(gelu, tile + 3)
                g = G[:, :, bass.ds(tile, 1)].rearrange("p t o -> p (t o)")
                nc.vector.tensor_tensor(gated[:, b, :], ge[:, b, :], g, ALU.mult).then_inc(weighted, 1)
                nc.vector.tensor_tensor(gated_high[:, b, :], ge[:, b, :], g, ALU.mult).then_inc(rounded, 1)
                dve.wait_ge(weighted, tile + 1)
                dve.wait_ge(rounded, tile + 1)
                nc.vector.tensor_tensor(gated_low[:, b, :], gated[:, b, :], gated_high[:, b, :].bitcast(F32),
                                        ALU.subtract).then_inc(split, 1)
                m.stream.low(dve, name, k, it)

            def passing(name, k, it):
                m.stream.done(dve, name, k, it)
                m.stream.low(dve, name, k, it)

            gate(first, 0, 0, 0, 0)
            with dve.Fori(0, (KEYS - 2) // STEP) as it:
                for j in range(STEP):
                    gate(loop, 2 * j, it, it * STEP + (j + 1), (j + 1) % 2)
                    passing(loop, 2 * j + 1, it)
            gate(last_tiles, 0, 0, KEYS - 1, 1)
            passing(last_tiles, 1, 0)
            passing(last_tiles, 2, 0)


def last_norm(nc, m, blk, out, x):
    turned, scaled, loaded, steps, chain_s, stored = (m.sem(f"ln{blk}_{n}") for n in (
        "turned", "scaled", "loaded", "steps", "chain", "stored"))
    with nc.Block() as block, ExitStack() as mem:
        sb = lambda n, s: mem.enter_context(nc.sbuf_tensor(f"ln{blk}_{n}", s, F32))
        st, ln2 = sb("st", [P, 2, 2]), sb("ln2", [P, 2, D])
        y, sq = sb("y", [P, 2, D]), sb("sq", [P, 2, D])

        @block.sync
        def _(sp):
            sp.dma_start(ln2[:, 0, :], m.i["ln2"][0:1, :].broadcast_to([P, D])).then_inc(loaded, 16)
            sp.dma_start(ln2[:, 1, :], m.i["ln2"][1:2, :].broadcast_to([P, D])).then_inc(loaded, 16)
            for tt in range(2):
                sp.wait_ge(chain_s, 10 + tt)
                sp.dma_start(out[blk * BLK + tt * P:blk * BLK + (tt + 1) * P, :], y[:, tt, :]).then_inc(stored, 16)
            sp.wait_ge(stored, 32)

        @block.tensor
        def _(pe):
            for tt in range(2):
                for k in range(KT):
                    last = nc.tensor.transpose(m.ps[:, 4 + 2 * tt + k // 4, (k % 4) * P:(k % 4 + 1) * P],
                                               x[:, k, tt * P:(tt + 1) * P], m.ident[:])
                last.then_inc(turned, 1)

        @block.scalar
        def _(act):
            for tt in range(2):
                act.wait_ge(turned, tt + 1)
                nc.scalar.mul(sq[:, tt, :], m.ps[:, 4 + 2 * tt:6 + 2 * tt, :].rearrange("p a f -> p (a f)"), ALPHA
                              ).then_inc(scaled, 1)
            for tt in range(2):
                act.wait_ge(chain_s, tt + 1)
                nc.scalar.activation(sq[:, tt, :], y[:, tt, :], ACT.Copy, accum_out=st[:, 0, tt:tt + 1]
                                     ).then_inc(steps, 1)
            for tt in range(2):
                act.wait_ge(chain_s, tt + 4)
                nc.scalar.activation(sq[:, tt, :], y[:, tt, :], ACT.Square, accum_out=st[:, 1, tt:tt + 1]
                                     ).then_inc(steps, 1)
            act.wait_ge(chain_s, 6)
            nc.scalar.activation(st[:, 1, :], st[:, 1, :], ACT.Sqrt).then_inc(steps, 1)

        @block.vector
        def _(dve):
            link = Chain(dve, chain_s)
            for tt in range(2):
                dve.wait_ge(scaled, tt + 1)
                experts_y = m.ps[:, 2 * tt:2 * tt + 2, :].rearrange("p a f -> p (a f)")
                link(nc.vector.tensor_tensor(y[:, tt, :], sq[:, tt, :], experts_y, ALU.add))
            dve.wait_ge(steps, 2)
            link(nc.vector.tensor_scalar(st[:, 0, :], st[:, 0, :], -1.0 / D, None, ALU.mult))
            for tt in range(2):
                link(nc.vector.tensor_scalar(y[:, tt, :], y[:, tt, :], st[:, 0, tt:tt + 1], None, ALU.add))
            dve.wait_ge(steps, 4)
            link(nc.vector.tensor_scalar(st[:, 1, :], st[:, 1, :], 1.0 / D, LN_EPS, ALU.mult, ALU.add))
            dve.wait_ge(steps, 5)
            link(nc.vector.reciprocal(st[:, 1, :], st[:, 1, :]))
            dve.wait_ge(loaded, 32)
            for tt in range(2):
                link(nc.vector.scalar_tensor_tensor(out=y[:, tt, :], in0=y[:, tt, :], scalar=st[:, 1, tt:tt + 1],
                                                    in1=ln2[:, 0, :], op0=ALU.mult, op1=ALU.mult))
            for tt in range(2):
                link(nc.vector.tensor_tensor(y[:, tt, :], y[:, tt, :], ln2[:, 1, :], ALU.add))


def segments(i):
    w = i["w_in"]
    table = {
        "table_first": (1, 1, table_parts(i["u"], i["v"], [("u", 0)])),
        "table": ((KEYS - 2) // STEP, 2 * STEP, table_parts(i["u"], i["v"], [
            t for j in range(STEP) for t in (("u", j + 1), ("v", j))])),
        "table_last": (1, 3, table_parts(i["u"], i["v"], [("u", KEYS - 1), ("v", KEYS - 2), ("v", KEYS - 1)])),
    }
    return {
        "ada": (2, 3 * KT, wide_columns(i["ada_w"], 3 * KT)),
        "attn_qk": (1, 16, columns(i["attn_w_in"][:, 0:2 * D], 16)),
        "attn_v": (1, 8, wide_columns(i["attn_w_in"][:, 2 * D:3 * D], 8)),
        "attn_out": (1, 8, columns(i["attn_w_out"], 8)),
        "experts": (EXPERTS, 12, expert_parts(i["w_gate"], i["w_up"], i["w_down"])),
        "fox_qk": (1, 8, columns(w[:, 0:D], 8)),
        "fox_v": (1, 4, wide_columns(w[:, FOX_V:FOX_F], 4)),
        "rwkv_in": (1, 14, columns(w[:, RWKV_AT:GATE_AT], 14)),
        "merge": (2, 12, merge_parts(w, i["p_fox"], i["p_rwkv"])),
        "w_o": (1, 8, columns(i["w_o"], 8)),
        "peer_q": (1, 2 * HEADS, columns(i["peer_w_q"], 2 * HEADS)),
        **{name + str(blk): segment for blk in range(T // BLK) for name, segment in table.items()},
    }


def recycle(nc, sems):
    numbers = sorted(s.num for s in sems)
    with nc.Block() as block:
        @block.gpsimd
        def _(pool):
            at = 0
            while at < len(numbers):
                end = at
                while end + 1 < len(numbers) and numbers[end + 1] == numbers[end] + 1:
                    end += 1
                pool.sem_clear(range(numbers[at], numbers[end] + 1))
                at = end + 1
    for s in sems:
        nc.release_semaphore(s)
    sems.clear()


def build_program(nc, i, out):
    stage_sems = []

    def keep_sem(name):
        return ctx.enter_context(nc.semaphore(name))

    def sem(name):
        stage_sems.append(nc.alloc_semaphore(name))
        return stage_sems[-1]

    with ExitStack() as ctx:
        def allocate(scope, dt=F32):
            return lambda n, s, dt=dt: scope.enter_context(nc.sbuf_tensor(n, s, dt))

        def pair(scope, name, shape):
            return [allocate(scope)(name + part, shape, F32R) for part in ("_high", "_low")]

        sb = allocate(ctx)
        m = Shared()
        m.nc, m.i, m.sem = nc, i, sem
        m.raw = sb("raw", [P, RAW, CH])
        m.w_high, m.w_low = pair(ctx, "w", [P, AHEAD, CH])
        m.slot_full = [keep_sem(f"slot_full{n}") for n in range(RAW)]
        m.high_done, m.split_done, m.chunk_done, m.settled = (
            keep_sem(n) for n in ("high_done", "split_done", "chunk_done", "settled"))
        m.stream = Stream(m, segments(i))
        m.ps = ctx.enter_context(nc.psum_tensor("ps", [P, 8, T], F32))
        m.vec = sb("vec", [P, NVEC])
        m.v = lambda name: m.vec[:, VEC_AT[name][0]:VEC_AT[name][1]]
        m.ones, m.ident, m.zeros, m.iota = (sb(n, [P, P]) for n in ("ones", "ident", "zeros", "iota"))
        iT, jT, gT = sb("iT", [P, T]), sb("jT", [P, T]), sb("gT", [P, T])
        x4 = nc.dram_tensor("x4", (D, T), F32, kind="Internal").ap()
        with ExitStack() as early:
            sb = allocate(early)
            m.halves, m.iota_i = sb("halves", [P, P]), sb("iota_i", [P, P], I32)
            m.neg_lam, m.mod = sb("neg_lam", [P, 1]), sb("mod", [P, 6 * KT])
            m.norm1, m.norm2 = sb("norm1", [P, KT]), sb("norm2", [P, KT])
            m.router_w, m.router_b = sb("router_w", [P, KT, 20]), sb("router_b", [P, 20])
            m.router_h, m.router_l = pair(early, "router", [P, KT, 20])
            m.xT = sb("xT", [P, KT, T])

            with ExitStack() as mem:
                sb = allocate(mem)
                m.lam_row, m.lam_prod = sb("lam_row", [P, 4 * DH]), sb("lam_prod", [P, 2, DH])
                m.lam_dot, m.lam_e, m.cond = sb("lam_dot", [P, 2]), sb("lam_e", [P, 2]), sb("cond", [P, KT])
                m.cond_high, m.cond_low = pair(mem, "cond", [P, KT, P])
                setup(nc, m)
                modulation(nc, m)
            with ExitStack() as mem:
                m.oT = allocate(mem)("oT", [P, HEADS, T])
                with ExitStack() as inner:
                    sb = allocate(inner)
                    qT, kT, v = sb("qT", [P, HEADS, T]), sb("kT", [P, HEADS, T]), sb("v", [P, TT, D])
                    with ExitStack() as normed:
                        h = pair(normed, "h1", [P, KT, T])
                        rms_norm(nc, m, "norm_mix", m.norm1, m.mod[:, 0:KT], *h)
                        qkv_projection(nc, m, *h, qT, kT, v)
                    diff_attention(nc, m, qT, kT, v)
                o = pair(mem, "o", [P, HEADS, T])
                head_norm(nc, m, *o)
                add_projection(nc, m, *o)
            with ExitStack() as mem:
                h = pair(mem, "h2", [P, KT, T])
                rms_norm(nc, m, "norm_ffn", m.norm2, m.mod[:, 3 * KT:4 * KT], *h)
                gate_bc = allocate(mem)("gate_bc", [P, EXPERTS, T])
                router(nc, m, *h, gate_bc)
                experts(nc, m, *h, gate_bc)
            with ExitStack() as mem:
                sb = allocate(mem)
                yf, yr = sb("yf", [P, 4, T]), sb("yr", [P, 4, T])
                with ExitStack() as inner:
                    sb = allocate(inner)
                    cols = sb("cols", [P, 14, T + 1])
                    with ExitStack() as attn:
                        sb = allocate(attn)
                        fq, fk, fv = sb("fq", [P, 4, T]), sb("fk", [P, 4, T]), sb("fv", [P, TT, T])
                        negc, cq = sb("negc", [P, HEADS, T]), sb("cq", [P, TT, HEADS])
                        with ExitStack() as normed:
                            x3 = pair(normed, "x3", [P, KT, T])
                            rms_norm(nc, m, "norm_final", m.v("norm_final"), None, *x3, keep=True)
                            second_projection(nc, m, *x3, fq, fk, fv, cols, negc, cq)
                        fox_attention(nc, m, fq, fk, fv, negc, cq, yf)
                    w = Shared()
                    sb = allocate(inner)
                    w.kk, w.bonus, w.b, w.g = (sb("w_" + n, [P, 4, T]) for n in ("kk", "bonus", "b", "g"))
                    w.r, w.k, w.v = (cols[:, n:n + 4, 1:T + 1] for n in (0, 4, 8))
                    w.carry = sb("w_carry", [P, 4, NCHUNK])
                    masks = allocate_masks(sb)
                    time_mix_inputs(nc, m, cols, w, masks)
                    recurrence(nc, m, w, masks, yr)
                    time_mix_output(nc, m, w, yr)
                recycle(nc, stage_sems)
                merged = pair(mem, "merged", [P, KT, T])
                with ExitStack() as inner:
                    merge(nc, m, yf, yr, pair(inner, "x3m", [P, KT, T]), pair(inner, "yf", [P, 4, T]),
                          pair(inner, "yr", [P, 4, T]), merged)
                output_and_norm(nc, m, *merged)
            with ExitStack() as mem:
                choose_experts(nc, m, *pair(mem, "x4", [P, KT, T]), x4, iT, jT, gT)
        for blk in range(T // BLK):
            with ExitStack() as mem:
                sb = allocate(mem)
                x = sb(f"x{blk}", [P, KT, BLK])
                with ExitStack() as inner:
                    parts = pair(inner, f"x{blk}", [P, KT, BLK])
                    G = allocate(inner)(f"G{blk}", [P, BLK, KEYS])
                    gate_matrices(nc, m, blk, G, iT, jT, gT, x4, x, *parts)
                    key_experts(nc, m, blk, G, x, *parts)
                last_norm(nc, m, blk, out, x)


def lay_out(x):
    tile = lambda v: np.asarray(v).reshape(-1, P).T
    src = {"c": "c", "norm_mix": "norm_mix", "norm_ffn": "norm_ffn", "norm_final": "norm_final", "ln1_g": "ln1_g_2",
           "ln1_b": "ln1_b_2", "ada_b": "ada_b", "subln": "attn_subln", "mu": "rwkv_mu_2", "w0": "rwkv_w0_2",
           "a0": "rwkv_a0_2", "k_k": "rwkv_k_k_2", "k_a": "rwkv_k_a_2", "r_k": "rwkv_r_k_2", "ln_g": "rwkv_ln_g_2",
           "ln_b": "rwkv_ln_b_2"}
    a = {}
    a["vecs"] = np.concatenate([tile(x[src[n]]) for n, _ in VEC_NAMES], 1)
    a["lams"] = np.concatenate([np.asarray(x["attn_lam_" + n]) for n in ("q1", "k1", "q2", "k2")], 1)
    a["xT"] = np.asarray(x["x"])[0].T
    a["ada_w"] = np.asarray(x["ada_w"])[0]
    a["attn_w_in"] = np.asarray(x["attn_w_in"])[0]
    a["attn_w_out"] = np.asarray(x["attn_w_out"])[0]
    a["router_w"] = np.concatenate([np.asarray(x["router_group_w"])[0],
                                    np.asarray(x["router_expert_w"])[0].reshape(D, EXPERTS)], 1)
    a["router_b"] = np.concatenate([np.asarray(x["router_group_b"]),
                                    np.asarray(x["router_expert_b"]).reshape(1, EXPERTS)], 1)
    for n in ("gate", "up", "down"):
        a["w_" + n] = np.asarray(x["expert_w_" + n])[0]
    a["w_in"] = np.asarray(x["w_in_2"])[0]
    a["f_w"] = a["w_in"][:, FOX_F:RWKV_AT]
    a["f_b"] = np.asarray(x["fox_f_bias_2"]).reshape(HEADS, 1)
    a["w2a2"] = np.concatenate([np.asarray(x["rwkv_w2_2"])[0], np.asarray(x["rwkv_a2_2"])[0]], 0)
    a["g2"] = np.asarray(x["rwkv_g2_2"])[0]
    for n in ("p_fox", "p_rwkv", "w_o", "peer_w_q"):
        a[n] = np.asarray(x[n + "_2"])[0]
    a["keys"] = np.asarray(x["peer_sub_keys_2"])[0].transpose(3, 0, 1, 2).reshape(P, 2 * HEADS * KEYS)
    a["u"] = np.asarray(x["peer_u_2"])[0].reshape(KEYS, KEYS, KT, P).transpose(0, 3, 2, 1).reshape(KEYS, P, D)
    a["v"] = np.asarray(x["peer_v_2"])[0].reshape(KEYS, KEYS, D)
    a["ln2"] = np.concatenate([np.asarray(x["ln2_g_2"]), np.asarray(x["ln2_b_2"])], 0)
    return {n: np.ascontiguousarray(v) for n, v in a.items()}


def kernel(**inputs):
    import concourse.bacc as bacc
    from concourse.bass_utils import run_bass_kernel_spmd

    nc = bacc.Bacc("TRN2", target_bir_lowering=False, num_devices=1)
    arrays = lay_out(inputs)
    i = {n: nc.dram_tensor("in_" + n, a.shape, mybir.dt.from_np(a.dtype), kind="ExternalInput").ap()
         for n, a in arrays.items()}
    out = nc.dram_tensor("out", (T, D), F32, kind="ExternalOutput").ap()
    build_program(nc, i, out)
    r = run_bass_kernel_spmd(nc, [{"in_" + n: a for n, a in arrays.items()}], core_ids=[0])
    return r.results[0]["out"].reshape(1, T, D)
```
